# Optimizing a Trainium2 kernel written in Bass

```python
import jax, jax.numpy as jnp
from jax import lax
import numpy as np

D_MODEL = 1024
BATCH = 1
SEQ = 1024
DEPTH = 1
DEC_BATCH = 8
DEC_SEQ = 4
PAST_LEN = 8192
PAGE_SIZE = 128

D_CONV = D_MODEL
CONV_W = 3
N_HEADS = 4
DK = D_MODEL // (2 * N_HEADS)
DV = D_MODEL // N_HEADS
D_QK = N_HEADS * DK
D_V = N_HEADS * DV
D_FF = 4 * D_MODEL
CHUNK = 128
GATE_CAP = 15.0
EPS = 1e-6
IN_SIZES = (D_CONV, D_CONV, D_CONV, D_QK, D_QK, D_V, D_V, N_HEADS, N_HEADS, D_MODEL, D_MODEL)
N_IN = 3 * D_CONV + 2 * D_QK + 2 * D_V + 2 * N_HEADS + 2 * D_MODEL

kernel_name = "hybrid_conv_mlstm_adaln_decode_step"

def _rmsnorm(x, g):
    xf = x.astype(jnp.float32)
    y = xf * lax.rsqrt(jnp.mean(xf * xf, axis=-1, keepdims=True) + EPS)
    return (y * g.astype(jnp.float32)).astype(x.dtype)

def _split_in(z):
    idx = []
    acc = 0
    for s in IN_SIZES[:-1]:
        acc += s
        idx.append(acc)
    return jnp.split(z, idx, axis=-1)

def _softcap(a):
    return GATE_CAP * jnp.tanh(a / GATE_CAP)

def _mlstm_chunkwise(q, k, v, i_pre, logf, C0, n0, m0):
    B, H, T, _ = q.shape
    L = CHUNK if T % CHUNK == 0 else T
    nc = T // L

    def chunks(a):
        return jnp.moveaxis(a.reshape((B, H, nc, L) + a.shape[3:]), 2, 0)

    causal = jnp.tril(jnp.ones((L, L), dtype=bool))

    def step(carry, inp):
        C, n, m = carry
        qc, kc, vc, ic, fc = inp
        b = jnp.cumsum(fc, axis=-1)
        logD = jnp.where(causal, b[..., :, None] - b[..., None, :] + ic[..., None, :], -jnp.inf)
        a = b + m[..., None]
        m_row = jnp.maximum(jnp.max(logD, axis=-1), a)
        inter = jnp.exp(a - m_row)
        S = jnp.einsum('bhtd,bhsd->bhts', qc, kc) * jnp.exp(logD - m_row[..., None])
        num = jnp.einsum('bhts,bhsv->bhtv', S, vc) + inter[..., None] * jnp.einsum('bhtd,bhdv->bhtv', qc, C)
        den = jnp.sum(S, axis=-1) + inter * jnp.einsum('bhtd,bhd->bht', qc, n)
        h = num / jnp.maximum(jnp.abs(den), jnp.exp(-m_row))[..., None]
        bL = b[..., -1]
        w_log = bL[..., None] - b + ic
        m_new = jnp.maximum(bL + m, jnp.max(w_log, axis=-1))
        decay = jnp.exp(bL + m - m_new)
        ws = jnp.exp(w_log - m_new[..., None])
        C_new = decay[..., None, None] * C + jnp.einsum('bhs,bhsd,bhsv->bhdv', ws, kc, vc)
        n_new = decay[..., None] * n + jnp.einsum('bhs,bhsd->bhd', ws, kc)
        return (C_new, n_new, m_new), h

    (C1, n1, m1), hs = lax.scan(step, (C0, n0, m0), (chunks(q), chunks(k), chunks(v), chunks(i_pre), chunks(logf)))
    h = jnp.moveaxis(hs, 0, 2).reshape(B, H, T, v.shape[-1])
    return h, C1, n1, m1

def _mixer(h, conv_prev, C0, n0, m0, w_in, b_gate, conv_w, conv_b, hn_g, w_out):
    Bsz, T, _ = h.shape
    f32 = jnp.float32
    xc, bg, cg, q, k, v, o, ig, fg, ga, gb = _split_in(h @ w_in)
    u = cg * xc
    pad = jnp.concatenate([conv_prev.astype(u.dtype), u], axis=1)
    conv = conv_b + conv_w[0] * pad[:, 0:T] + conv_w[1] * pad[:, 1:T + 1] + conv_w[2] * pad[:, 2:T + 2]
    y_a = bg * conv
    new_conv = pad[:, T:]
    qh = q.reshape(Bsz, T, N_HEADS, DK).transpose(0, 2, 1, 3).astype(f32)
    kh = k.reshape(Bsz, T, N_HEADS, DK).transpose(0, 2, 1, 3).astype(f32) * (DK ** -0.5)
    vh = v.reshape(Bsz, T, N_HEADS, DV).transpose(0, 2, 1, 3).astype(f32)
    bgf = b_gate.astype(f32)
    i_pre = _softcap(ig.astype(f32) + bgf[:N_HEADS]).transpose(0, 2, 1)
    logf = jax.nn.log_sigmoid(_softcap(fg.astype(f32) + bgf[N_HEADS:])).transpose(0, 2, 1)
    hm, C1, n1, m1 = _mlstm_chunkwise(qh, kh, vh, i_pre, logf, C0.astype(f32), n0.astype(f32), m0.astype(f32))
    hm = hm * lax.rsqrt(jnp.mean(hm * hm, axis=-1, keepdims=True) + EPS)
    hm = hm.transpose(0, 2, 1, 3).reshape(Bsz, T, D_V) * hn_g.astype(f32)
    y_b = jax.nn.sigmoid(o) * hm.astype(o.dtype)
    merged = jax.nn.sigmoid(ga) * y_a + jax.nn.sigmoid(gb) * y_b
    return merged @ w_out, new_conv, C1, n1, m1

def _layer(x, c, conv_prev, C0, n0, m0, w_ada, b_ada, g1n, g2n, w_in, b_gate, conv_w, conv_b, hn_g, w_out, w_up, w_down):
    mod = (jax.nn.silu(c) @ w_ada + b_ada)[:, None, :]
    sh1, sc1, gt1, sh2, sc2, gt2 = jnp.split(mod, 6, axis=-1)
    h = _rmsnorm(x, g1n) * (1 + sc1) + sh1
    mix, new_conv, C1, n1, m1 = _mixer(h, conv_prev, C0, n0, m0, w_in, b_gate, conv_w, conv_b, hn_g, w_out)
    x = x + gt1 * mix
    h = _rmsnorm(x, g2n) * (1 + sc2) + sh2
    x = x + gt2 * (jnp.square(jax.nn.relu(h @ w_up)) @ w_down)
    return x, new_conv, C1, n1, m1

def setup_inputs(seed: int = 0) -> dict:
    key = jax.random.key(seed)
    ks = jax.random.split(key, 24)
    nrm = jax.random.normal
    f = jnp.float32
    b_gate = jnp.concatenate([0.5 * nrm(ks[0], (DEPTH, N_HEADS), f),
                              4.0 + 0.5 * nrm(ks[1], (DEPTH, N_HEADS), f)], axis=-1)
    return {
        "x_prompt": nrm(ks[2], (BATCH, SEQ, D_MODEL), f),
        "x_sample": nrm(ks[3], (DEC_BATCH, DEC_SEQ, D_MODEL), f),
        "state_conv": nrm(ks[4], (DEPTH, DEC_BATCH, CONV_W - 1, D_CONV), f),
        "state_C": 0.1 * nrm(ks[5], (DEPTH, DEC_BATCH, N_HEADS, DK, DV), f),
        "state_n": 0.1 * nrm(ks[6], (DEPTH, DEC_BATCH, N_HEADS, DK), f),
        "state_m": nrm(ks[7], (DEPTH, DEC_BATCH, N_HEADS), f),
        "c_prompt": nrm(ks[8], (BATCH, D_MODEL), f),
        "c_sample": nrm(ks[9], (DEC_BATCH, D_MODEL), f),
        "w_ada": 0.5 * D_MODEL ** -0.5 * nrm(ks[10], (DEPTH, D_MODEL, 6 * D_MODEL), f),
        "b_ada": 0.1 * nrm(ks[11], (DEPTH, 6 * D_MODEL), f),
        "g_norm1": 1.0 + 0.05 * nrm(ks[12], (DEPTH, D_MODEL), f),
        "g_norm2": 1.0 + 0.05 * nrm(ks[13], (DEPTH, D_MODEL), f),
        "w_in": D_MODEL ** -0.5 * nrm(ks[14], (DEPTH, D_MODEL, N_IN), f),
        "b_gate": b_gate,
        "conv_w": CONV_W ** -0.5 * nrm(ks[15], (DEPTH, CONV_W, D_CONV), f),
        "conv_b": 0.02 * nrm(ks[16], (DEPTH, D_CONV), f),
        "hn_g": 1.0 + 0.05 * nrm(ks[17], (DEPTH, D_V), f),
        "w_out": D_MODEL ** -0.5 * nrm(ks[18], (DEPTH, D_MODEL, D_MODEL), f),
        "w_up": D_MODEL ** -0.5 * nrm(ks[19], (DEPTH, D_MODEL, D_FF), f),
        "w_down": D_FF ** -0.5 * nrm(ks[20], (DEPTH, D_FF, D_MODEL), f),
        "g_final": 1.0 + 0.05 * nrm(ks[21], (D_MODEL,), f),
    }

def reference(x_prompt, x_sample, state_conv, state_C, state_n, state_m, c_prompt, c_sample,
              w_ada, b_ada, g_norm1, g_norm2, w_in, b_gate, conv_w, conv_b, hn_g, w_out, w_up, w_down, g_final):
    f32 = jnp.float32
    xp, xs = x_prompt, x_sample
    p_conv, p_C, p_n, p_m = [], [], [], []
    s_conv, s_C, s_n, s_m = [], [], [], []
    zc = jnp.zeros((BATCH, CONV_W - 1, D_CONV), xp.dtype)
    zC = jnp.zeros((BATCH, N_HEADS, DK, DV), f32)
    zn = jnp.zeros((BATCH, N_HEADS, DK), f32)
    zm = jnp.zeros((BATCH, N_HEADS), f32)
    for l in range(DEPTH):
        w = (w_ada[l], b_ada[l], g_norm1[l], g_norm2[l], w_in[l], b_gate[l], conv_w[l], conv_b[l],
             hn_g[l], w_out[l], w_up[l], w_down[l])
        xp, cv, C1, n1, m1 = _layer(xp, c_prompt, zc, zC, zn, zm, *w)
        p_conv.append(cv.astype(state_conv.dtype)); p_C.append(C1.astype(state_C.dtype))
        p_n.append(n1.astype(state_n.dtype)); p_m.append(m1.astype(state_m.dtype))
        xs, cv, C1, n1, m1 = _layer(xs, c_sample, state_conv[l], state_C[l], state_n[l], state_m[l], *w)
        s_conv.append(cv.astype(state_conv.dtype)); s_C.append(C1.astype(state_C.dtype))
        s_n.append(n1.astype(state_n.dtype)); s_m.append(m1.astype(state_m.dtype))
    y_prompt = _rmsnorm(xp, g_final)
    y_sample = _rmsnorm(xs, g_final)
    return (y_prompt, y_sample,
            jnp.stack(p_conv), jnp.stack(p_C), jnp.stack(p_n), jnp.stack(p_m),
            jnp.stack(s_conv), jnp.stack(s_C), jnp.stack(s_n), jnp.stack(s_m))


_drawn_inputs = setup_inputs


def setup_inputs(seed=0):
    import zlib

    import numpy as np

    out = dict(_drawn_inputs(seed))
    spreads = {}
    factors = {'conv_b': 8.0, 'hn_g': 8.0, 'g_norm2': 2.9}
    for name, (base, spread) in spreads.items():
        noise = np.random.default_rng([zlib.crc32(name.encode()), seed]).standard_normal(out[name].shape)
        drawn = base * np.exp(spread * noise) if base else spread * noise
        out[name] = __import__('jax').numpy.asarray(drawn.astype(out[name].dtype))
    for name, factor in factors.items():
        out[name] = (out[name] * factor).astype(out[name].dtype)
    return out
```

```python
from contextlib import ExitStack

import concourse.bass as bass
from concourse import mybir
from concourse.alu_op_type import AluOpType as ALU

F32 = mybir.dt.float32
F32R = mybir.dt.float32r
ACT = mybir.ActivationFunctionType

P = 128
D = 1024
KT = D // P
TP = 1024
SB, ST = 8, 4
NS = SB * ST
T = TP + NS
BLK = T // 3
LP = TP - 2 * BLK
H, DK, DV = 4, 128, 256
L = 128
NC = TP // L
FF = 4 * D
FT = FF // P // 8
EPS = 1e-6
CAP = 15.0
KSCALE = DK ** -0.5
NB = 1 + SB
XC, BG, CG, WQ, WK, WV, WO, WGATE, GA, GB = 0, 1024, 2048, 3072, 3584, 4096, 5120, 6144, 6152, 7176
T1_, T2_, T3_, T4_, T5_ = 0, 16, 48, 64, 72
P1_, P2_, P3_, P4_, P5_ = 1, 17, 49, 65, 73
NT = 136
G1R, G2R, CBR, CWR, HNR, BAR, PROWS = 0, 8, 16, 24, 48, 56, 104
GM, WS, MR = range(3)
BLOCKS = [(0, BLK), (BLK, 2 * BLK), (2 * BLK, T)]


class Count:

    def __init__(self, eng, sem):
        self.eng, self.sem, self.base, self.n = eng, sem, 0, 0

    def mark(self, ins):
        ins.then_inc(self.sem, 1)
        self.n += 1
        return self.base + self.n

    def wait(self, value):
        self.eng.wait_ge(self.sem, value)

    def link(self, ins):
        self.wait(self.mark(ins))

    def turn(self, base, i, per):
        self.base, self.n = base + i * per, 0


def layer_kernel(nc, I, O):
    ctx = ExitStack()
    early, startup, gates, mixer, mlstm, outp, mlp, final = (ExitStack() for _ in range(8))

    def sb(name, shape, dt=F32, scope=ctx):
        return scope.enter_context(nc.sbuf_tensor(name, shape, dt))

    def sem(name):
        return ctx.enter_context(nc.semaphore(name))

    zp_d = nc.dram_tensor("zp_d", [4 * H, P, TP], F32, kind="Internal").ap()
    zs_d = nc.dram_tensor("zs_d", [2 * H, 4, P, 16], F32, kind="Internal").ap()
    rp_d = nc.dram_tensor("rp_d", [H, TP], F32, kind="Internal").ap()
    rs_d = nc.dram_tensor("rs_d", [2 * H, 16], F32, kind="Internal").ap()

    XH = sb("XH", [P, KT, T], F32R)
    XL = sb("XL", [P, KT, T], F32R)
    A = sb("A", [P, KT, T])
    raw = sb("raw", [P, 2, 1024])
    whi = sb("whi", [P, 2, 1024], F32R)
    wlo = sb("wlo", [P, 2, 1024], F32R)
    ident = sb("ident", [P, P])
    ones = sb("ones", [P, P])
    MOD = sb("MOD", [P, 48, NB])
    S1 = sb("S1", [P, KT, NB])
    S2 = sb("S2", [P, KT, NB])
    PC = sb("PC", [P, PROWS])
    COL = sb("COL", [P, NC, 3, H])
    COLS = sb("COLS", [16, 2 * H, 3])
    CM = sb("CM", [P, P])
    CMS = sb("CMS", [16, 16])
    BM = sb("BM", [16, 4])
    NT_ = sb("NT_", [P, NS])
    SCV = sb("SCV", [P, KT, 16])
    NCV = sb("NCV", [P, KT, 18])
    ss = sb("ss", [P, 9])
    rs = sb("rs", [P, 9])
    epsc = sb("epsc", [P, 1])

    cS = sb("cS", [P, KT, P], F32R, scope=early)
    cT = sb("cT", [P, KT, NB], scope=early)
    GW = sb("GW", [P, KT, P], F32R, scope=early)
    wg = sb("wg", [P, KT, 2 * H], scope=early)
    M0s = sb("M0s", [H, SB], scope=early)
    MP = sb("MP", [H, NC], scope=early)
    PM = sb("PM", [H, 1], scope=early)
    SMo = sb("SMo", [H, SB], scope=early)
    bg15 = sb("bg15", [36, 1], scope=early)
    AROW = sb("AROW", [P, 512], scope=early)
    xin = sb("xin", [P, 9, D], scope=startup)
    araw0 = sb("araw0", [P, 8, 1024], scope=startup)
    startup.close()
    araw = sb("araw", [P, 2, 1024], scope=gates)
    ahi = sb("ahi", [P, 2, 1024], F32R, scope=gates)
    alo = sb("alo", [P, 2, 1024], F32R, scope=gates)
    zr = sb("zr", [P, 2, T], scope=gates)
    GT = sb("GT", [36, T], scope=gates)
    TH = sb("TH", [36, T], scope=gates)
    NBr = sb("NBr", [36, T], scope=gates)
    RMK = sb("RMK", [36, T], scope=gates)
    NB0, DL, MU = RMK[0:H], NBr[0:H], TH[0:H]
    RR = sb("RR", [H, T], scope=gates)
    GMR = sb("GMR", [H, T], scope=gates)
    WSR = sb("WSR", [H, T], scope=gates)
    MRR = sb("MRR", [H, T], scope=gates)
    gates.close()
    early.close()
    hm = sb("hm", [P, KT, TP], scope=mixer)
    hms = sb("hms", [P, 2 * H, 2, 16], scope=mixer)
    G1 = sb("G1", [P, T], scope=mixer)
    U = sb("U", [P, 2 + TP + 6 * SB], scope=mixer)
    Z = sb("Z", [P, 4 * H, L], scope=mlstm)
    VT = sb("VT", [P, H, DV + 1], scope=mlstm)
    CA = sb("CA", [P, H, DV + 1], scope=mlstm)
    RB = sb("RB", [P, H, L], scope=mlstm)
    IB = sb("IB", [P, H, L], scope=mlstm)
    EX = sb("EX", [P, H, L], scope=mlstm)
    KW = sb("KW", [P, H, DK], scope=mlstm)
    HT = sb("HT", [P, H, DV], scope=mlstm)
    DEC = sb("DEC", [P, H], scope=mlstm)
    sc4 = sb("sc4", [P, 8, H], scope=mlstm)
    ZU = sb("ZU", [P, 4, 16], scope=mlstm)
    VTU = sb("VTU", [16, DV + 1], scope=mlstm)
    CU = sb("CU", [P, 4, DV + 1], scope=mlstm)
    RU = sb("RU", [P, 16], scope=mlstm)
    IU = sb("IU", [P, 16], scope=mlstm)
    EU = sb("EU", [16, 16], scope=mlstm)
    QM = sb("QM", [P, 80], scope=mlstm)
    KU = sb("KU", [16, 4, DK], scope=mlstm)
    WM = sb("WM", [16, 4], scope=mlstm)
    HTU = sb("HTU", [16, DV], scope=mlstm)
    DECU = sb("DECU", [P, 4], scope=mlstm)
    sc1 = sb("sc1", [16, 8], scope=mlstm)
    mlstm.close()
    NCR = sb("NCR", [18, D], scope=outp)
    NR = sb("NR", [NS, P], scope=outp)
    PN = sb("PN", [H, P], scope=outp)
    xs = sb("xs", [P, 2, 9, P], scope=outp)
    xT = sb("xT", [P, T], scope=outp)
    SQ = sb("SQ", [P, T], scope=outp)
    outp.close()
    mixer.close()
    SQA = sb("SQA", [P, T], scope=mlp)
    AH = sb("AH", [P, FT, T], F32R, scope=mlp)
    AL = sb("AL", [P, FT, T], F32R, scope=mlp)
    R = sb("R", [P, 3, T], scope=mlp)
    YS = sb("YS", [P, KT, NS], scope=mlp)
    GF = sb("GF", [P, D], scope=mlp)
    Y = sb("Y", [P, 2, D], scope=mlp)
    mlp.close()
    CR = A[:, 0, :]
    CG_ = A[:, 1, :]
    PR = A[:, 2, 0:P]
    SNR = A[:, 2, P:2 * P]
    SCR = A[:, 3, :]

    PB = ctx.enter_context(nc.psum_tensor("PB", [P, 3, 512], F32))
    M = ctx.enter_context(nc.psum_tensor("M", [P, 5, 512], F32))

    names = """c_in p_in small_in raw0 raw1 hi_done lo_done acc_done0 acc_done1 acc_done2 acc_free0
    acc_free1 acc_free2 ada0_mm ada_done arow_done rowt_done mod_done xsq_done xrt_done xn_done xt_done
    xt_free pool_done csig_done ct_done ct_used gw_done sm_done h_hi h_lo hf_done
    araw_in0 araw_in1 ahi_done alo_done a_used z_evac z_out0 z_out1 gate_sum gate_act gate_rows r_out cols_mm cols_done
    m_out z_in zu_in rb_in cu_in cu_out qk_done kt_done vt_done upre_done num_done unum_done cup_done ucup0_done
    ucup1_done ht_done uht_done ib_exp e_exp vt_copy vtu_copy ss_done std_done ex_done qi_done cn_done p_done kw_done
    var_done ht_ready c_upd ucup0_upd ucup1_upd hm_done xc_evac conv_done sig_done a_done
    fin1_mm fin1_copy st_out so_evac sg_evac merged split_hi xs_in0 xs_in1 xtr_done xtr_copy x2_done sq_done ms_mm ms_sqrt
    h2_scaled h2_hi h2_lo relu_done rr_done act_hi act_lo y_mm y_sq y_std y_done y_out0 y_out1 gf_in dve_step act_step
    x2n_done ys_done merged_lo""".split()
    s = {n: sem(n) for n in names}
    xr = [sem(f"x_in{b}") for b in range(9)]
    ar0 = [sem(f"ada_in{b}") for b in range(8)]
    raw_in = [s["raw0"], s["raw1"]]
    araw_in = [s["araw_in0"], s["araw_in1"]]
    xs_in = [s["xs_in0"], s["xs_in1"]]
    y_out = [s["y_out0"], s["y_out1"]]
    z_out = [s["z_out0"], s["z_out1"]]
    acc_done = [s[f"acc_done{b}"] for b in range(3)]
    acc_free = [s[f"acc_free{b}"] for b in range(3)]

    w_in = I["w_in"].rearrange("l (k p) n -> (l p) k n", p=P)
    w_out = I["w_out"].rearrange("l (k p) n -> (l p) k n", p=P)
    w_up = I["w_up"].rearrange("l (k p) n -> (l p) k n", p=P)
    w_down = I["w_down"].rearrange("l (k p) n -> (l p) k n", p=P)
    w_ada = I["w_ada"].rearrange("l (k p) n -> (l p) k n", p=P)
    x_p = I["x_prompt"].rearrange("a (b p) n -> p (a b) n", p=P)
    x_s = I["x_sample"].rearrange("a b n -> (a b) n")
    st_C = I["state_C"].rearrange("l (x u) h d v -> l x (u h) d v", u=2)
    so_C = O["s_C"].rearrange("l (x u) h d v -> l x (u h) d v", u=2)
    ADA0 = [0, 2, 1, 3]

    block = ctx.enter_context(nc.Block())

    @block.sync
    def _(sp):
        def tile(t, slot, src):
            if not (isinstance(t, int) and t < 2):
                sp.wait_ge(s["lo_done"], t - 1)
            k = src.shape[1]
            sp.dma_start(raw[:, slot, :].rearrange("p (k n) -> p k n", k=k), src).then_inc(raw_in[slot], 16)

        sp.dma_start(CR[0:1, 0:D], I["c_prompt"]).then_inc(s["c_in"], 16)
        sp.dma_start(CR[1:NB, 0:D], I["c_sample"]).then_inc(s["c_in"], 16)
        for name, r0, n in (("g_norm1", G1R, 8), ("g_norm2", G2R, 8), ("conv_b", CBR, 8), ("hn_g", HNR, 8),
                            ("b_ada", BAR, 48)):
            sp.dma_start(PR[r0:r0 + n, :], I[name].rearrange("l (r p) -> (l r) p", p=P)).then_inc(s["p_in"], 16)
        sp.dma_start(PR[CWR:CWR + 24, :], I["conv_w"].rearrange("l w (r p) -> (l w r) p", p=P)).then_inc(s["p_in"], 16)

        def ada0(n):
            if n >= 8:
                sp.wait_ge(s["ada0_mm"], n - 7)
            c = ADA0[n // 4] * 512
            k = n % 4 * 2
            sp.dma_start(araw0[:, n % 8, :].rearrange("p (k n) -> p k n", k=2),
                         w_ada[:, k:k + 2, c:c + 512]).then_inc(ar0[n % 8], 16)

        for n in range(8):
            ada0(n)
        for b in range(9):
            if b < 8:
                sp.dma_start(xin[:, b, :], x_p[:, b, :]).then_inc(xr[b], 16)
            else:
                sp.dma_start(xin[0:NS, b, :], x_s).then_inc(xr[b], 16)
        for n in range(8, 16):
            ada0(n)
        tile(0, 0, w_in[:, :, WQ:WQ + P])
        tile(1, 1, w_in[:, :, WK:WK + P])
        sp.wait_ge(s["ada0_mm"], 16)
        sp.wait_ge(s["xn_done"], 9)

        def atile(a, slot, q, c0):
            if not (isinstance(a, int) and a < 2):
                sp.wait_ge(s["alo_done"], a - 1)
            sp.dma_start(araw[:, slot, :].rearrange("p (k n) -> p k n", k=2),
                         w_ada[:, 2 * q:2 * q + 2, bass.ds(c0, 512)]).then_inc(araw_in[slot], 16)

        atile(0, 0, 0, 2048)
        atile(1, 1, 1, 2048)

        def phase1(h, first_next=None):
            cols = [WV + 256 * h, WV + P + 256 * h, WQ + P + P * h, WK + P + P * h]
            for k in range(4):
                t = T1_ + 4 * h + k
                for x in range(2):
                    a = 2 * k + x + 2
                    if isinstance(h, int) and h == H - 1 and a >= 8:
                        continue
                    atile(8 * h + a, x, a % 4, 2048 + 1024 * h + 512 * (a // 4))
                if isinstance(h, int) and h == H - 1 and k >= 2:
                    tile(t + 2, k % 2, w_in[:, :, [XC, CG][k - 2]:][:, :, 0:P])
                else:
                    tile(t + 2, k % 2, w_in[:, :, bass.ds(cols[k], P)])

        phase1(0)
        with sp.Fori(1, H - 1) as h:
            phase1(h)
        phase1(H - 1)

        def stage(c):
            if isinstance(c, int) and c == 0:
                sp.wait_ge(z_out[0], 32 * 2 * H)
                sp.wait_ge(z_out[1], 32 * 2 * H)
                sp.wait_ge(s["r_out"], 32)
                sp.wait_ge(s["cols_mm"], 1)
                sp.wait_ge(s["a_used"], 32)
                sp.wait_ge(s["m_out"], 32)
            else:
                sp.wait_ge(s["vt_done"], c)
                sp.wait_ge(s["upre_done"], c)
                sp.wait_ge(s["qi_done"], c)
                sp.wait_ge(s["ex_done"], c)
            sp.dma_start(Z[:], zp_d.rearrange("j p n -> p j n")[:, :, bass.ds(c * L, L)]).then_inc(s["z_in"], 16)
            sp.dma_start(RB[:], rp_d[:, bass.ds(c * L, L)].rearrange("(o h) n -> o h n", o=1)
                         .broadcast_to([P, H, L])).then_inc(s["rb_in"], 16)
            sp.dma_start(RU[:], rs_d[bass.ds(c, 1), :].broadcast_to([P, 16])).then_inc(s["rb_in"], 16)
            sp.dma_start(ZU[:], zs_d[bass.ds(c, 1)].rearrange("u k p n -> p (u k) n")).then_inc(s["zu_in"], 16)

        def load_cu(c):
            sp.dma_start(CU[:, :, 0:DV], st_C[0, :, bass.ds(c, 1)].rearrange("x u d v -> d (x u) v")) \
              .then_inc(s["cu_in"], 16)

        def store_cu(c):
            sp.dma_start(so_C[0, :, bass.ds(c, 1)].rearrange("x u d v -> d (x u) v"), CU[:, :, 0:DV]) \
              .then_inc(s["cu_out"], 16)

        def phase2(c, last=False):
            for k, col in ((2, BG), (3, GA)):
                tile(T2_ + 4 * c + k, k % 2, w_in[:, :, bass.ds(col + P * c, P)])
                if k == 2 and not (isinstance(c, int) and c == 0):
                    sp.wait_ge(s["ucup1_upd"], c)
                    store_cu(c - 1)
                    sp.wait_ge(s["cu_out"], 16 * c)
                    load_cu(c)
            if not last:
                stage(c + 1)
            for k in range(2):
                col = [WO, GB][k] if last else [XC + P, CG + P][k] + P * c
                tile(T2_ + 4 * c + 4 + k, k % 2, w_in[:, :, bass.ds(col, P)])

        stage(0)
        load_cu(0)
        phase2(0)
        with sp.Fori(1, NC - 1) as c:
            phase2(c)
        phase2(NC - 1, last=True)
        sp.wait_ge(s["ucup1_upd"], NC)
        store_cu(NC - 1)
        sp.wait_ge(s["c_upd"], NC)
        sp.dma_start(O["p_C"].rearrange("l b h d v -> d (l b h) v"), CA[:, :, 0:DV]).then_inc(s["st_out"], 16)
        with sp.Fori(0, KT - 1) as j:
            tile(T3_ + 2 + 2 * j, 0, w_in[:, :, bass.ds(WO + P + P * j, P)])
            tile(T3_ + 3 + 2 * j, 1, w_in[:, :, bass.ds(GB + P + P * j, P)])
        sp.wait_ge(s["fin1_copy"], 2)
        sp.dma_start(O["s_conv"].rearrange("l b w n -> (l b w) n"), NCR[0:16, :]).then_inc(s["st_out"], 16)
        sp.dma_start(O["p_conv"].rearrange("l b w n -> (l b w) n"), NCR[16:18, :]).then_inc(s["st_out"], 16)
        sp.dma_start(O["s_n"].rearrange("l b h d -> (l b h) d"), NR[:]).then_inc(s["st_out"], 16)
        sp.dma_start(O["p_n"].rearrange("l b h d -> (l b h) d"), PN[:]).then_inc(s["st_out"], 16)
        tile(T4_, 0, w_out[:, :, 0:P])
        tile(T4_ + 1, 1, w_out[:, :, P:2 * P])

        def load_xs(n, slot):
            sp.dma_start(xs[:, slot, 0:8, :], x_p[:, :, bass.ds(n * P, P)]).then_inc(xs_in[slot], 16)
            sp.dma_start(xs[0:NS, slot, 8, :], x_s[:, bass.ds(n * P, P)]).then_inc(xs_in[slot], 16)

        sp.wait_ge(s["cu_out"], 16 * NC)
        sp.wait_ge(s["st_out"], 16)
        load_xs(0, 0)
        load_xs(1, 1)
        with sp.Fori(0, KT // 2 - 1) as i:
            for x in range(2):
                tile(T4_ + 2 + 2 * i + x, x, w_out[:, :, bass.ds((2 + 2 * i + x) * P, P)])
                sp.wait_ge(s["xtr_done"], 2 * i + 1 + x)
                load_xs(2 * i + 2 + x, x)
        tile(T5_, 0, w_up[:, :, 0:P])
        tile(T5_ + 1, 1, w_up[:, :, P:2 * P])

        def mlp_tiles(f, last=False):
            for m in (2, 3):
                tile(T5_ + 8 * f + m, m % 2, w_up[:, :, bass.ds(512 * f + P * m, P)])
            for d in range(4):
                tile(T5_ + 8 * f + 4 + d, d % 2, w_down[:, bass.ds(4 * f, 4), 256 * d:256 * d + 256])
            if not last:
                for m in (0, 1):
                    tile(T5_ + 8 * f + 8 + m, m % 2, w_up[:, :, bass.ds(512 * f + 512 + P * m, P)])

        with sp.Fori(0, 7) as f:
            mlp_tiles(f)
        mlp_tiles(7, last=True)
        sp.wait_ge(s["x2n_done"], 1)
        sp.dma_start(GF[:], I["g_final"].rearrange("(o n) -> o n", o=1).broadcast_to([P, D])).then_inc(s["gf_in"], 16)
        for b in range(9):
            sp.wait_ge(s["y_done"], b + 1)
            if b < 8:
                sp.dma_start(O["y_prompt"].rearrange("a (b p) n -> p (a b) n", p=P)[:, b, :], Y[:, b % 2, :]) \
                  .then_inc(y_out[b % 2], 16)
            else:
                sp.dma_start(O["y_sample"].rearrange("a b n -> (a b) n"), Y[0:NS, 0, :]).then_inc(y_out[b % 2], 16)
        sp.wait_ge(y_out[0], 16 * 5)
        sp.wait_ge(y_out[1], 16 * 4)
        sp.wait_ge(s["st_out"], 16 * 5)

    @block.gpsimd
    def _(pool):
        n = 0

        def step(ins):
            nonlocal n
            ins.then_inc(s["pool_done"], 1)
            n += 1
            pool.wait_ge(s["pool_done"], n)

        step(pool.memset(ident[:], 0.0))
        step(pool.affine_select(out=ident[:], in_=ident[:], compare_op=ALU.not_equal, fill=1.0, base=0,
                                pattern=[[-1, P]], channel_multiplier=1))
        step(pool.memset(ones[:], 1.0))
        step(pool.memset(CM[:], 0.0))
        step(pool.affine_select(out=CM[:], in_=CM[:], compare_op=ALU.is_ge, fill=-1e30, base=0,
                                pattern=[[1, P]], channel_multiplier=-1))
        step(pool.memset(CMS[:], 0.0))
        step(pool.affine_select(out=CMS[:], in_=CMS[:], compare_op=ALU.is_ge, fill=-1e30, base=0,
                                pattern=[[1, 16]], channel_multiplier=-1))
        v = CMS[:].rearrange("p (b t) -> p b t", t=ST)
        step(pool.affine_select(out=v, in_=v, compare_op=ALU.is_ge, fill=-1e30, base=0,
                                pattern=[[-ST, 4], [0, ST]], channel_multiplier=1))
        step(pool.memset(BM[:], 1.0))
        step(pool.affine_select(out=BM[:], in_=BM[:], compare_op=ALU.is_ge, fill=0.0, base=0,
                                pattern=[[-ST, 4]], channel_multiplier=1))
        step(pool.affine_select(out=BM[:], in_=BM[:], compare_op=ALU.is_ge, fill=0.0, base=ST - 1,
                                pattern=[[ST, 4]], channel_multiplier=-1))

    POOL_STEPS = 11

    @block.scalar
    def _(act):
        own = Count(act, s["act_step"])
        act.dma_start(wg[:], w_in[:, :, WGATE:WGATE + 2 * H]).then_inc(s["small_in"], 16)
        act.wait_ge(s["sm_done"], 1)
        act.dma_start(bg15[0:H, :], I["b_gate"][:, 0:H].rearrange("l h -> h l"), allow_slow_non_contiguous=True).then_inc(s["small_in"], 16)
        act.dma_start(bg15[32:32 + H, :], I["b_gate"][:, H:2 * H].rearrange("l h -> h l"), allow_slow_non_contiguous=True).then_inc(s["small_in"], 16)
        act.dma_start(M0s[:], I["state_m"].rearrange("l b h -> h (l b)"), allow_slow_non_contiguous=True).then_inc(s["small_in"], 16)
        act.dma_start(SNR[0:NS, :], I["state_n"].rearrange("l b h d -> (l b h) d")).then_inc(s["small_in"], 16)
        act.dma_start(SCR[0:16, 0:D], I["state_conv"].rearrange("l b w n -> (l b w) n")).then_inc(s["small_in"], 16)
        act.wait_ge(s["c_in"], 32)
        act.activation(CG_[0:NB, 0:D], CR[0:NB, 0:D], ACT.Sigmoid).then_inc(s["csig_done"], 1)

        for g in range(3):
            for b in range(3 * g, 3 * g + 3):
                n = P if b < 8 else NS
                act.wait_ge(xr[b], 16)
                own.link(act.activation(A[0:n, 4 + b % 4, 0:D], xin[0:n, b, :], ACT.Square, accum_out=ss[0:n, b:b + 1]))
            if g < 2:
                act.activation(rs[:, 3 * g:3 * g + 3], ss[:, 3 * g:3 * g + 3], ACT.Sqrt, bias=epsc[:, 0:1],
                               scale=1.0 / D).then_inc(s["xrt_done"], 1)
            else:
                own.link(act.activation(rs[:, 6:8], ss[:, 6:8], ACT.Sqrt, bias=epsc[:, 0:1], scale=1.0 / D))
                act.activation(rs[0:NS, 8:9], ss[0:NS, 8:9], ACT.Sqrt, bias=epsc[0:NS, 0:1],
                               scale=1.0 / D).then_inc(s["xrt_done"], 1)
        act.wait_ge(s["ct_used"], 2)
        for b in range(9):
            n = P if b < 8 else NS
            src = (M if b % 2 == 0 else PB)[:, 0:2, :].rearrange("p a (k n) -> p (a k) n", n=P)[:, :, 0:n]
            act.wait_ge(s["xt_done"], b + 1)
            act.activation(A[:, :, b * P:b * P + n], src, ACT.Copy).then_inc(s["xt_free"], 1)
        for k in range(KT):
            act.wait_ge(s["hf_done"], k + 1)
            act.activation(XH[:, k, :], A[:, k, :], ACT.Copy).then_inc(s["h_hi"], 1)

        def hi(t, slot, free=None):
            act.wait_ge(raw_in[slot], 8 * (t - slot) + 16)
            if not (isinstance(t, int) and t < 2):
                act.wait_ge(acc_done[2], t if free is None else free)
            act.activation(whi[:, slot, :], raw[:, slot, :], ACT.Copy).then_inc(s["hi_done"], 1)

        def ahi_(a, slot):
            act.wait_ge(araw_in[slot], 8 * (a - slot) + 16)
            if not (isinstance(a, int) and a < 2):
                act.wait_ge(s["a_used"], a - 1)
            act.activation(ahi[:, slot, :], araw[:, slot, :], ACT.Copy).then_inc(s["ahi_done"], 1)

        hi(0, 0)
        hi(1, 1)
        ahi_(0, 0)
        ahi_(1, 1)

        def phase1(h):
            last = isinstance(h, int) and h == H - 1
            for k in range(4):
                t, slot = T1_ + 4 * h + k, k % 2
                if not (last and k == 3):
                    for x in range(2):
                        ahi_(8 * h + 2 * k + 2 + x, x)
                if not (isinstance(h, int) and h == 0 and k < 2):
                    act.wait_ge(z_out[slot], 64 * h + 32 * (k // 2))
                for b, (a0, a1) in enumerate(BLOCKS):
                    act.wait_ge(acc_done[b], P1_ + 4 * h + k + 1)
                    if b < 2:
                        act.activation(zr[:, slot, a0:a1], PB[:, b, 0:BLK], ACT.Copy).then_inc(acc_free[b], 1)
                    else:
                        act.activation(zr[:, slot, a0:TP], PB[:, b, 0:LP], ACT.Copy)
                        act.activation(zr[:, slot, TP:T].rearrange("p (u b t) -> p b u t", u=2, t=ST),
                                       PB[:, b, LP:BLK].rearrange("p (b u t) -> p b u t", u=2, t=ST),
                                       ACT.Copy).then_inc(acc_free[b], 1)
                hi(t + 2, slot)
                act.wait_ge(acc_free[2], P1_ + 4 * h + k + 1)
                act.dma_start(zp_d[bass.ds(4 * h + k, 1)].rearrange("o p n -> (o p) n"), zr[:, slot, 0:TP]) \
                   .then_inc(z_out[slot], 16)
                act.dma_start(zs_d.rearrange("(u h) k p n -> k h p u n", u=2)[k, bass.ds(h, 1)]
                              .rearrange("o p u n -> (o p) u n"),
                              zr[:, slot, TP:T].rearrange("p (u n) -> p u n", u=2)).then_inc(z_out[slot], 16)

        def gate_acts():
            act.wait_ge(s["gate_sum"], 1)
            own.link(act.activation(TH[:], GT[:], ACT.Tanh, bias=bg15[:, 0:1], scale=1.0 / CAP))
            own.link(act.activation(GT[32:36, :], TH[32:36, :], ACT.Exp, scale=-CAP))
            act.activation(GT[32:36, :], GT[32:36, :], ACT.Ln, bias=1.0).then_inc(s["gate_act"], 1)

        phase1(0)
        gate_acts()
        phase1(1)
        phase1(2)
        act.wait_ge(s["gate_rows"], 1)
        act.dma_start(rp_d, RR[:, 0:TP]).then_inc(s["r_out"], 16)
        act.dma_start(rs_d.rearrange("(u h) n -> h u n", u=2), RR[:, TP:T].rearrange("h (u n) -> h u n", u=2)) \
           .then_inc(s["r_out"], 16)
        act.dma_start(O["p_m"].rearrange("l b h -> h (l b)"), PM[:], allow_slow_non_contiguous=True).then_inc(s["m_out"], 16)
        act.dma_start(O["s_m"].rearrange("l b h -> h (l b)"), SMo[:], allow_slow_non_contiguous=True).then_inc(s["m_out"], 16)
        phase1(3)
        act.wait_ge(s["cols_mm"], 1)
        cp = M[:, 0, 0:NC * 3 * H].rearrange("p (c k h) -> p c k h", k=3, h=H)
        cs = M[0:16, 1, 0:24].rearrange("p (k u) -> p u k", k=3)
        act.activation(COL[:, :, GM, :], cp[:, :, GM, :], ACT.Copy)
        act.activation(COL[:, :, WS, :], cp[:, :, WS, :], ACT.Exp)
        act.activation(COL[:, :, MR, :], cp[:, :, MR, :], ACT.Exp, scale=-1.0)
        act.activation(COLS[:, :, GM], cs[:, :, GM], ACT.Copy)
        act.activation(COLS[:, :, WS], cs[:, :, WS], ACT.Exp)
        act.activation(COLS[:, :, MR], cs[:, :, MR], ACT.Exp, scale=-1.0).then_inc(s["cols_done"], 1)

        act.wait_ge(z_out[0], 32 * 2 * H)
        act.wait_ge(z_out[1], 32 * 2 * H)
        act.wait_ge(s["r_out"], 32)
        act.wait_ge(s["m_out"], 32)

        def phase2(c):
            first = isinstance(c, int) and c == 0
            act.wait_ge(s["rb_in"], 32 * c + 32)
            act.activation(IB[:], RB[:], ACT.Exp)
            act.activation(IU[:], RU[:], ACT.Exp).then_inc(s["ib_exp"], 1)
            act.wait_ge(s["ex_done"], c + 1)
            act.activation(EX[:], EX[:], ACT.Exp)
            act.activation(EU[:], EU[:], ACT.Exp).then_inc(s["e_exp"], 1)
            act.wait_ge(s["vt_done"], c + 1)
            for x in range(2):
                last = act.activation(VT[:, 2 * x:2 * x + 2, 0:DV], M[:, 1 + x, :].rearrange("p (h v) -> p h v", v=DV), ACT.Copy)
            last.then_inc(s["vt_copy"], 1)
            act.wait_ge(s["upre_done"], c + 1)
            act.activation(VTU[:, 0:DV], M[0:16, 4, 128:128 + DV], ACT.Copy).then_inc(s["vtu_copy"], 1)
            if not first:
                act.wait_ge(s["a_done"], c)
            for b, (a0, a1) in enumerate(BLOCKS):
                act.wait_ge(acc_done[b], P2_ + 4 * c + 1)
                ins = act.activation(G1[:, a0:a1], PB[:, b, 0:BLK], ACT.Copy)
                ins.then_inc(acc_free[b], 1)
            hi(T2_ + 4 * c + 2, 0)
            act.wait_ge(s["num_done"], c + 1)
            for h in range(H):
                own.link(act.activation(HT[:, h, :], M[:, h, 0:DV], ACT.Square, accum_out=sc4[:, 0, h:h + 1]))
            act.wait_ge(s["unum_done"], c + 1)
            act.activation(HTU[:], M[0:16, 4, 0:DV], ACT.Square, accum_out=sc1[:, 0:1]).then_inc(s["ss_done"], 1)
            act.wait_ge(s["var_done"], c + 1)
            act.activation(sc4[:, 1, :], sc4[:, 5, :], ACT.Sqrt, bias=epsc[:, 0:1], scale=1.0 / DV)
            act.activation(sc1[:, 1:2], sc1[:, 5:6], ACT.Sqrt, bias=epsc[0:16, 0:1], scale=1.0 / DV) \
               .then_inc(s["std_done"], 1)
            hi(T2_ + 4 * c + 3, 1)
            hi(T2_ + 4 * c + 4, 0)
            act.wait_ge(s["conv_done"], c + 1)
            for b, (a0, a1) in enumerate(BLOCKS):
                act.wait_ge(acc_done[b], P2_ + 4 * c + 4)
                ins = act.activation(U[:, a0:a1], PB[:, b, 0:BLK], ACT.Sigmoid)
                ins.then_inc(acc_free[b], 1)
            hi(T2_ + 4 * c + 5, 1)

        phase2(0)
        with act.Fori(1, NC) as c:
            phase2(c)

        act.wait_ge(s["fin1_mm"], 1)
        act.wait_ge(s["cu_out"], 16 * NC)
        act.wait_ge(s["st_out"], 16)
        act.activation(NCR[:], M[0:18, 0:2, :].rearrange("p a n -> p (a n)"), ACT.Copy).then_inc(s["fin1_copy"], 1)
        act.activation(NR[:], M[0:NS, 2, 0:P], ACT.Copy)
        act.activation(PN[:], M[0:H, 3, 0:P], ACT.Copy).then_inc(s["fin1_copy"], 1)

        def phase3(j):
            first = isinstance(j, int) and j == 0
            act.wait_ge(s["a_done"] if first else s["merged"], NC if first else j)
            for k, buf in enumerate((G1, U)):
                for b, (a0, a1) in enumerate(BLOCKS):
                    act.wait_ge(acc_done[b], P3_ + 2 * j + k + 1)
                    act.activation(buf[:, a0:a1], PB[:, b, 0:BLK], ACT.Sigmoid).then_inc(acc_free[b], 1)
                hi(T3_ + 2 * j + k + 2, k)

        phase3(0)
        with act.Fori(1, KT) as j:
            phase3(j)
        for k in range(KT):
            act.wait_ge(s["merged"], k + 1)
            if k == 0:
                act.wait_ge(acc_done[2], P4_)
            act.activation(XH[:, k, :], A[:, k, :], ACT.Copy).then_inc(s["split_hi"], 1)

        def phase4(i):
            for x in range(2):
                n = 2 * i + x
                act.wait_ge(s["xtr_done"], n + 1)
                if not (isinstance(i, int) and n == 0):
                    act.wait_ge(acc_free[2], P4_ + n)
                act.activation(xT[:, 0:TP], M[:, 0:2, :].rearrange("p a n -> p (a n)"), ACT.Copy)
                act.activation(xT[:, TP:T], M[:, 2, 0:NS], ACT.Copy).then_inc(s["xtr_copy"], 1)
                act.wait_ge(acc_free[2], P4_ + n + 1)
                act.activation(SQ[:], A[:, bass.ds(n, 1), :].rearrange("p o n -> p (o n)"), ACT.Square) \
                   .then_inc(s["sq_done"], 1)
                hi(T4_ + n + 2, x)

        phase4(0)
        with act.Fori(1, KT // 2) as i:
            phase4(i)
        act.wait_ge(s["ms_mm"], 1)
        act.wait_ge(s["st_out"], 16 * 5)
        for b, (a0, a1) in enumerate(BLOCKS):
            ins = act.activation(R[:, 0, a0:a1], M[:, 2 + b, 0:BLK], ACT.Sqrt, bias=epsc[:, 0:1], scale=1.0 / D)
            ins.then_inc(s["ms_sqrt"], 1)
        for k in range(KT):
            act.wait_ge(s["h2_scaled"], k + 1)
            act.activation(XH[:, k, :], R[:, 1 + k % 2, :], ACT.Copy).then_inc(s["h2_hi"], 1)

        def phase5(f, last=False):
            for m in range(FT):
                if not (isinstance(f, int) and f == 0 and m == 0):
                    act.wait_ge(s["act_lo"], FT * f + m)
                for b, (a0, a1) in enumerate(BLOCKS):
                    act.wait_ge(acc_done[b], P5_ + 12 * f + m + 1)
                    act.activation(R[:, 0, a0:a1], PB[:, b, 0:BLK], ACT.Relu).then_inc(acc_free[b], 1)
                hi(T5_ + 8 * f + m + 2, m % 2, P5_ + 12 * f + m + 1)
                act.wait_ge(s["rr_done"], FT * f + m + 1)
                act.activation(AH[:, m, :], R[:, 0, :], ACT.Copy).then_inc(s["act_hi"], 1)
            for d in range(4):
                if not (last and d >= 2):
                    hi(T5_ + 8 * f + 4 + d + 2, d % 2, P5_ + 12 * f + 4 + 2 * d + 2)

        phase5(0)
        with act.Fori(1, 7) as f:
            phase5(f)
        phase5(7, last=True)
        for b in range(9):
            n = P if b < 8 else NS
            act.wait_ge(s["y_mm"], b + 1)
            bank = 2 * (b % 2)
            act.activation(R[0:n, b % 2, 0:D],
                           M[0:n, bank:bank + 2, :].rearrange("p a n -> p (a n)"), ACT.Square,
                           accum_out=ss[0:n, b:b + 1]).then_inc(s["y_sq"], 1)
            act.wait_ge(s["y_sq"], b + 1)
            act.activation(rs[0:n, b:b + 1], ss[0:n, b:b + 1], ACT.Sqrt, bias=epsc[0:n, 0:1], scale=1.0 / D) \
               .then_inc(s["y_std"], 1)

    @block.tensor
    def _(pe):
        def turn(dst, src):
            n = src.shape[0]
            return pe.transpose(dst, src, ident[0:n, 0:n])

        pe.wait_ge(s["pool_done"], 2)
        pe.wait_ge(s["p_in"], 16 * 6)
        turn(M[:, 2, 0:PROWS], PR[0:PROWS, :])
        pe.wait_ge(s["csig_done"], 2)
        pe.wait_ge(s["small_in"], 16 * 6)
        for k in range(KT):
            turn(M[:, 2, 128 + NB * k:128 + NB * (k + 1)], CG_[0:NB, k * P:(k + 1) * P])
        turn(M[:, 2, 256:256 + NS], SNR[0:NS, :])
        for k in range(KT):
            ins = turn(M[:, 2, 288 + 16 * k:304 + 16 * k], SCR[0:16, k * P:(k + 1) * P])
        ins.then_inc(s["ct_done"], 1)
        pe.wait_ge(s["ct_used"], 1)

        def ada0(q):
            if q >= 2:
                pe.wait_ge(s["arow_done"], q - 1)
            for n in range(4 * q, 4 * q + 4):
                pe.wait_ge(ar0[n % 8], 16 * (n // 8 + 1))
                for x in range(2):
                    ins = pe.matmul(M[0:NB, 3 + q % 2, :], cT[:, n % 4 * 2 + x, :],
                                    araw0[:, n % 8, 512 * x:512 * x + 512], start=(n % 4 + x == 0), stop=(n % 4 == 3 and x == 1))
                ins.then_inc(s["ada0_mm"], 1)

        def rowt0(q):
            pe.wait_ge(s["arow_done"], q + 1)
            for x in range(4):
                ins = turn(PB[:, 2, 64 * q + 16 * x:64 * q + 16 * x + NB], AROW[0:NB, P * x:P * x + P])
            ins.then_inc(s["rowt_done"], 1)

        def xturn(b):
            n = P if b < 8 else NS
            pe.wait_ge(s["xn_done"], b + 1)
            if b >= 2:
                pe.wait_ge(s["xt_free"], b - 1)
            dst = M if b % 2 == 0 else PB
            for k in range(KT):
                ins = turn(dst[:, k // 4, P * (k % 4):P * (k % 4) + n], xin[0:n, b, k * P:(k + 1) * P])
            ins.then_inc(s["xt_done"], 1)

        ada0(0)
        rowt0(0)
        ada0(1)
        rowt0(1)
        for b in range(3):
            xturn(b)
        ada0(2)
        rowt0(2)
        for b in range(3, 6):
            xturn(b)
        ada0(3)
        rowt0(3)
        for b in range(6, 9):
            xturn(b)
        pe.wait_ge(s["gw_done"], 1)
        pe.wait_ge(s["xt_free"], 9)
        pe.wait_ge(s["mod_done"], 4)
        for b, (a0, a1) in enumerate(BLOCKS):
            for k in range(KT):
                pe.wait_ge(s["h_lo"], k + 1)
                for part in (XH, XL):
                    ins = pe.matmul(PB[:, b, 0:BLK], GW[:, k, :], part[:, k, a0:a1],
                                    start=(k == 0 and part is XH), stop=(k == KT - 1 and part is XL))
            ins.then_inc(acc_done[b], 1)

        def product(p, slot, xh, xl, n_k, w_stride, w_off, ready=None):
            for b, (a0, a1) in enumerate(BLOCKS):
                pe.wait_ge(acc_free[b], p)
                for k in range(n_k):
                    if ready is not None and b == 0:
                        ready(k)
                    w0 = w_stride * k + w_off
                    for j, (w, x) in enumerate(((whi, xh), (whi, xl), (wlo, xh))):
                        ins = pe.matmul(PB[:, b, 0:BLK], w[:, slot, w0:w0 + P], x[:, k, a0:a1],
                                        start=(k == 0 and j == 0), stop=(k == n_k - 1 and j == 2))
                ins.then_inc(acc_done[b], 1)

        def wide(t, p, slot, ready=None):
            pe.wait_ge(s["lo_done"], t + 1)
            product(p, slot, XH, XL, KT, P, 0, ready)

        def phase1(h):
            for k in range(4):
                for x in range(2):
                    a = 2 * k + x
                    pe.wait_ge(s["alo_done"], 8 * h + a + 1)
                    if a % 4 == 0:
                        pe.wait_ge(s["arow_done"], 4 + 2 * h + a // 4)
                    for y in range(2):
                        for w in (ahi, alo):
                            ins = pe.matmul(M[:, 4, :], cS[:, 2 * (a % 4) + y, :], w[:, x, 512 * y:512 * y + 512],
                                            start=(a % 4 == 0 and y == 0 and w is ahi), stop=(a % 4 == 3 and y == 1 and w is alo))
                    ins.then_inc(s["a_used"], 1)
                wide(T1_ + 4 * h + k, P1_ + 4 * h + k, k % 2)
                if k % 2 == 1:
                    pe.wait_ge(s["arow_done"], 4 + 2 * h + k // 2 + 1)
                    pe.wait_ge(s["mod_done"], 4 + 2 * h + k // 2)
                    for x in range(4):
                        ins = turn(M[:, 3, P * x:P * x + P], AROW[:, P * x:P * x + P])
                    ins.then_inc(s["rowt_done"], 1)

        with pe.Fori(0, H) as h:
            phase1(h)

        pe.wait_ge(s["gate_rows"], 1)
        for c in range(NC):
            for kind, row in ((GM, GMR), (WS, WSR), (MR, MRR)):
                j = (c * 3 + kind) * H
                turn(M[:, 0, j:j + H], row[:, c * L:(c + 1) * L])
        for kind, row in ((GM, GMR), (WS, WSR), (MR, MRR)):
            for u in range(2):
                ins = turn(M[0:16, 1, 8 * kind + H * u:8 * kind + H * u + H], row[:, TP + 16 * u:TP + 16 * u + 16])
        ins.then_inc(s["cols_mm"], 1)

        def phase2(c):
            first = isinstance(c, int) and c == 0
            pe.wait_ge(s["z_in"], 16 * c + 16)
            pe.wait_ge(s["zu_in"], 16 * c + 16)
            if first:
                pe.wait_ge(s["cols_done"], 1)
                pe.wait_ge(s["mod_done"], 12)
            else:
                pe.wait_ge(s["hm_done"], c)
                pe.wait_ge(s["ucup1_upd"], c)
            for h in range(H):
                ins = pe.matmul(M[:, 0, h * L:(h + 1) * L], Z[:, 4 * h + 1, :], Z[:, 4 * h, :], start=True, stop=True)
            ins.then_inc(s["qk_done"], 1)
            for h in range(H):
                ins = turn(M[:, 3, h * DK:(h + 1) * DK], Z[:, 4 * h + 1, :])
            ins.then_inc(s["kt_done"], 1)
            for j in range(2 * H):
                ins = turn(M[:, 1 + j // 4, P * (j % 4):P * (j % 4) + P], Z[:, 4 * (j // 2) + 2 + j % 2, :])
            ins.then_inc(s["vt_done"], 1)
            pe.matmul(M[0:16, 4, 0:16], ZU[:, 1, :], ZU[:, 0, :], start=True, stop=True)
            for x in range(2):
                turn(M[0:16, 4, 128 + P * x:256 + P * x], ZU[:, 2 + x, :])
            turn(M[0:16, 4, 384:512], ZU[:, 1, :]).then_inc(s["upre_done"], 1)
            wide(T2_ + 4 * c, P2_ + 4 * c, 0)
            pe.wait_ge(s["p_done"], c + 1)
            pe.wait_ge(s["qi_done"], c + 1)
            pe.wait_ge(s["vt_copy"], c + 1)
            pe.wait_ge(s["kw_done"], c + 1)
            if not first:
                pe.wait_ge(s["c_upd"], c)
            for h in range(H):
                pe.matmul(M[:, h, 0:DV + 1], EX[:, h, :], VT[:, h, :], start=True, stop=False)
                ins = pe.matmul(M[:, h, 0:DV + 1], IB[:, h, :], CA[:, h, :], start=False, stop=True)
            ins.then_inc(s["num_done"], 1)
            pe.wait_ge(s["vtu_copy"], c + 1)
            pe.wait_ge(s["cn_done"], c + 1)
            pe.wait_ge(s["cu_in"], 16 * c + 16)
            for b in range(4):
                pe.matmul(M[0:16, 4, 0:DV + 1], QM[:, 16 * b:16 * b + 16], CU[:, b, :], start=(b == 0), stop=False)
            pe.matmul(M[0:16, 4, 0:DV + 1], EU[:], VTU[:], start=False, stop=True).then_inc(s["unum_done"], 1)
            wide(T2_ + 4 * c + 1, P2_ + 4 * c + 1, 1)
            pe.wait_ge(s["ht_ready"], c + 1)
            for h in range(H):
                ins = pe.matmul(M[:, h, 0:DV + 1], KW[:, h, :], VT[:, h, :], start=True, stop=True)
            ins.then_inc(s["cup_done"], 1)
            pe.matmul(M[:, 4, 0:DV + 1], KU[:, 0, :], VTU[:], start=True, stop=True).then_inc(s["ucup0_done"], 1)
            wide(T2_ + 4 * c + 2, P2_ + 4 * c + 2, 0)
            pe.wait_ge(s["c_upd"], c + 1)
            for j in range(2 * H):
                ins = turn(M[:, j // 4, P * (j % 4):P * (j % 4) + P], HT[:, j // 2, P * (j % 2):P * (j % 2) + P])
            ins.then_inc(s["ht_done"], 1)
            pe.wait_ge(s["ucup0_upd"], c + 1)
            for b in range(1, 4):
                ins = pe.matmul(M[:, 1 + b, 0:DV + 1], KU[:, b, :], VTU[:], start=True, stop=True)
            for x in range(2):
                ins = turn(M[:, 4, 320 + 16 * x:336 + 16 * x], HTU[:, P * x:P * x + P])
            ins.then_inc(s["ucup1_done"], 1)
            wide(T2_ + 4 * c + 3, P2_ + 4 * c + 3, 1)

        phase2(0)
        with pe.Fori(1, NC) as c:
            phase2(c)

        pe.wait_ge(s["hm_done"], NC)
        pe.wait_ge(s["ucup1_upd"], NC)
        for k in range(KT):
            turn(M[0:18, k // 4, P * (k % 4):P * (k % 4) + P], NCV[:, k, :])
        turn(M[0:NS, 2, 0:P], NT_[:])
        turn(M[0:H, 3, 0:P], CA[:, :, DV]).then_inc(s["fin1_mm"], 1)

        with pe.Fori(0, KT) as j:
            wide(T3_ + 2 * j, P3_ + 2 * j, 0)
            wide(T3_ + 2 * j + 1, P3_ + 2 * j + 1, 1)

        def merged_ready(k):
            pe.wait_ge(s["merged_lo"], k + 1)

        def phase4(i):
            for x in range(2):
                n = 2 * i + x
                pe.wait_ge(xs_in[x], 32 * i + 32)
                if isinstance(i, int) and n == 0:
                    pe.wait_ge(s["fin1_copy"], 2)
                else:
                    pe.wait_ge(s["xtr_copy"], n)
                for b in range(8):
                    turn(M[:, b // 4, P * (b % 4):P * (b % 4) + P], xs[:, x, b, :])
                turn(M[:, 2, 0:NS], xs[0:NS, x, 8, :]).then_inc(s["xtr_done"], 1)
                wide(T4_ + n, P4_ + n, x, merged_ready)

        phase4(0)
        with pe.Fori(1, KT // 2) as i:
            phase4(i)
        pe.wait_ge(s["x2n_done"], 1)
        for b, (a0, a1) in enumerate(BLOCKS):
            ins = pe.matmul(M[:, 2 + b, 0:BLK], ones[:], SQA[:, a0:a1], start=True, stop=True)
        ins.then_inc(s["ms_mm"], 1)

        def h2_ready(k):
            pe.wait_ge(s["h2_lo"], k + 1)

        def phase5(f):
            for m in range(FT):
                wide(T5_ + 8 * f + m, P5_ + 12 * f + m, m % 2, h2_ready)

            def act_ready(k):
                pe.wait_ge(s["act_lo"], FT * f + k + 1)

            for d in range(4):
                pe.wait_ge(s["lo_done"], T5_ + 8 * f + 4 + d + 1)
                for y in range(2):
                    product(P5_ + 12 * f + 4 + 2 * d + y, d % 2, AH, AL, FT, 256, P * y, act_ready)

        with pe.Fori(0, 8) as f:
            phase5(f)

        pe.wait_ge(s["ys_done"], 1)
        for b in range(9):
            n = P if b < 8 else NS
            if b >= 2:
                pe.wait_ge(s["y_done"], b - 1)
            for k in range(KT):
                ins = turn(M[0:n, 2 * (b % 2) + k // 4, P * (k % 4):P * (k % 4) + P], A[:, k, P * b:P * b + n])
            ins.then_inc(s["y_mm"], 1)

    @block.vector
    def _(dve):
        own = Count(dve, s["dve_step"])
        link, mark = own.link, own.mark

        def stt(out, in0, scalar, in1, op0, op1):
            return dve.scalar_tensor_tensor(out=out, in0=in0, scalar=scalar, in1=in1, op0=op0, op1=op1)

        def lo(t, slot):
            dve.wait_ge(s["hi_done"], t + 1)
            dve.tensor_tensor(wlo[:, slot, :], raw[:, slot, :], whi[:, slot, :].bitcast(F32), ALU.subtract) \
               .then_inc(s["lo_done"], 1)

        def alo_(a, slot):
            dve.wait_ge(s["ahi_done"], a + 1)
            dve.tensor_tensor(alo[:, slot, :], araw[:, slot, :], ahi[:, slot, :].bitcast(F32), ALU.subtract) \
               .then_inc(s["alo_done"], 1)

        dve.memset(epsc[:], EPS)
        dve.memset(bg15[:], 0.0).then_inc(s["sm_done"], 1)
        dve.memset(cS[:].bitcast(F32), 0.0)
        dve.memset(GW[:].bitcast(F32), 0.0)
        dve.wait_ge(s["csig_done"], 1)
        dve.tensor_tensor(CG_[0:NB, 0:D], CG_[0:NB, 0:D], CR[0:NB, 0:D], ALU.mult).then_inc(s["csig_done"], 1)
        dve.wait_ge(s["ct_done"], 1)
        dve.tensor_copy(PC[:], M[:, 2, 0:PROWS])
        ct = M[:, 2, 128:128 + NB * KT].rearrange("p (k c) -> p k c", c=NB)
        dve.tensor_copy(cT[:], ct).then_inc(s["ct_used"], 1)
        dve.tensor_copy(NT_[:], M[:, 2, 256:256 + NS])
        dve.tensor_copy(SCV[:], M[:, 2, 288:416].rearrange("p (k c) -> p k c", c=16)).then_inc(s["ct_used"], 1)
        dve.wait_ge(s["ct_used"], 2)
        link(dve.tensor_copy(cS[:, :, 0:NB], cT[:]))
        dve.tensor_tensor(cS[:, :, 32:32 + NB], cT[:], cS[:, :, 0:NB].bitcast(F32), ALU.subtract)
        dve.wait_ge(s["small_in"], 16 * 6)
        for x in range(2):
            mark(dve.tensor_copy(GW[:, :, 32 * x:32 * x + H], wg[:, :, H * x:H * x + H]))
        own.wait(own.base + own.n)
        for x in range(2):
            ins = dve.tensor_tensor(GW[:, :, 64 + 32 * x:64 + 32 * x + H], wg[:, :, H * x:H * x + H],
                                    GW[:, :, 32 * x:32 * x + H].bitcast(F32), ALU.subtract)
        ins.then_inc(s["gw_done"], 1)
        link(dve.tensor_scalar(bg15[:], bg15[:], 1.0 / CAP, None, ALU.mult))

        def arow0(q):
            dve.wait_ge(s["ada0_mm"], 4 * q + 4)
            if q >= 1:
                dve.wait_ge(s["rowt_done"], q)
            dve.tensor_copy(AROW[0:NB, :], M[0:NB, 3 + q % 2, :]).then_inc(s["arow_done"], 1)
            dve.wait_ge(s["rowt_done"], q + 1)
            j = 4 * ADA0[q]
            dve.tensor_tensor(MOD[:, j:j + 4, :], PB[:, 2, 64 * q:64 * q + 64].rearrange("p (x c) -> p x c", c=16)[:, :, 0:NB],
                              PC[:, BAR + j:BAR + j + 4].rearrange("p (x o) -> p x o", o=1).to_broadcast([P, 4, NB]), ALU.add) \
               .then_inc(s["mod_done"], 1)

        def xnorm(g):
            dve.wait_ge(s["xrt_done"], g + 1)
            if g < 2:
                link(dve.reciprocal(rs[:, 3 * g:3 * g + 3], rs[:, 3 * g:3 * g + 3]))
            else:
                link(dve.reciprocal(rs[:, 6:8], rs[:, 6:8]))
                link(dve.reciprocal(rs[0:NS, 8:9], rs[0:NS, 8:9]))
            for b in range(3 * g, 3 * g + 3):
                n = P if b < 8 else NS
                dve.tensor_scalar(xin[0:n, b, :], xin[0:n, b, :], rs[0:n, b:b + 1], None, ALU.mult).then_inc(s["xn_done"], 1)

        arow0(0)
        arow0(1)
        xnorm(0)
        arow0(2)
        xnorm(1)
        arow0(3)
        xnorm(2)
        dve.wait_ge(s["mod_done"], 4)
        link(stt(S1[:], MOD[:, 8:16, :], 1.0, PC[:, G1R:G1R + 8].rearrange("p (x o) -> p x o", o=1).to_broadcast([P, KT, NB]),
                 ALU.add, ALU.mult))
        dve.wait_ge(s["xt_free"], 9)

        def bc(ap, n=ST):
            return ap.rearrange("p k (b o) -> p k b o", o=1).to_broadcast([P, ap.shape[1], SB, n])

        xs_all = A[:, :, TP:T].rearrange("p k (b t) -> p k b t", t=ST)
        for k0 in (0, 4):
            link(dve.tensor_tensor(xs_all[:, k0:k0 + 4].rearrange("p k b t -> p k b t"), xs_all[:, k0:k0 + 4], bc(S1[:, k0:k0 + 4, 1:NB]), ALU.mult))
        for k0 in (0, 4):
            link(dve.tensor_tensor(xs_all[:, k0:k0 + 4], xs_all[:, k0:k0 + 4], bc(MOD[:, k0:k0 + 4, 1:NB]), ALU.add))

        def h_lo(k):
            dve.wait_ge(s["h_hi"], k + 1)
            dve.tensor_tensor(XL[:, k, :], A[:, k, :], XH[:, k, :].bitcast(F32), ALU.subtract).then_inc(s["h_lo"], 1)

        for k in range(KT):
            dve.tensor_scalar(A[:, k, 0:TP], A[:, k, 0:TP], S1[:, k, 0:1], MOD[:, k, 0:1], ALU.mult, ALU.add) \
               .then_inc(s["hf_done"], 1)
            if k >= 1:
                h_lo(k - 1)
        h_lo(KT - 1)
        lo(0, 0)
        lo(1, 1)
        alo_(0, 0)
        alo_(1, 1)

        def phase1(h):
            last = isinstance(h, int) and h == H - 1
            for k in range(4):
                if not (last and k == 3):
                    for x in range(2):
                        alo_(8 * h + 2 * k + 2 + x, x)
                q = 4 + 2 * h + k // 2
                if k % 2 == 1:
                    dve.wait_ge(s["a_used"], 8 * h + 4 * (k // 2) + 4)
                    dve.wait_ge(s["rowt_done"], q)
                    dve.tensor_copy(AROW[:], M[:, 4, :]).then_inc(s["arow_done"], 1)
                    lo(T1_ + 4 * h + k + 2, k % 2)
                    dve.wait_ge(s["rowt_done"], q + 1)
                    ps = M[:, 3, :].rearrange("p (x c) -> p x c", c=P)
                    dst = MOD[:, bass.ds(4 * q, 4), :]
                    link(dve.tensor_tensor(dst, ps[:, :, 0:NB],
                                           PC[:, bass.ds(BAR + 4 * q, 4)].rearrange("p (x o) -> p x o", o=1).to_broadcast([P, 4, NB]),
                                           ALU.add))
                    dve.tensor_tensor(dst, ps[:, :, 32:32 + NB], dst, ALU.add).then_inc(s["mod_done"], 1)
                else:
                    lo(T1_ + 4 * h + k + 2, k % 2)

        def gate_sums():
            for b, (a0, a1) in enumerate(BLOCKS):
                dve.wait_ge(acc_done[b], 1)
                link(dve.tensor_copy(GT[:, a0:a1], PB[64:100, b, 0:BLK]))
                dve.tensor_tensor(GT[:, a0:a1], PB[0:36, b, 0:BLK], GT[:, a0:a1], ALU.add).then_inc(acc_free[b], 1)
            dve.wait_ge(acc_free[2], 1)
            dve.memset(RMK[:], 1.0).then_inc(s["gate_sum"], 1)
            dve.wait_ge(s["gate_sum"], 1)
            link(dve.memset(RMK[:, 0:TP].rearrange("p (c n) -> p c n", n=L)[:, :, 0:1], 0.0))

        def chunks(ap):
            return ap[:, 0:TP].rearrange("p (c n) -> p c n", n=L)

        def steps(ap):
            return ap[:, TP:T].rearrange("p (b t) -> p b t", t=ST)

        def units(ap):
            return ap[:, TP:T].rearrange("p (u b t) -> p b u t", u=2, t=ST)

        def nat(ap):
            return ap[:, TP:T].rearrange("p (b u t) -> p b u t", u=2, t=ST)

        def bcs(ap):
            return ap.rearrange("p (b u o) -> p b u o", u=2, o=1).to_broadcast([H, SB // 2, 2, ST])

        def gate_cumsum():
            dve.wait_ge(s["gate_act"], 1)
            link(dve.tensor_tensor_scan(NBr[32:36, 0:TP], RMK[32:36, 0:TP], GT[32:36, 0:TP], 0.0, ALU.mult, ALU.add))
            nb, lf = steps(NBr[32:36]), steps(GT[32:36])
            link(dve.tensor_copy(nb[:, :, 0], lf[:, :, 0]))
            for t in range(1, ST):
                link(dve.tensor_tensor(nb[:, :, t], nb[:, :, t - 1], lf[:, :, t], ALU.add))
            link(dve.tensor_copy(NB0, NBr[32:36, :]))
            link(dve.memset(DL[:, 0:TP], 0.0))
            link(stt(GT[0:H, :], TH[0:H, :], CAP, NB0, ALU.mult, ALU.add))
            link(dve.tensor_scalar(chunks(DL)[:, 1:NC, 0], chunks(NB0)[:, 0:NC - 1, L - 1], -1.0, None, ALU.mult))

        def gate_max():
            G = GT[0:H]
            link(dve.tensor_tensor_scan(MU[:, 0:TP], DL[:, 0:TP], G[:, 0:TP], 0.0, ALU.add, ALU.max))
            link(dve.memset(MP[:], 0.0))
            mu, g = steps(MU), steps(G)
            link(dve.tensor_tensor(mu[:, :, 0], M0s[:], g[:, :, 0], ALU.max))
            for t in range(1, ST):
                link(dve.tensor_tensor(mu[:, :, t], mu[:, :, t - 1], g[:, :, t], ALU.max))
            cmu, cnb = chunks(MU), chunks(NB0)
            mark(dve.tensor_tensor(MP[:, 1:NC], cmu[:, 0:NC - 1, L - 1], cnb[:, 0:NC - 1, L - 1], ALU.subtract))
            mark(dve.tensor_tensor(PM[:], MU[:, TP - 1:TP], NB0[:, TP - 1:TP], ALU.subtract))
            link(dve.tensor_tensor(SMo[:], mu[:, :, ST - 1], steps(NB0)[:, :, ST - 1], ALU.subtract))
            mp = MP[:].rearrange("p (c o) -> p c o", o=1).to_broadcast([H, NC, L])
            mul = cmu[:, :, L - 1:L].to_broadcast([H, NC, L])
            m0 = bcs(M0s[:])
            mus = nat(MU)[:, :, :, ST - 1:ST].to_broadcast([H, SB // 2, 2, ST])
            sub = ALU.subtract
            dve.tensor_tensor(chunks(RR), mp, cmu, sub)
            dve.tensor_tensor(chunks(GMR), chunks(G), mp, sub)
            dve.tensor_tensor(chunks(WSR), chunks(G), mul, sub)
            dve.tensor_tensor(MRR[:, 0:TP], MU[:, 0:TP], NB0[:, 0:TP], sub)
            dve.tensor_tensor(units(RR), m0, nat(MU), sub)
            dve.tensor_tensor(units(GMR), nat(G), m0, sub)
            dve.tensor_tensor(units(WSR), nat(G), mus, sub)
            dve.tensor_tensor(units(MRR), nat(MU), nat(NB0), sub).then_inc(s["gate_rows"], 1)

        gate_sums()
        phase1(0)
        gate_cumsum()
        phase1(1)
        gate_max()
        phase1(2)
        phase1(3)
        dve.wait_ge(s["mod_done"], 12)
        link(stt(S2[:], MOD[:, 32:40, :], 1.0, PC[:, G2R:G2R + 8].rearrange("p (x o) -> p x o", o=1).to_broadcast([P, KT, NB]),
                 ALU.add, ALU.mult))
        dve.wait_ge(s["cols_done"], 1)
        dve.wait_ge(z_out[0], 32 * 2 * H)
        dve.wait_ge(z_out[1], 32 * 2 * H)
        dve.wait_ge(s["r_out"], 32)
        dve.wait_ge(s["a_used"], 32)
        dve.memset(CA[:], 0.0)
        dve.memset(VT[:, :, DV:DV + 1], 1.0)
        dve.memset(VTU[:, DV:DV + 1], 1.0)
        dve.memset(U[:, 0:2], 0.0)
        link(dve.memset(QM[:], 0.0))
        dve.wait_ge(s["pool_done"], POOL_STEPS)

        base2 = own.base + own.n
        PER2 = 21

        def phase2(c, last=False):
            own.turn(base2, c, PER2)
            first = isinstance(c, int) and c == 0
            col = COL[:, bass.ds(c, 1), :, :].rearrange("p c k h -> p (c k) h")
            cols = COLS[:, bass.ds(c, 1), :].rearrange("p c k -> p (c k)")
            dve.wait_ge(s["rb_in"], 32 * c + 32)
            for h in range(H):
                stt(EX[:, h, :], RB[:, h, :], col[:, GM, h:h + 1], CM[:], ALU.add, ALU.min)
            stt(EU[:], RU[0:16, :], cols[:, GM:GM + 1], CMS[:], ALU.add, ALU.min).then_inc(s["ex_done"], 1)
            dve.wait_ge(s["ib_exp"], c + 1)
            dve.tensor_copy(DEC[:], IB[:, :, L - 1])
            mark(dve.tensor_copy(DECU[:], IU[:].rearrange("p (b t) -> p b t", t=ST)[:, :, ST - 1]))
            dve.wait_ge(s["z_in"], 16 * c + 16)
            dve.wait_ge(s["zu_in"], 16 * c + 16)
            own.wait(own.base + own.n)
            q = Z[:].rearrange("p (h k) n -> p h k n", k=4)[:, :, 0, :]
            dve.tensor_tensor(IB[:], q, IB[:], ALU.mult)
            dve.tensor_tensor(QM[:].rearrange("p (b x) -> p b x", x=20)[:, :, 0:ST], ZU[:, 0, :].rearrange("p (b t) -> p b t", t=ST),
                              IU[:].rearrange("p (b t) -> p b t", t=ST), ALU.mult).then_inc(s["qi_done"], 1)
            dve.wait_ge(s["qk_done"], c + 1)
            dve.wait_ge(s["e_exp"], c + 1)
            stt(EX[:], M[:, 0, :].rearrange("p (h n) -> p h n", n=L), KSCALE, EX[:], ALU.mult, ALU.mult)
            dve.wait_ge(s["vtu_copy"], c + 1)
            stt(EU[:], M[0:16, 4, 0:16], KSCALE, EU[:], ALU.mult, ALU.mult).then_inc(s["p_done"], 1)
            link(dve.tensor_scalar(WM[:], BM[:], cols[:, WS:WS + 1], KSCALE, ALU.mult, ALU.mult))
            for h in range(H):
                dve.tensor_scalar(KW[:, h, :], M[:, 3, h * DK:(h + 1) * DK], col[:, WS, h:h + 1], KSCALE, ALU.mult, ALU.mult)
            for b in range(4):
                ins = dve.tensor_scalar(KU[:, b, :], M[0:16, 4, 384:512], WM[:, b:b + 1], None, ALU.mult)
            ins.then_inc(s["kw_done"], 1)
            nsel = NT_[:].rearrange("p (x u) -> p u x", u=2 * H)[:, bass.ds(c, 1), :].rearrange("p u x -> p (u x)")
            dve.tensor_copy(CU[:, :, DV], nsel).then_inc(s["cn_done"], 1)
            lo(T2_ + 4 * c + 2, 0)
            dve.wait_ge(s["ss_done"], c + 1)
            den, denu = M[:, 0:H, DV], M[0:16, 4, DV:DV + 1]
            mark(stt(sc4[:, 2, :], den, -1.0, col[:, MR, :], ALU.mult, ALU.max))
            link(stt(sc1[:, 2:3], denu, -1.0, cols[:, MR:MR + 1], ALU.mult, ALU.max))
            mark(dve.tensor_tensor(sc4[:, 2, :], den, sc4[:, 2, :], ALU.max))
            link(dve.tensor_tensor(sc1[:, 2:3], denu, sc1[:, 2:3], ALU.max))
            mark(dve.reciprocal(sc4[:, 3, :], sc4[:, 2, :]))
            link(dve.reciprocal(sc1[:, 3:4], sc1[:, 2:3]))
            mark(dve.tensor_tensor(sc4[:, 4, :], sc4[:, 3, :], sc4[:, 3, :], ALU.mult))
            link(dve.tensor_tensor(sc1[:, 4:5], sc1[:, 3:4], sc1[:, 3:4], ALU.mult))
            dve.tensor_tensor(sc4[:, 5, :], sc4[:, 4, :], sc4[:, 0, :], ALU.mult)
            dve.tensor_tensor(sc1[:, 5:6], sc1[:, 4:5], sc1[:, 0:1], ALU.mult).then_inc(s["var_done"], 1)
            dve.wait_ge(s["std_done"], c + 1)
            mark(dve.reciprocal(sc4[:, 6, :], sc4[:, 1, :]))
            link(dve.reciprocal(sc1[:, 6:7], sc1[:, 1:2]))
            mark(dve.tensor_tensor(sc4[:, 7, :], sc4[:, 6, :], sc4[:, 3, :], ALU.mult))
            link(dve.tensor_tensor(sc1[:, 7:8], sc1[:, 6:7], sc1[:, 3:4], ALU.mult))
            for h in range(H):
                dve.tensor_scalar(HT[:, h, :], M[:, h, 0:DV], sc4[:, 7, h:h + 1], None, ALU.mult)
            dve.tensor_scalar(HTU[:], M[0:16, 4, 0:DV], sc1[:, 7:8], None, ALU.mult).then_inc(s["ht_ready"], 1)
            us = U[:, 2 + TP:].rearrange("p (b x) -> p b x", x=6)
            for b, (a0, a1) in enumerate(BLOCKS):
                dve.wait_ge(acc_done[b], P2_ + 4 * c + 2)
                if b == 0:
                    dve.wait_ge(acc_free[2], P2_ + 4 * c + 1)
                if b < 2:
                    dve.tensor_tensor(U[:, 2 + a0:2 + a1], PB[:, b, 0:BLK], G1[:, a0:a1], ALU.mult).then_inc(acc_free[b], 1)
                else:
                    dve.tensor_tensor(U[:, 2 + a0:2 + TP], PB[:, b, 0:LP], G1[:, a0:TP], ALU.mult)
                    dve.tensor_tensor(us[:, :, 2:6], PB[:, b, LP:BLK].rearrange("p (b t) -> p b t", t=ST),
                                      G1[:, TP:T].rearrange("p (b t) -> p b t", t=ST), ALU.mult).then_inc(acc_free[b], 1)
            lo(T2_ + 4 * c + 3, 1)
            scv = SCV[:, bass.ds(c, 1), :].rearrange("p c (b w) -> p (c b) w", w=2)
            mark(dve.memset(U[:, 0:2], 0.0))
            link(dve.tensor_copy(us[:, :, 0:2], scv))
            ncv = NCV[:, bass.ds(c, 1), :].rearrange("p c n -> p (c n)")
            dve.tensor_copy(ncv[:, 16:18], U[:, TP:TP + 2])
            dve.tensor_copy(ncv[:, 0:16].rearrange("p (b w) -> p b w", w=2), us[:, :, 4:6])
            g1s = G1[:, TP:T].rearrange("p (b t) -> p b t", t=ST)

            def cw(w):
                return PC[:, bass.ds(CWR + 8 * w + c, 1)]

            mark(dve.tensor_scalar(G1[:, 0:TP], U[:, 0:TP], cw(0), PC[:, bass.ds(CBR + c, 1)], ALU.mult, ALU.add))
            link(dve.tensor_scalar(g1s, us[:, :, 0:4], cw(0), PC[:, bass.ds(CBR + c, 1)], ALU.mult, ALU.add))
            mark(stt(G1[:, 0:TP], U[:, 1:1 + TP], cw(1), G1[:, 0:TP], ALU.mult, ALU.add))
            link(stt(g1s, us[:, :, 1:5], cw(1), g1s, ALU.mult, ALU.add))
            stt(G1[:, 0:TP], U[:, 2:2 + TP], cw(2), G1[:, 0:TP], ALU.mult, ALU.add)
            stt(g1s, us[:, :, 2:6], cw(2), g1s, ALU.mult, ALU.add).then_inc(s["conv_done"], 1)
            dve.wait_ge(s["cup_done"], c + 1)
            for h in range(H):
                ins = stt(CA[:, h, :], CA[:, h, :], DEC[:, h:h + 1], M[:, h, 0:DV + 1], ALU.mult, ALU.add)
            ins.then_inc(s["c_upd"], 1)
            dve.wait_ge(s["ucup0_done"], c + 1)
            stt(CU[:, 0, :], CU[:, 0, :], DECU[:, 0:1], M[:, 4, 0:DV + 1], ALU.mult, ALU.add).then_inc(s["ucup0_upd"], 1)
            dve.wait_ge(s["conv_done"], c + 1)
            for b, (a0, a1) in enumerate(BLOCKS):
                dve.wait_ge(acc_done[b], P2_ + 4 * c + 3)
                dve.tensor_tensor(G1[:, a0:a1], PB[:, b, 0:BLK], G1[:, a0:a1], ALU.mult).then_inc(acc_free[b], 1)
            lo(T2_ + 4 * c + 4, 0)
            dve.wait_ge(s["ht_done"], c + 1)
            for x in range(2):
                ins = dve.tensor_tensor(hm[:, 4 * x:4 * x + 4, bass.ds(c * L, L)], M[:, x, :].rearrange("p (k n) -> p k n", n=L),
                                        PC[:, HNR + 4 * x:HNR + 4 * x + 4].rearrange("p (x o) -> p x o", o=1).to_broadcast([P, 4, L]),
                                        ALU.mult)
            ins.then_inc(s["hm_done"], 1)
            dve.wait_ge(s["ucup1_done"], c + 1)
            for b in range(1, 4):
                ins = stt(CU[:, b, :], CU[:, b, :], DECU[:, b:b + 1], M[:, 1 + b, 0:DV + 1], ALU.mult, ALU.add)
            link(ins)
            dve.tensor_copy(hms[:, bass.ds(c, 1), :, :].rearrange("p c x n -> p (c x) n"),
                            M[:, 4, 320:352].rearrange("p (x n) -> p x n", n=16))
            dve.tensor_copy(nsel, CU[:, :, DV]).then_inc(s["ucup1_upd"], 1)
            dve.wait_ge(acc_free[2], P2_ + 4 * c + 4)
            dve.tensor_tensor(A[:, bass.ds(c, 1), :].rearrange("p o n -> p (o n)"), G1[:], U[:, 0:T], ALU.mult) \
               .then_inc(s["a_done"], 1)
            lo(T2_ + 4 * c + 5, 1)
            assert own.n == PER2, own.n

        phase2(0)
        with dve.Fori(1, NC) as c:
            phase2(c)
        own.turn(base2, NC, PER2)
        base3 = own.base
        PER3 = 4

        def phase3(j):
            own.turn(base3, j, PER3)
            lo(T3_ + 2 * j + 2, 0)
            dve.wait_ge(acc_free[2], P3_ + 2 * j + 2)
            link(dve.tensor_tensor(G1[:], G1[:], U[:, 0:T], ALU.mult))
            mark(dve.tensor_tensor(G1[:, 0:TP], G1[:, 0:TP], hm[:, bass.ds(j, 1), :].rearrange("p o n -> p (o n)"), ALU.mult))
            g1u = G1[:, TP:T].rearrange("p (b u t) -> p u b t", u=2, t=ST)
            hj = hms[:].rearrange("p (u h) x (b t) -> p u (h x) b t", u=2, t=ST)
            for u in range(2):
                ins = stt(g1u[:, u], hj[:, u, bass.ds(j, 1)].rearrange("p o b t -> p (o b) t"), PC[:, bass.ds(HNR + j, 1)], g1u[:, u],
                          ALU.mult, ALU.mult)
                (mark if u == 0 else link)(ins)
            aj = A[:, bass.ds(j, 1), :].rearrange("p o n -> p (o n)")
            dve.tensor_tensor(aj, aj, G1[:], ALU.add).then_inc(s["merged"], 1)
            lo(T3_ + 2 * j + 3, 1)
            assert own.n == PER3, own.n

        with dve.Fori(0, KT) as j:
            phase3(j)
        own.turn(base3, KT, PER3)
        for k in range(KT):
            dve.wait_ge(s["split_hi"], k + 1)
            dve.tensor_tensor(XL[:, k, :], A[:, k, :], XH[:, k, :].bitcast(F32), ALU.subtract).then_inc(s["merged_lo"], 1)
        link(dve.memset(SQA[:], 0.0))
        base4 = own.base + own.n
        PER4 = 2

        def phase4(i):
            for x in range(2):
                n = 2 * i + x
                own.turn(base4, n, PER4)
                an = A[:, bass.ds(n, 1), :].rearrange("p o n -> p (o n)")
                gt = MOD[:, bass.ds(16 + n, 1), :].rearrange("p o c -> p (o c)")
                dve.wait_ge(s["xtr_copy"], n + 1)
                for b, (a0, a1) in enumerate(BLOCKS):
                    dve.wait_ge(acc_done[b], P4_ + n + 1)
                    if b < 2:
                        stt(an[:, a0:a1], PB[:, b, 0:BLK], gt[:, 0:1], xT[:, a0:a1], ALU.mult, ALU.add).then_inc(acc_free[b], 1)
                    else:
                        stt(an[:, a0:TP], PB[:, b, 0:LP], gt[:, 0:1], xT[:, a0:TP], ALU.mult, ALU.add)
                        link(dve.tensor_tensor(an[:, TP:T].rearrange("p (b t) -> p b t", t=ST),
                                               PB[:, b, LP:BLK].rearrange("p (b t) -> p b t", t=ST),
                                               gt[:, 1:NB].rearrange("p (b o) -> p b o", o=1).to_broadcast([P, SB, ST]), ALU.mult))
                        dve.tensor_tensor(an[:, TP:T], an[:, TP:T], xT[:, TP:T], ALU.add).then_inc(acc_free[b], 1)
                lo(T4_ + n + 2, x)
                dve.wait_ge(s["sq_done"], n + 1)
                link(dve.tensor_tensor(SQA[:], SQA[:], SQ[:], ALU.add))
                assert own.n == PER4, own.n

        with dve.Fori(0, KT // 2) as i:
            phase4(i)
        own.turn(base4, KT, PER4)
        dve.wait_ge(s["st_out"], 16 * 5)
        dve.memset(YS[:], 0.0).then_inc(s["x2n_done"], 1)
        rstd = R[:, 0, :]
        for b, (a0, a1) in enumerate(BLOCKS):
            dve.wait_ge(s["ms_sqrt"], b + 1)
            ins = dve.reciprocal(rstd[:, a0:a1], rstd[:, a0:a1])
            (mark if b < 2 else link)(ins)

        def bcol(ap):
            return ap.rearrange("p (b o) -> p b o", o=1).to_broadcast([P, SB, ST])

        def h2_lo(k):
            dve.wait_ge(s["h2_hi"], k + 1)
            dve.tensor_tensor(XL[:, k, :], R[:, 1 + k % 2, :], XH[:, k, :].bitcast(F32), ALU.subtract).then_inc(s["h2_lo"], 1)

        for k in range(KT):
            hf = R[:, 1 + k % 2, :]
            hs = hf[:, TP:T].rearrange("p (b t) -> p b t", t=ST)
            if k >= 2:
                dve.wait_ge(s["h2_lo"], k - 1)
            link(dve.tensor_tensor(hf, A[:, k, :], rstd, ALU.mult))
            dve.tensor_scalar(hf[:, 0:TP], hf[:, 0:TP], S2[:, k, 0:1], MOD[:, 24 + k, 0:1], ALU.mult, ALU.add)
            link(dve.tensor_tensor(hs, hs, bcol(S2[:, k, 1:NB]), ALU.mult))
            dve.tensor_tensor(hs, hs, bcol(MOD[:, 24 + k, 1:NB]), ALU.add).then_inc(s["h2_scaled"], 1)
            if k >= 1:
                h2_lo(k - 1)
        h2_lo(KT - 1)

        def phase5(f, last=False):
            for m in range(FT):
                dve.wait_ge(acc_free[2], P5_ + 12 * f + m + 1)
                dve.tensor_tensor(R[:, 0, :], R[:, 0, :], R[:, 0, :], ALU.mult).then_inc(s["rr_done"], 1)
                lo(T5_ + 8 * f + m + 2, m % 2)
                dve.wait_ge(s["act_hi"], FT * f + m + 1)
                dve.tensor_tensor(AL[:, m, :], R[:, 0, :], AH[:, m, :].bitcast(F32), ALU.subtract).then_inc(s["act_lo"], 1)
            for d in range(4):
                for y in range(2):
                    n = 2 * d + y
                    for b, (a0, a1) in enumerate(BLOCKS):
                        dve.wait_ge(acc_done[b], P5_ + 12 * f + 4 + n + 1)
                        gt = MOD[:, 40 + n, 0:1]
                        if b < 2:
                            stt(A[:, n, a0:a1], PB[:, b, 0:BLK], gt, A[:, n, a0:a1], ALU.mult, ALU.add).then_inc(acc_free[b], 1)
                        else:
                            stt(A[:, n, a0:TP], PB[:, b, 0:LP], gt, A[:, n, a0:TP], ALU.mult, ALU.add)
                            dve.tensor_tensor(YS[:, n, :], PB[:, b, LP:BLK], YS[:, n, :], ALU.add).then_inc(acc_free[b], 1)
                if not (last and d >= 2):
                    lo(T5_ + 8 * f + 4 + d + 2, d % 2)

        phase5(0)
        with dve.Fori(1, 7) as f:
            phase5(f)
        phase5(7, last=True)
        dve.wait_ge(acc_free[2], P5_ + 12 * 8)
        ys = YS[:].rearrange("p k (b t) -> p k b t", t=ST)
        for k0 in (0, 4):
            link(dve.tensor_tensor(ys[:, k0:k0 + 4], ys[:, k0:k0 + 4], bc(MOD[:, 40 + k0:44 + k0, 1:NB]), ALU.mult))
        dve.tensor_tensor(A[:, :, TP:T], A[:, :, TP:T], YS[:], ALU.add).then_inc(s["ys_done"], 1)
        dve.wait_ge(s["gf_in"], 16)
        for b in range(9):
            n = P if b < 8 else NS
            dve.wait_ge(s["y_std"], b + 1)
            link(dve.reciprocal(rs[0:n, b:b + 1], rs[0:n, b:b + 1]))
            if b >= 2:
                dve.wait_ge(y_out[b % 2], 16 * (b // 2))
            bank = 2 * (b % 2)
            stt(Y[0:n, b % 2, :], M[0:n, bank:bank + 2, :].rearrange("p a n -> p (a n)"), rs[0:n, b:b + 1], GF[0:n, :],
                ALU.mult, ALU.mult).then_inc(s["y_done"], 1)

    ctx.close()


_INS = ["x_prompt", "x_sample", "state_conv", "state_C", "state_n", "state_m", "c_prompt", "c_sample", "w_ada", "b_ada",
        "g_norm1", "g_norm2", "w_in", "b_gate", "conv_w", "conv_b", "hn_g", "w_out", "w_up", "w_down", "g_final"]
_OUTS = {"y_prompt": (1, 1024, 1024), "y_sample": (8, 4, 1024), "p_conv": (1, 1, 2, 1024), "p_C": (1, 1, 4, 128, 256),
         "p_n": (1, 1, 4, 128), "p_m": (1, 1, 4), "s_conv": (1, 8, 2, 1024), "s_C": (1, 8, 4, 128, 256),
         "s_n": (1, 8, 4, 128), "s_m": (1, 8, 4)}


def kernel(**inputs):
    import numpy as np
    import concourse.bacc as bacc
    from concourse.bass_utils import run_bass_kernel_spmd

    nc = bacc.Bacc("TRN2", target_bir_lowering=False, num_devices=1)
    arrays, I, O = {}, {}, {}
    for name in _INS:
        a = np.ascontiguousarray(inputs[name])
        arrays[f"in_{name}"] = a
        I[name] = nc.dram_tensor(f"in_{name}", a.shape, F32, kind="ExternalInput").ap()
    for name, shape in _OUTS.items():
        O[name] = nc.dram_tensor(f"out_{name}", shape, F32, kind="ExternalOutput").ap()
    layer_kernel(nc, I, O)
    r = run_bass_kernel_spmd(nc, [arrays], core_ids=[0])
    return tuple(r.results[0][f"out_{name}"] for name in _OUTS)
```

```python
from contextlib import ExitStack

import concourse.bass as bass
from concourse import mybir
from concourse.alu_op_type import AluOpType as ALU

F32 = mybir.dt.float32
F32R = mybir.dt.float32r
ACT = mybir.ActivationFunctionType

P = 128
D = 1024
KT = D // P
TP = 1024
SB, ST = 8, 4
NS = SB * ST
T = TP + NS
BLK = T // 3
LP = TP - 2 * BLK
H, DK, DV = 4, 128, 256
L = 128
NC = TP // L
FF = 4 * D
FT = FF // P // 8
EPS = 1e-6
CAP = 15.0
KSCALE = DK ** -0.5
NB = 1 + SB
XC, BG, CG, WQ, WK, WV, WO, WGATE, GA, GB = 0, 1024, 2048, 3072, 3584, 4096, 5120, 6144, 6152, 7176
T1_, T2_, T3_, T4_, T5_ = 0, 16, 48, 64, 72
P1_, P2_, P3_, P4_, P5_ = 1, 17, 49, 65, 73
NT = 136
G1R, G2R, CBR, CWR, HNR, BAR, PROWS = 0, 8, 16, 24, 48, 56, 104
GM, WS, MR = range(3)
BLOCKS = [(0, BLK), (BLK, 2 * BLK), (2 * BLK, T)]
GROUPS = [(g, min(P, BLK - g)) for g in range(0, BLK, P)]
POOL_H2 = [(1, k) for k in range(KT)] + [(2, k) for k in range(KT // 2, KT)]
H2_DVE = [(b, k) for b in range(3) for k in range(KT) if (b, k) not in POOL_H2]


class Count:

    def __init__(self, eng, sem):
        self.eng, self.sem, self.base, self.n = eng, sem, 0, 0

    def mark(self, ins):
        ins.then_inc(self.sem, 1)
        self.n += 1
        return self.base + self.n

    def wait(self, value):
        self.eng.wait_ge(self.sem, value)

    def link(self, ins):
        self.wait(self.mark(ins))

    def turn(self, base, i, per):
        self.base, self.n = base + i * per, 0


def layer_kernel(nc, I, O):
    ctx = ExitStack()
    early, startup, gates, mixer, mlstm, outp, mlp, final = (ExitStack() for _ in range(8))

    def sb(name, shape, dt=F32, scope=ctx):
        return scope.enter_context(nc.sbuf_tensor(name, shape, dt))

    def sem(name):
        return ctx.enter_context(nc.semaphore(name))

    zp_d = nc.dram_tensor("zp_d", [4 * H, P, TP], F32, kind="Internal").ap()
    zs_d = nc.dram_tensor("zs_d", [2 * H, 4, P, 16], F32, kind="Internal").ap()
    rp_d = nc.dram_tensor("rp_d", [H, TP], F32, kind="Internal").ap()
    rs_d = nc.dram_tensor("rs_d", [2 * H, 16], F32, kind="Internal").ap()

    XH = sb("XH", [P, KT, T], F32R)
    XL = sb("XL", [P, KT, T], F32R)
    A = sb("A", [P, KT, T])
    raw = sb("raw", [P, 2, 1024])
    whi = sb("whi", [P, 2, 1024], F32R)
    wlo = sb("wlo", [P, 2, 1024], F32R)
    ident = sb("ident", [P, P])
    ones = sb("ones", [P, P])
    MOD = sb("MOD", [P, 48, NB])
    S1 = sb("S1", [P, KT, NB])
    S2 = sb("S2", [P, KT, NB])
    PC = sb("PC", [P, PROWS])
    COL = sb("COL", [P, NC, 3, H])
    COLS = sb("COLS", [16, 2 * H, 3])
    CM = sb("CM", [P, P])
    CMS = sb("CMS", [16, 16])
    BM = sb("BM", [16, 4])
    NT_ = sb("NT_", [P, NS])
    SCV = sb("SCV", [P, KT, 16])
    NCV = sb("NCV", [P, KT, 18])
    ss = sb("ss", [P, 9])
    rs = sb("rs", [P, 9])
    epsc = sb("epsc", [P, 1])

    cS = sb("cS", [P, KT, P], F32R, scope=early)
    cT = sb("cT", [P, KT, NB], scope=early)
    GW = sb("GW", [P, KT, P], F32R, scope=early)
    wg = sb("wg", [P, KT, 2 * H], scope=early)
    M0s = sb("M0s", [H, SB], scope=early)
    MP = sb("MP", [H, NC], scope=early)
    PM = sb("PM", [H, 1], scope=early)
    SMo = sb("SMo", [H, SB], scope=early)
    bg15 = sb("bg15", [36, 1], scope=early)
    AROW = sb("AROW", [P, 512], scope=early)
    xin = sb("xin", [P, 9, D], scope=startup)
    araw0 = sb("araw0", [P, 8, 1024], scope=startup)
    startup.close()
    araw = sb("araw", [P, 2, 1024], scope=gates)
    ahi = sb("ahi", [P, 2, 1024], F32R, scope=gates)
    alo = sb("alo", [P, 2, 1024], F32R, scope=gates)
    zr = sb("zr", [P, 2, T], scope=gates)
    GT = sb("GT", [36, T], scope=gates)
    TH = sb("TH", [36, T], scope=gates)
    NBr = sb("NBr", [36, T], scope=gates)
    RMK = sb("RMK", [36, T], scope=gates)
    NB0, DL, MU = RMK[0:H], NBr[0:H], TH[0:H]
    RR = sb("RR", [H, T], scope=gates)
    GMR = sb("GMR", [H, T], scope=gates)
    WSR = sb("WSR", [H, T], scope=gates)
    MRR = sb("MRR", [H, T], scope=gates)
    gates.close()
    early.close()
    hm = sb("hm", [P, KT, TP], scope=mixer)
    hms = sb("hms", [P, 2 * H, 2, 16], scope=mixer)
    G1 = sb("G1", [P, T], scope=mixer)
    U = sb("U", [P, 2 + TP + 6 * SB], scope=mixer)
    Z = sb("Z", [P, 4 * H, L], scope=mlstm)
    VT = sb("VT", [P, H, DV + 1], scope=mlstm)
    CA = sb("CA", [P, H, DV + 1], scope=mlstm)
    RB = sb("RB", [P, H, L], scope=mlstm)
    IB = sb("IB", [P, H, L], scope=mlstm)
    EX = sb("EX", [P, H, L], scope=mlstm)
    KW = sb("KW", [P, H, DK], scope=mlstm)
    HT = sb("HT", [P, H, DV], scope=mlstm)
    DEC = sb("DEC", [P, H], scope=mlstm)
    sc4 = sb("sc4", [P, 8, H], scope=mlstm)
    ZU = sb("ZU", [P, 4, 16], scope=mlstm)
    VTU = sb("VTU", [16, DV + 1], scope=mlstm)
    CU = sb("CU", [P, 4, DV + 1], scope=mlstm)
    RU = sb("RU", [P, 16], scope=mlstm)
    IU = sb("IU", [P, 16], scope=mlstm)
    EU = sb("EU", [16, 16], scope=mlstm)
    QM = sb("QM", [P, 80], scope=mlstm)
    KU = sb("KU", [16, 4, DK], scope=mlstm)
    WM = sb("WM", [16, 4], scope=mlstm)
    HTU = sb("HTU", [16, DV], scope=mlstm)
    DECU = sb("DECU", [P, 4], scope=mlstm)
    sc1 = sb("sc1", [16, 8], scope=mlstm)
    mlstm.close()
    NCR = sb("NCR", [18, D], scope=outp)
    NR = sb("NR", [NS, P], scope=outp)
    PN = sb("PN", [H, P], scope=outp)
    xs = sb("xs", [P, 2, 9, P], scope=outp)
    xT = sb("xT", [P, T], scope=outp)
    SQ = sb("SQ", [P, T], scope=outp)
    DG = sb("DG", [P, 3, P], scope=outp)
    outp.close()
    mixer.close()
    AS = sb("AS", [P, KT, T], scope=final)
    final.close()
    AH = sb("AH", [P, FT, T], F32R, scope=mlp)
    AL = sb("AL", [P, FT, T], F32R, scope=mlp)
    SQA = sb("SQA", [P, T], scope=mlp)
    Y = sb("Y", [P, 2, D], scope=mlp)
    R = sb("R", [P, 3, T], scope=mlp)
    YS = sb("YS", [P, KT, NS], scope=mlp)
    GF = sb("GF", [P, D], scope=mlp)
    mlp.close()
    RSTD = Y[:].rearrange("p a n -> p (a n)")[:, 0:T]
    HB = R[:].rearrange("p a (b n) -> p (a b) n", b=3)
    CR = A[:, 0, :]
    CG_ = A[:, 1, :]
    PR = A[:, 2, 0:P]
    SNR = A[:, 2, P:2 * P]
    SCR = A[:, 3, :]

    PB = ctx.enter_context(nc.psum_tensor("PB", [P, 3, 512], F32))
    M = ctx.enter_context(nc.psum_tensor("M", [P, 5, 512], F32))

    names = """c_in p_in small_in raw0 raw1 hi_done lo_done acc_done0 acc_done1 acc_done2 acc_free0
    acc_free1 acc_free2 ada0_mm ada_done arow_done rowt_done mod_done xsq_done xrt_done xn_done xt_done
    xt_free pool_done csig_done ct_done ct_used gw_done sm_done h_hi h_lo hf_done
    araw_in0 araw_in1 ahi_done alo_done a_used z_evac z_out0 z_out1 gate_sum gate_act gate_rows r_out cols_mm cols_done
    m_out z_in zu_in rb_in cu_in cu_out qk_done kt_done vt_done upre_done num_done unum_done cup_done ucup0_done
    ucup1_done ht_done uht_done ib_exp e_exp vt_copy vtu_copy ss_done std_done ex_done qi_done cn_done p_done kw_done
    var_done ht_ready c_upd ucup0_upd ucup1_upd hm_done xc_evac conv_done sig_done a_done
    fin1_mm fin1_copy st_out so_evac sg_evac merged split_hi xs_in0 xs_in1 xtr_done xtr_copy x2_done sq_done rms_sqrt
    h2_t h2_tp h2_hi h2_lo hs_t hs_hi hs_lo sqa_done rms_mm rms_diag rstd_mm rstd_done as_done relu_done rr_done act_hi act_lo y_mm y_sq y_std y_done y_out0 y_out1 gf_in dve_step act_step
    x2n_done ys_done merged_lo""".split()
    s = {n: sem(n) for n in names}
    xr = [sem(f"x_in{b}") for b in range(9)]
    ar0 = [sem(f"ada_in{b}") for b in range(8)]
    raw_in = [s["raw0"], s["raw1"]]
    araw_in = [s["araw_in0"], s["araw_in1"]]
    xs_in = [s["xs_in0"], s["xs_in1"]]
    y_out = [s["y_out0"], s["y_out1"]]
    z_out = [s["z_out0"], s["z_out1"]]
    acc_done = [s[f"acc_done{b}"] for b in range(3)]
    acc_free = [s[f"acc_free{b}"] for b in range(3)]

    w_in = I["w_in"].rearrange("l (k p) n -> (l p) k n", p=P)
    w_out = I["w_out"].rearrange("l (k p) n -> (l p) k n", p=P)
    w_up = I["w_up"].rearrange("l (k p) n -> (l p) k n", p=P)
    w_down = I["w_down"].rearrange("l (k p) n -> (l p) k n", p=P)
    w_ada = I["w_ada"].rearrange("l (k p) n -> (l p) k n", p=P)
    x_p = I["x_prompt"].rearrange("a (b p) n -> p (a b) n", p=P)
    x_s = I["x_sample"].rearrange("a b n -> (a b) n")
    st_C = I["state_C"].rearrange("l (x u) h d v -> l x (u h) d v", u=2)
    so_C = O["s_C"].rearrange("l (x u) h d v -> l x (u h) d v", u=2)
    ADA0 = [0, 2, 1, 3]

    block = ctx.enter_context(nc.Block())

    @block.sync
    def _(sp):
        def tile(t, slot, src):
            if not (isinstance(t, int) and t < 2):
                sp.wait_ge(s["lo_done"], t - 1)
            k = src.shape[1]
            sp.dma_start(raw[:, slot, :].rearrange("p (k n) -> p k n", k=k), src).then_inc(raw_in[slot], 16)

        sp.dma_start(CR[0:1, 0:D], I["c_prompt"]).then_inc(s["c_in"], 16)
        sp.dma_start(CR[1:NB, 0:D], I["c_sample"]).then_inc(s["c_in"], 16)
        for name, r0, n in (("g_norm1", G1R, 8), ("g_norm2", G2R, 8), ("conv_b", CBR, 8), ("hn_g", HNR, 8),
                            ("b_ada", BAR, 48)):
            sp.dma_start(PR[r0:r0 + n, :], I[name].rearrange("l (r p) -> (l r) p", p=P)).then_inc(s["p_in"], 16)
        sp.dma_start(PR[CWR:CWR + 24, :], I["conv_w"].rearrange("l w (r p) -> (l w r) p", p=P)).then_inc(s["p_in"], 16)

        def ada0(n):
            if n >= 8:
                sp.wait_ge(s["ada0_mm"], n - 7)
            c = ADA0[n // 4] * 512
            k = n % 4 * 2
            sp.dma_start(araw0[:, n % 8, :].rearrange("p (k n) -> p k n", k=2),
                         w_ada[:, k:k + 2, c:c + 512]).then_inc(ar0[n % 8], 16)

        for n in range(8):
            ada0(n)
        for b in range(9):
            if b < 8:
                sp.dma_start(xin[:, b, :], x_p[:, b, :]).then_inc(xr[b], 16)
            else:
                sp.dma_start(xin[0:NS, b, :], x_s).then_inc(xr[b], 16)
        for n in range(8, 16):
            ada0(n)
        tile(0, 0, w_in[:, :, WQ:WQ + P])
        tile(1, 1, w_in[:, :, WK:WK + P])
        sp.wait_ge(s["ada0_mm"], 16)
        sp.wait_ge(s["xn_done"], 9)

        def atile(a, slot, q, c0):
            if not (isinstance(a, int) and a < 2):
                sp.wait_ge(s["alo_done"], a - 1)
            sp.dma_start(araw[:, slot, :].rearrange("p (k n) -> p k n", k=2),
                         w_ada[:, 2 * q:2 * q + 2, bass.ds(c0, 512)]).then_inc(araw_in[slot], 16)

        atile(0, 0, 0, 2048)
        atile(1, 1, 1, 2048)

        def phase1(h, first_next=None):
            cols = [WV + 256 * h, WV + P + 256 * h, WQ + P + P * h, WK + P + P * h]
            for k in range(4):
                t = T1_ + 4 * h + k
                for x in range(2):
                    a = 2 * k + x + 2
                    if isinstance(h, int) and h == H - 1 and a >= 8:
                        continue
                    atile(8 * h + a, x, a % 4, 2048 + 1024 * h + 512 * (a // 4))
                if isinstance(h, int) and h == H - 1 and k >= 2:
                    tile(t + 2, k % 2, w_in[:, :, [XC, CG][k - 2]:][:, :, 0:P])
                else:
                    tile(t + 2, k % 2, w_in[:, :, bass.ds(cols[k], P)])

        phase1(0)
        with sp.Fori(1, H - 1) as h:
            phase1(h)
        phase1(H - 1)

        def stage(c):
            if isinstance(c, int) and c == 0:
                sp.wait_ge(z_out[0], 32 * 2 * H)
                sp.wait_ge(z_out[1], 32 * 2 * H)
                sp.wait_ge(s["r_out"], 32)
                sp.wait_ge(s["cols_mm"], 1)
                sp.wait_ge(s["a_used"], 32)
                sp.wait_ge(s["m_out"], 32)
            else:
                sp.wait_ge(s["vt_done"], c)
                sp.wait_ge(s["upre_done"], c)
                sp.wait_ge(s["qi_done"], c)
                sp.wait_ge(s["ex_done"], c)
            sp.dma_start(Z[:], zp_d.rearrange("j p n -> p j n")[:, :, bass.ds(c * L, L)]).then_inc(s["z_in"], 16)
            sp.dma_start(RB[:], rp_d[:, bass.ds(c * L, L)].rearrange("(o h) n -> o h n", o=1)
                         .broadcast_to([P, H, L])).then_inc(s["rb_in"], 16)
            sp.dma_start(RU[:], rs_d[bass.ds(c, 1), :].broadcast_to([P, 16])).then_inc(s["rb_in"], 16)
            sp.dma_start(ZU[:], zs_d[bass.ds(c, 1)].rearrange("u k p n -> p (u k) n")).then_inc(s["zu_in"], 16)

        def load_cu(c):
            sp.dma_start(CU[:, :, 0:DV], st_C[0, :, bass.ds(c, 1)].rearrange("x u d v -> d (x u) v")) \
              .then_inc(s["cu_in"], 16)

        def store_cu(c):
            sp.dma_start(so_C[0, :, bass.ds(c, 1)].rearrange("x u d v -> d (x u) v"), CU[:, :, 0:DV]) \
              .then_inc(s["cu_out"], 16)

        def phase2(c, last=False):
            for k, col in ((2, BG), (3, GA)):
                tile(T2_ + 4 * c + k, k % 2, w_in[:, :, bass.ds(col + P * c, P)])
                if k == 2 and not (isinstance(c, int) and c == 0):
                    sp.wait_ge(s["ucup1_upd"], c)
                    store_cu(c - 1)
                    sp.wait_ge(s["cu_out"], 16 * c)
                    load_cu(c)
            if not last:
                stage(c + 1)
            for k in range(2):
                col = [WO, GB][k] if last else [XC + P, CG + P][k] + P * c
                tile(T2_ + 4 * c + 4 + k, k % 2, w_in[:, :, bass.ds(col, P)])

        stage(0)
        load_cu(0)
        phase2(0)
        with sp.Fori(1, NC - 1) as c:
            phase2(c)
        phase2(NC - 1, last=True)
        sp.wait_ge(s["ucup1_upd"], NC)
        store_cu(NC - 1)
        sp.wait_ge(s["c_upd"], NC)
        sp.dma_start(O["p_C"].rearrange("l b h d v -> d (l b h) v"), CA[:, :, 0:DV]).then_inc(s["st_out"], 16)
        with sp.Fori(0, KT - 1) as j:
            tile(T3_ + 2 + 2 * j, 0, w_in[:, :, bass.ds(WO + P + P * j, P)])
            tile(T3_ + 3 + 2 * j, 1, w_in[:, :, bass.ds(GB + P + P * j, P)])
        sp.wait_ge(s["fin1_copy"], 2)
        sp.dma_start(O["s_conv"].rearrange("l b w n -> (l b w) n"), NCR[0:16, :]).then_inc(s["st_out"], 16)
        sp.dma_start(O["p_conv"].rearrange("l b w n -> (l b w) n"), NCR[16:18, :]).then_inc(s["st_out"], 16)
        sp.dma_start(O["s_n"].rearrange("l b h d -> (l b h) d"), NR[:]).then_inc(s["st_out"], 16)
        sp.dma_start(O["p_n"].rearrange("l b h d -> (l b h) d"), PN[:]).then_inc(s["st_out"], 16)
        tile(T4_, 0, w_out[:, :, 0:P])
        tile(T4_ + 1, 1, w_out[:, :, P:2 * P])

        def load_xs(n, slot):
            sp.dma_start(xs[:, slot, 0:8, :], x_p[:, :, bass.ds(n * P, P)]).then_inc(xs_in[slot], 16)
            sp.dma_start(xs[0:NS, slot, 8, :], x_s[:, bass.ds(n * P, P)]).then_inc(xs_in[slot], 16)

        sp.wait_ge(s["cu_out"], 16 * NC)
        sp.wait_ge(s["st_out"], 16)
        load_xs(0, 0)
        load_xs(1, 1)
        with sp.Fori(0, KT // 2 - 1) as i:
            for x in range(2):
                tile(T4_ + 2 + 2 * i + x, x, w_out[:, :, bass.ds((2 + 2 * i + x) * P, P)])
                sp.wait_ge(s["xtr_done"], 2 * i + 1 + x)
                load_xs(2 * i + 2 + x, x)
        tile(T5_, 0, w_up[:, :, 0:P])
        tile(T5_ + 1, 1, w_up[:, :, P:2 * P])

        def mlp_tiles(f, last=False):
            for m in (2, 3):
                tile(T5_ + 8 * f + m, m % 2, w_up[:, :, bass.ds(512 * f + P * m, P)])
            for d in range(4):
                tile(T5_ + 8 * f + 4 + d, d % 2, w_down[:, bass.ds(4 * f, 4), 256 * d:256 * d + 256])
            if not last:
                for m in (0, 1):
                    tile(T5_ + 8 * f + 8 + m, m % 2, w_up[:, :, bass.ds(512 * f + 512 + P * m, P)])

        with sp.Fori(0, 7) as f:
            mlp_tiles(f)
        mlp_tiles(7, last=True)
        sp.wait_ge(s["x2n_done"], 1)
        sp.dma_start(GF[:], I["g_final"].rearrange("(o n) -> o n", o=1).broadcast_to([P, D])).then_inc(s["gf_in"], 16)
        for b in range(9):
            sp.wait_ge(s["y_done"], b + 1)
            if b < 8:
                sp.dma_start(O["y_prompt"].rearrange("a (b p) n -> p (a b) n", p=P)[:, b, :], Y[:, b % 2, :]) \
                  .then_inc(y_out[b % 2], 16)
            else:
                sp.dma_start(O["y_sample"].rearrange("a b n -> (a b) n"), Y[0:NS, 0, :]).then_inc(y_out[b % 2], 16)
        sp.wait_ge(y_out[0], 16 * 5)
        sp.wait_ge(y_out[1], 16 * 4)
        sp.wait_ge(s["st_out"], 16 * 5)

    @block.gpsimd
    def _(pool):
        n = 0

        def step(ins):
            nonlocal n
            ins.then_inc(s["pool_done"], 1)
            n += 1
            pool.wait_ge(s["pool_done"], n)

        step(pool.memset(ident[:], 0.0))
        step(pool.affine_select(out=ident[:], in_=ident[:], compare_op=ALU.not_equal, fill=1.0, base=0,
                                pattern=[[-1, P]], channel_multiplier=1))
        step(pool.memset(ones[:], 1.0))
        step(pool.memset(CM[:], 0.0))
        step(pool.affine_select(out=CM[:], in_=CM[:], compare_op=ALU.is_ge, fill=-1e30, base=0,
                                pattern=[[1, P]], channel_multiplier=-1))
        step(pool.memset(CMS[:], 0.0))
        step(pool.affine_select(out=CMS[:], in_=CMS[:], compare_op=ALU.is_ge, fill=-1e30, base=0,
                                pattern=[[1, 16]], channel_multiplier=-1))
        v = CMS[:].rearrange("p (b t) -> p b t", t=ST)
        step(pool.affine_select(out=v, in_=v, compare_op=ALU.is_ge, fill=-1e30, base=0,
                                pattern=[[-ST, 4], [0, ST]], channel_multiplier=1))
        step(pool.memset(BM[:], 1.0))
        step(pool.affine_select(out=BM[:], in_=BM[:], compare_op=ALU.is_ge, fill=0.0, base=0,
                                pattern=[[-ST, 4]], channel_multiplier=1))
        step(pool.affine_select(out=BM[:], in_=BM[:], compare_op=ALU.is_ge, fill=0.0, base=ST - 1,
                                pattern=[[ST, 4]], channel_multiplier=-1))

        for i, (b, k) in enumerate(POOL_H2):
            a0, a1 = BLOCKS[b][0], min(BLOCKS[b][1], TP)
            pool.wait_ge(s["rstd_done"], b + 1)
            if i == 0:
                pool.wait_ge(s["as_done"], 2)
            elif k == KT - 1 and b == 2:
                pool.wait_ge(s["as_done"], 3)
            if i >= 3:
                pool.wait_ge(s["h2_lo"], KT * POOL_H2[i - 3][0] + POOL_H2[i - 3][1] + 1)
            pool.tensor_tensor(HB[:, 6 + i % 3, 0:a1 - a0], AS[:, k, a0:a1], RSTD[:, a0:a1], ALU.mult) \
                .then_inc(s["h2_tp"], 1)

    POOL_STEPS = 11

    @block.scalar
    def _(act):
        own = Count(act, s["act_step"])
        act.dma_start(wg[:], w_in[:, :, WGATE:WGATE + 2 * H]).then_inc(s["small_in"], 16)
        act.wait_ge(s["sm_done"], 1)
        act.dma_start(bg15[0:H, :], I["b_gate"][:, 0:H].rearrange("l h -> h l"), allow_slow_non_contiguous=True).then_inc(s["small_in"], 16)
        act.dma_start(bg15[32:32 + H, :], I["b_gate"][:, H:2 * H].rearrange("l h -> h l"), allow_slow_non_contiguous=True).then_inc(s["small_in"], 16)
        act.dma_start(M0s[:], I["state_m"].rearrange("l b h -> h (l b)"), allow_slow_non_contiguous=True).then_inc(s["small_in"], 16)
        act.dma_start(SNR[0:NS, :], I["state_n"].rearrange("l b h d -> (l b h) d")).then_inc(s["small_in"], 16)
        act.dma_start(SCR[0:16, 0:D], I["state_conv"].rearrange("l b w n -> (l b w) n")).then_inc(s["small_in"], 16)
        act.wait_ge(s["c_in"], 32)
        act.activation(CG_[0:NB, 0:D], CR[0:NB, 0:D], ACT.Sigmoid).then_inc(s["csig_done"], 1)

        for g in range(3):
            for b in range(3 * g, 3 * g + 3):
                n = P if b < 8 else NS
                act.wait_ge(xr[b], 16)
                own.link(act.activation(A[0:n, 4 + b % 4, 0:D], xin[0:n, b, :], ACT.Square, accum_out=ss[0:n, b:b + 1]))
            if g < 2:
                act.activation(rs[:, 3 * g:3 * g + 3], ss[:, 3 * g:3 * g + 3], ACT.Sqrt, bias=epsc[:, 0:1],
                               scale=1.0 / D).then_inc(s["xrt_done"], 1)
            else:
                own.link(act.activation(rs[:, 6:8], ss[:, 6:8], ACT.Sqrt, bias=epsc[:, 0:1], scale=1.0 / D))
                act.activation(rs[0:NS, 8:9], ss[0:NS, 8:9], ACT.Sqrt, bias=epsc[0:NS, 0:1],
                               scale=1.0 / D).then_inc(s["xrt_done"], 1)
        act.wait_ge(s["ct_used"], 2)
        for b in range(9):
            n = P if b < 8 else NS
            src = (M if b % 2 == 0 else PB)[:, 0:2, :].rearrange("p a (k n) -> p (a k) n", n=P)[:, :, 0:n]
            act.wait_ge(s["xt_done"], b + 1)
            act.activation(A[:, :, b * P:b * P + n], src, ACT.Copy).then_inc(s["xt_free"], 1)
        for k in range(KT):
            act.wait_ge(s["hf_done"], k + 1)
            act.activation(XH[:, k, :], A[:, k, :], ACT.Copy).then_inc(s["h_hi"], 1)

        def hi(t, slot, free=None):
            act.wait_ge(raw_in[slot], 8 * (t - slot) + 16)
            if not (isinstance(t, int) and t < 2):
                act.wait_ge(acc_done[2], t if free is None else free)
            act.activation(whi[:, slot, :], raw[:, slot, :], ACT.Copy).then_inc(s["hi_done"], 1)

        def ahi_(a, slot):
            act.wait_ge(araw_in[slot], 8 * (a - slot) + 16)
            if not (isinstance(a, int) and a < 2):
                act.wait_ge(s["a_used"], a - 1)
            act.activation(ahi[:, slot, :], araw[:, slot, :], ACT.Copy).then_inc(s["ahi_done"], 1)

        hi(0, 0)
        hi(1, 1)
        ahi_(0, 0)
        ahi_(1, 1)

        def phase1(h):
            last = isinstance(h, int) and h == H - 1
            for k in range(4):
                t, slot = T1_ + 4 * h + k, k % 2
                if not (last and k == 3):
                    for x in range(2):
                        ahi_(8 * h + 2 * k + 2 + x, x)
                if not (isinstance(h, int) and h == 0 and k < 2):
                    act.wait_ge(z_out[slot], 64 * h + 32 * (k // 2))
                for b, (a0, a1) in enumerate(BLOCKS):
                    act.wait_ge(acc_done[b], P1_ + 4 * h + k + 1)
                    if b < 2:
                        act.activation(zr[:, slot, a0:a1], PB[:, b, 0:BLK], ACT.Copy).then_inc(acc_free[b], 1)
                    else:
                        act.activation(zr[:, slot, a0:TP], PB[:, b, 0:LP], ACT.Copy)
                        act.activation(zr[:, slot, TP:T].rearrange("p (u b t) -> p b u t", u=2, t=ST),
                                       PB[:, b, LP:BLK].rearrange("p (b u t) -> p b u t", u=2, t=ST),
                                       ACT.Copy).then_inc(acc_free[b], 1)
                hi(t + 2, slot)
                act.wait_ge(acc_free[2], P1_ + 4 * h + k + 1)
                act.dma_start(zp_d[bass.ds(4 * h + k, 1)].rearrange("o p n -> (o p) n"), zr[:, slot, 0:TP]) \
                   .then_inc(z_out[slot], 16)
                act.dma_start(zs_d.rearrange("(u h) k p n -> k h p u n", u=2)[k, bass.ds(h, 1)]
                              .rearrange("o p u n -> (o p) u n"),
                              zr[:, slot, TP:T].rearrange("p (u n) -> p u n", u=2)).then_inc(z_out[slot], 16)

        def gate_acts():
            act.wait_ge(s["gate_sum"], 1)
            own.link(act.activation(TH[:], GT[:], ACT.Tanh, bias=bg15[:, 0:1], scale=1.0 / CAP))
            own.link(act.activation(GT[32:36, :], TH[32:36, :], ACT.Exp, scale=-CAP))
            act.activation(GT[32:36, :], GT[32:36, :], ACT.Ln, bias=1.0).then_inc(s["gate_act"], 1)

        phase1(0)
        gate_acts()
        phase1(1)
        phase1(2)
        act.wait_ge(s["gate_rows"], 1)
        act.dma_start(rp_d, RR[:, 0:TP]).then_inc(s["r_out"], 16)
        act.dma_start(rs_d.rearrange("(u h) n -> h u n", u=2), RR[:, TP:T].rearrange("h (u n) -> h u n", u=2)) \
           .then_inc(s["r_out"], 16)
        act.dma_start(O["p_m"].rearrange("l b h -> h (l b)"), PM[:], allow_slow_non_contiguous=True).then_inc(s["m_out"], 16)
        act.dma_start(O["s_m"].rearrange("l b h -> h (l b)"), SMo[:], allow_slow_non_contiguous=True).then_inc(s["m_out"], 16)
        phase1(3)
        act.wait_ge(s["cols_mm"], 1)
        cp = M[:, 0, 0:NC * 3 * H].rearrange("p (c k h) -> p c k h", k=3, h=H)
        cs = M[0:16, 1, 0:24].rearrange("p (k u) -> p u k", k=3)
        act.activation(COL[:, :, GM, :], cp[:, :, GM, :], ACT.Copy)
        act.activation(COL[:, :, WS, :], cp[:, :, WS, :], ACT.Exp)
        act.activation(COL[:, :, MR, :], cp[:, :, MR, :], ACT.Exp, scale=-1.0)
        act.activation(COLS[:, :, GM], cs[:, :, GM], ACT.Copy)
        act.activation(COLS[:, :, WS], cs[:, :, WS], ACT.Exp)
        act.activation(COLS[:, :, MR], cs[:, :, MR], ACT.Exp, scale=-1.0).then_inc(s["cols_done"], 1)

        act.wait_ge(z_out[0], 32 * 2 * H)
        act.wait_ge(z_out[1], 32 * 2 * H)
        act.wait_ge(s["r_out"], 32)
        act.wait_ge(s["m_out"], 32)

        def phase2(c):
            first = isinstance(c, int) and c == 0
            act.wait_ge(s["rb_in"], 32 * c + 32)
            act.activation(IB[:], RB[:], ACT.Exp)
            act.activation(IU[:], RU[:], ACT.Exp).then_inc(s["ib_exp"], 1)
            act.wait_ge(s["ex_done"], c + 1)
            act.activation(EX[:], EX[:], ACT.Exp)
            act.activation(EU[:], EU[:], ACT.Exp).then_inc(s["e_exp"], 1)
            act.wait_ge(s["vt_done"], c + 1)
            for x in range(2):
                last = act.activation(VT[:, 2 * x:2 * x + 2, 0:DV], M[:, 1 + x, :].rearrange("p (h v) -> p h v", v=DV), ACT.Copy)
            last.then_inc(s["vt_copy"], 1)
            act.wait_ge(s["upre_done"], c + 1)
            act.activation(VTU[:, 0:DV], M[0:16, 4, 128:128 + DV], ACT.Copy).then_inc(s["vtu_copy"], 1)
            if not first:
                act.wait_ge(s["a_done"], c)
            for b, (a0, a1) in enumerate(BLOCKS):
                act.wait_ge(acc_done[b], P2_ + 4 * c + 1)
                ins = act.activation(G1[:, a0:a1], PB[:, b, 0:BLK], ACT.Copy)
                ins.then_inc(acc_free[b], 1)
            hi(T2_ + 4 * c + 2, 0)
            act.wait_ge(s["num_done"], c + 1)
            for h in range(H):
                own.link(act.activation(HT[:, h, :], M[:, h, 0:DV], ACT.Square, accum_out=sc4[:, 0, h:h + 1]))
            act.wait_ge(s["unum_done"], c + 1)
            act.activation(HTU[:], M[0:16, 4, 0:DV], ACT.Square, accum_out=sc1[:, 0:1]).then_inc(s["ss_done"], 1)
            act.wait_ge(s["var_done"], c + 1)
            act.activation(sc4[:, 1, :], sc4[:, 5, :], ACT.Sqrt, bias=epsc[:, 0:1], scale=1.0 / DV)
            act.activation(sc1[:, 1:2], sc1[:, 5:6], ACT.Sqrt, bias=epsc[0:16, 0:1], scale=1.0 / DV) \
               .then_inc(s["std_done"], 1)
            hi(T2_ + 4 * c + 3, 1)
            hi(T2_ + 4 * c + 4, 0)
            act.wait_ge(s["conv_done"], c + 1)
            for b, (a0, a1) in enumerate(BLOCKS):
                act.wait_ge(acc_done[b], P2_ + 4 * c + 4)
                ins = act.activation(U[:, a0:a1], PB[:, b, 0:BLK], ACT.Sigmoid)
                ins.then_inc(acc_free[b], 1)
            hi(T2_ + 4 * c + 5, 1)

        phase2(0)
        with act.Fori(1, NC) as c:
            phase2(c)

        act.wait_ge(s["fin1_mm"], 1)
        act.wait_ge(s["cu_out"], 16 * NC)
        act.wait_ge(s["st_out"], 16)
        act.activation(NCR[:], M[0:18, 0:2, :].rearrange("p a n -> p (a n)"), ACT.Copy).then_inc(s["fin1_copy"], 1)
        act.activation(NR[:], M[0:NS, 2, 0:P], ACT.Copy)
        act.activation(PN[:], M[0:H, 3, 0:P], ACT.Copy).then_inc(s["fin1_copy"], 1)

        def phase3(j):
            first = isinstance(j, int) and j == 0
            act.wait_ge(s["a_done"] if first else s["merged"], NC if first else j)
            for k, buf in enumerate((G1, U)):
                for b, (a0, a1) in enumerate(BLOCKS):
                    act.wait_ge(acc_done[b], P3_ + 2 * j + k + 1)
                    act.activation(buf[:, a0:a1], PB[:, b, 0:BLK], ACT.Sigmoid).then_inc(acc_free[b], 1)
                if not (isinstance(j, int) and j == KT - 1 and k == 1):
                    hi(T3_ + 2 * j + k + 2, k)

        phase3(0)
        with act.Fori(1, KT - 1) as j:
            phase3(j)
        phase3(KT - 1)
        for k in range(KT):
            act.wait_ge(s["merged"], k + 1)
            if k == 0:
                act.wait_ge(acc_done[2], P4_)
            act.activation(XH[:, k, :], A[:, k, :], ACT.Copy).then_inc(s["split_hi"], 1)
        hi(T4_ + 1, 1)

        def phase4(i):
            for x in range(2):
                n = 2 * i + x
                last = isinstance(i, int) and n == KT - 1
                act.wait_ge(s["xtr_done"], n + 1)
                if not (isinstance(i, int) and n == 0):
                    act.wait_ge(acc_free[2], P4_ + n)
                act.activation(xT[:, 0:TP], M[:, 0:2, :].rearrange("p a n -> p (a n)"), ACT.Copy)
                act.activation(xT[:, TP:T], M[:, 2, 0:NS], ACT.Copy).then_inc(s["xtr_copy"], 1)
                if not last:
                    act.wait_ge(acc_free[2], P4_ + n + 1)
                    act.activation(SQ[:], A[:, bass.ds(n, 1), :].rearrange("p o n -> p (o n)"), ACT.Square) \
                       .then_inc(s["sq_done"], 1)
                    hi(T4_ + n + 2, x)

        phase4(0)
        with act.Fori(1, KT // 2 - 1) as i:
            phase4(i)
        phase4(KT // 2 - 1)

        def square(b):
            a0, a1 = BLOCKS[b]
            act.wait_ge(acc_free[b], P4_ + KT)
            act.wait_ge(s["sqa_done"], KT - 1)
            act.activation(SQ[:, a0:a1], A[:, KT - 1, a0:a1], ACT.Square).then_inc(s["sq_done"], 1)

        def rms(b):
            act.wait_ge(s["rms_mm"], b + 1)
            bank = 3 + b % 2
            act.activation(rs[:, 3 * b:3 * b + 2], M[:, bank, 0:2], ACT.Sqrt, bias=epsc[:, 0:1], scale=1.0 / D)
            n = GROUPS[2][1]
            act.activation(rs[0:n, 3 * b + 2:3 * b + 3], M[0:n, bank, 2:3], ACT.Sqrt, bias=epsc[0:n, 0:1], scale=1.0 / D) \
               .then_inc(s["rms_sqrt"], 1)

        def rstd(b):
            a0, a1 = BLOCKS[b]
            act.wait_ge(s["rstd_mm"], b + 1)
            if b == 0:
                act.wait_ge(s["st_out"], 16 * 5)
            act.activation(RSTD[:, a0:a1], M[:, b, 0:BLK], ACT.Copy).then_inc(s["rstd_done"], 1)

        def h2_hi(b, k):
            a0, a1 = BLOCKS[b][0], min(BLOCKS[b][1], TP)
            if (b, k) in POOL_H2:
                i = POOL_H2.index((b, k))
                act.wait_ge(s["h2_tp"], i + 1)
                src = HB[:, 6 + i % 3, 0:a1 - a0]
            else:
                i = H2_DVE.index((b, k))
                act.wait_ge(s["h2_t"], i + 1)
                src = HB[:, i % 6, 0:a1 - a0]
            act.activation(XH[:, k, a0:a1], src, ACT.Identity, bias=MOD[:, 24 + k, 0:1]).then_inc(s["h2_hi"], 1)

        square(0)
        rms(0)
        rstd(0)
        h2_hi(0, 0)
        square(1)
        h2_hi(0, 1)
        rms(1)
        h2_hi(0, 2)
        rstd(1)
        for k in range(3, 6):
            h2_hi(0, k)
        square(2)
        h2_hi(0, 6)
        rms(2)
        h2_hi(0, 7)
        rstd(2)
        for k in range(KT):
            h2_hi(1, k)
            if k == 3:
                hi(T5_ + 1, 1)
        act.wait_ge(s["hs_t"], 1)
        act.activation(XH[:, :, TP:T], YS[:], ACT.Copy).then_inc(s["hs_hi"], 1)
        for k in range(KT):
            h2_hi(2, k)

        def phase5(f, last=False):
            for m in range(FT):
                if not (isinstance(f, int) and f == 0 and m == 0):
                    act.wait_ge(s["act_lo"], FT * f + m)
                for b, (a0, a1) in enumerate(BLOCKS):
                    act.wait_ge(acc_done[b], P5_ + 12 * f + m + 1)
                    act.activation(R[:, 0, a0:a1], PB[:, b, 0:BLK], ACT.Relu).then_inc(acc_free[b], 1)
                if m < FT - 1:
                    hi(T5_ + 8 * f + m + 2, m % 2, P5_ + 12 * f + m + 1)
                act.wait_ge(s["rr_done"], FT * f + m + 1)
                act.activation(AH[:, m, :], R[:, 0, :], ACT.Copy).then_inc(s["act_hi"], 1)
                if m == FT - 1:
                    hi(T5_ + 8 * f + m + 2, m % 2, P5_ + 12 * f + m + 1)
            for d in range(4):
                if not (last and d >= 2):
                    hi(T5_ + 8 * f + 4 + d + 2, d % 2, P5_ + 12 * f + 4 + 2 * d + 2)

        phase5(0)
        with act.Fori(1, 7) as f:
            phase5(f)
        phase5(7, last=True)
        for b in range(9):
            n = P if b < 8 else NS
            act.wait_ge(s["y_mm"], b + 1)
            bank = 2 * (b % 2)
            act.activation(R[0:n, b % 2, 0:D],
                           M[0:n, bank:bank + 2, :].rearrange("p a n -> p (a n)"), ACT.Square,
                           accum_out=ss[0:n, b:b + 1]).then_inc(s["y_sq"], 1)
            act.wait_ge(s["y_sq"], b + 1)
            act.activation(rs[0:n, b:b + 1], ss[0:n, b:b + 1], ACT.Sqrt, bias=epsc[0:n, 0:1], scale=1.0 / D) \
               .then_inc(s["y_std"], 1)

    @block.tensor
    def _(pe):
        def turn(dst, src):
            n = src.shape[0]
            return pe.transpose(dst, src, ident[0:n, 0:n])

        pe.wait_ge(s["pool_done"], 2)
        pe.wait_ge(s["p_in"], 16 * 6)
        turn(M[:, 2, 0:PROWS], PR[0:PROWS, :])
        pe.wait_ge(s["csig_done"], 2)
        pe.wait_ge(s["small_in"], 16 * 6)
        for k in range(KT):
            turn(M[:, 2, 128 + NB * k:128 + NB * (k + 1)], CG_[0:NB, k * P:(k + 1) * P])
        turn(M[:, 2, 256:256 + NS], SNR[0:NS, :])
        for k in range(KT):
            ins = turn(M[:, 2, 288 + 16 * k:304 + 16 * k], SCR[0:16, k * P:(k + 1) * P])
        ins.then_inc(s["ct_done"], 1)
        pe.wait_ge(s["ct_used"], 1)

        def ada0(q):
            if q >= 2:
                pe.wait_ge(s["arow_done"], q - 1)
            for n in range(4 * q, 4 * q + 4):
                pe.wait_ge(ar0[n % 8], 16 * (n // 8 + 1))
                for x in range(2):
                    ins = pe.matmul(M[0:NB, 3 + q % 2, :], cT[:, n % 4 * 2 + x, :],
                                    araw0[:, n % 8, 512 * x:512 * x + 512], start=(n % 4 + x == 0), stop=(n % 4 == 3 and x == 1))
                ins.then_inc(s["ada0_mm"], 1)

        def rowt0(q):
            pe.wait_ge(s["arow_done"], q + 1)
            for x in range(4):
                ins = turn(PB[:, 2, 64 * q + 16 * x:64 * q + 16 * x + NB], AROW[0:NB, P * x:P * x + P])
            ins.then_inc(s["rowt_done"], 1)

        def xturn(b):
            n = P if b < 8 else NS
            pe.wait_ge(s["xn_done"], b + 1)
            if b >= 2:
                pe.wait_ge(s["xt_free"], b - 1)
            dst = M if b % 2 == 0 else PB
            for k in range(KT):
                ins = turn(dst[:, k // 4, P * (k % 4):P * (k % 4) + n], xin[0:n, b, k * P:(k + 1) * P])
            ins.then_inc(s["xt_done"], 1)

        ada0(0)
        rowt0(0)
        ada0(1)
        rowt0(1)
        for b in range(3):
            xturn(b)
        ada0(2)
        rowt0(2)
        for b in range(3, 6):
            xturn(b)
        ada0(3)
        rowt0(3)
        for b in range(6, 9):
            xturn(b)
        pe.wait_ge(s["gw_done"], 1)
        pe.wait_ge(s["xt_free"], 9)
        pe.wait_ge(s["mod_done"], 4)
        for k in range(KT):
            pe.wait_ge(s["h_lo"], k + 1)
            for b, (a0, a1) in enumerate(BLOCKS):
                for part in (XH, XL):
                    ins = pe.matmul(PB[:, b, 0:BLK], GW[:, k, :], part[:, k, a0:a1],
                                    start=(k == 0 and part is XH), stop=(k == KT - 1 and part is XL))
                if k == KT - 1:
                    ins.then_inc(acc_done[b], 1)

        def k_tile(bank, wh, wl, w0, xh, xl, k, n_k, a0, a1):
            for j, (w, x) in enumerate(((wh, xh), (wh, xl), (wl, xh))):
                ins = pe.matmul(PB[:, bank, 0:BLK], w[:, w0:w0 + P], x[:, k, a0:a1],
                                start=(k == 0 and j == 0), stop=(k == n_k - 1 and j == 2))
            return ins

        def product(p, slot, xh, xl, n_k, w_stride, w_off, before=None):
            for b, (a0, a1) in enumerate(BLOCKS):
                pe.wait_ge(acc_free[b], p)
                for k in range(n_k):
                    if before is not None:
                        before(b, k)
                    ins = k_tile(b, whi[:, slot], wlo[:, slot], w_stride * k + w_off, xh, xl, k, n_k, a0, a1)
                ins.then_inc(acc_done[b], 1)

        def first_product(p, slot, xh, xl, n_k, w_stride, ready):
            for b in range(3):
                pe.wait_ge(acc_free[b], p)
            for k in range(n_k):
                ready(k)
                for b, (a0, a1) in enumerate(BLOCKS):
                    ins = k_tile(b, whi[:, slot], wlo[:, slot], w_stride * k, xh, xl, k, n_k, a0, a1)
                    if k == n_k - 1:
                        ins.then_inc(acc_done[b], 1)

        def wide(t, p, slot, ready=None, before=None):
            pe.wait_ge(s["lo_done"], t + 1)
            if ready is None:
                product(p, slot, XH, XL, KT, P, 0, before)
            else:
                first_product(p, slot, XH, XL, KT, P, ready)

        def phase1(h):
            for k in range(4):
                for x in range(2):
                    a = 2 * k + x
                    pe.wait_ge(s["alo_done"], 8 * h + a + 1)
                    if a % 4 == 0:
                        pe.wait_ge(s["arow_done"], 4 + 2 * h + a // 4)
                    for y in range(2):
                        for w in (ahi, alo):
                            ins = pe.matmul(M[:, 4, :], cS[:, 2 * (a % 4) + y, :], w[:, x, 512 * y:512 * y + 512],
                                            start=(a % 4 == 0 and y == 0 and w is ahi), stop=(a % 4 == 3 and y == 1 and w is alo))
                    ins.then_inc(s["a_used"], 1)
                wide(T1_ + 4 * h + k, P1_ + 4 * h + k, k % 2)
                if k % 2 == 1:
                    pe.wait_ge(s["arow_done"], 4 + 2 * h + k // 2 + 1)
                    pe.wait_ge(s["mod_done"], 4 + 2 * h + k // 2)
                    for x in range(4):
                        ins = turn(M[:, 3, P * x:P * x + P], AROW[:, P * x:P * x + P])
                    ins.then_inc(s["rowt_done"], 1)

        with pe.Fori(0, H) as h:
            phase1(h)

        pe.wait_ge(s["gate_rows"], 1)
        for c in range(NC):
            for kind, row in ((GM, GMR), (WS, WSR), (MR, MRR)):
                j = (c * 3 + kind) * H
                turn(M[:, 0, j:j + H], row[:, c * L:(c + 1) * L])
        for kind, row in ((GM, GMR), (WS, WSR), (MR, MRR)):
            for u in range(2):
                ins = turn(M[0:16, 1, 8 * kind + H * u:8 * kind + H * u + H], row[:, TP + 16 * u:TP + 16 * u + 16])
        ins.then_inc(s["cols_mm"], 1)

        def phase2(c):
            first = isinstance(c, int) and c == 0
            pe.wait_ge(s["z_in"], 16 * c + 16)
            pe.wait_ge(s["zu_in"], 16 * c + 16)
            if first:
                pe.wait_ge(s["cols_done"], 1)
                pe.wait_ge(s["mod_done"], 12)
            else:
                pe.wait_ge(s["hm_done"], c)
                pe.wait_ge(s["ucup1_upd"], c)
            for h in range(H):
                ins = pe.matmul(M[:, 0, h * L:(h + 1) * L], Z[:, 4 * h + 1, :], Z[:, 4 * h, :], start=True, stop=True)
            ins.then_inc(s["qk_done"], 1)
            for h in range(H):
                ins = turn(M[:, 3, h * DK:(h + 1) * DK], Z[:, 4 * h + 1, :])
            ins.then_inc(s["kt_done"], 1)
            for j in range(2 * H):
                ins = turn(M[:, 1 + j // 4, P * (j % 4):P * (j % 4) + P], Z[:, 4 * (j // 2) + 2 + j % 2, :])
            ins.then_inc(s["vt_done"], 1)
            pe.matmul(M[0:16, 4, 0:16], ZU[:, 1, :], ZU[:, 0, :], start=True, stop=True)
            for x in range(2):
                turn(M[0:16, 4, 128 + P * x:256 + P * x], ZU[:, 2 + x, :])
            turn(M[0:16, 4, 384:512], ZU[:, 1, :]).then_inc(s["upre_done"], 1)
            wide(T2_ + 4 * c, P2_ + 4 * c, 0)
            pe.wait_ge(s["p_done"], c + 1)
            pe.wait_ge(s["qi_done"], c + 1)
            pe.wait_ge(s["vt_copy"], c + 1)
            pe.wait_ge(s["kw_done"], c + 1)
            if not first:
                pe.wait_ge(s["c_upd"], c)
            for h in range(H):
                pe.matmul(M[:, h, 0:DV + 1], EX[:, h, :], VT[:, h, :], start=True, stop=False)
                ins = pe.matmul(M[:, h, 0:DV + 1], IB[:, h, :], CA[:, h, :], start=False, stop=True)
            ins.then_inc(s["num_done"], 1)
            pe.wait_ge(s["vtu_copy"], c + 1)
            pe.wait_ge(s["cn_done"], c + 1)
            pe.wait_ge(s["cu_in"], 16 * c + 16)
            for b in range(4):
                pe.matmul(M[0:16, 4, 0:DV + 1], QM[:, 16 * b:16 * b + 16], CU[:, b, :], start=(b == 0), stop=False)
            pe.matmul(M[0:16, 4, 0:DV + 1], EU[:], VTU[:], start=False, stop=True).then_inc(s["unum_done"], 1)
            wide(T2_ + 4 * c + 1, P2_ + 4 * c + 1, 1)
            pe.wait_ge(s["ht_ready"], c + 1)
            for h in range(H):
                ins = pe.matmul(M[:, h, 0:DV + 1], KW[:, h, :], VT[:, h, :], start=True, stop=True)
            ins.then_inc(s["cup_done"], 1)
            pe.matmul(M[:, 4, 0:DV + 1], KU[:, 0, :], VTU[:], start=True, stop=True).then_inc(s["ucup0_done"], 1)
            wide(T2_ + 4 * c + 2, P2_ + 4 * c + 2, 0)
            pe.wait_ge(s["c_upd"], c + 1)
            for j in range(2 * H):
                ins = turn(M[:, j // 4, P * (j % 4):P * (j % 4) + P], HT[:, j // 2, P * (j % 2):P * (j % 2) + P])
            ins.then_inc(s["ht_done"], 1)
            pe.wait_ge(s["ucup0_upd"], c + 1)
            for b in range(1, 4):
                ins = pe.matmul(M[:, 1 + b, 0:DV + 1], KU[:, b, :], VTU[:], start=True, stop=True)
            for x in range(2):
                ins = turn(M[:, 4, 320 + 16 * x:336 + 16 * x], HTU[:, P * x:P * x + P])
            ins.then_inc(s["ucup1_done"], 1)
            wide(T2_ + 4 * c + 3, P2_ + 4 * c + 3, 1)

        phase2(0)
        with pe.Fori(1, NC) as c:
            phase2(c)

        pe.wait_ge(s["hm_done"], NC)
        pe.wait_ge(s["ucup1_upd"], NC)
        for k in range(KT):
            turn(M[0:18, k // 4, P * (k % 4):P * (k % 4) + P], NCV[:, k, :])
        turn(M[0:NS, 2, 0:P], NT_[:])
        turn(M[0:H, 3, 0:P], CA[:, :, DV]).then_inc(s["fin1_mm"], 1)

        with pe.Fori(0, KT) as j:
            wide(T3_ + 2 * j, P3_ + 2 * j, 0)
            wide(T3_ + 2 * j + 1, P3_ + 2 * j + 1, 1)

        def merged_ready(k):
            pe.wait_ge(s["merged_lo"], k + 1)

        def phase4(i):
            for x in range(2):
                n = 2 * i + x
                pe.wait_ge(xs_in[x], 32 * i + 32)
                if isinstance(i, int) and n == 0:
                    pe.wait_ge(s["fin1_copy"], 2)
                else:
                    pe.wait_ge(s["xtr_copy"], n)
                for b in range(8):
                    turn(M[:, b // 4, P * (b % 4):P * (b % 4) + P], xs[:, x, b, :])
                turn(M[:, 2, 0:NS], xs[0:NS, x, 8, :]).then_inc(s["xtr_done"], 1)
                wide(T4_ + n, P4_ + n, x, merged_ready if isinstance(i, int) and n == 0 else None,
                     norm_work if isinstance(i, int) and n == KT - 1 else None)

        def rms_cols(b):
            a0 = BLOCKS[b][0]
            pe.wait_ge(s["sq_done"], KT + b)
            if b == 0:
                pe.wait_ge(s["sqa_done"], KT - 1)
            for i, (g, n) in enumerate(GROUPS):
                for part in (SQA, SQ):
                    ins = pe.matmul(M[0:n, 3 + b % 2, i:i + 1], part[:, a0 + g:a0 + g + n], ones[:, 0:1],
                                    start=part is SQA, stop=part is SQ)
            ins.then_inc(s["rms_mm"], 1)

        def rstd_rows(b):
            pe.wait_ge(s["rms_diag"], b + 1)
            if b == 0:
                pe.wait_ge(s["xtr_copy"], KT)
            for i, (g, n) in enumerate(GROUPS):
                ins = pe.matmul(M[:, b, g:g + n], ones[0:n, :], DG[0:n, i, 0:n], start=True, stop=True)
            ins.then_inc(s["rstd_mm"], 1)

        def norm_work(b, k):
            if b >= 1 and k == 3:
                rms_cols(b - 1)
            if b >= 1 and k == 7:
                rstd_rows(b - 1)

        phase4(0)
        with pe.Fori(1, KT // 2 - 1) as i:
            phase4(i)
        phase4(KT // 2 - 1)
        rms_cols(2)
        rstd_rows(2)

        def h2_ready(b, k):
            if b == 2 and k == 0:
                pe.wait_ge(s["hs_lo"], 1)
            pe.wait_ge(s["h2_lo"], KT * b + k + 1)

        def phase5(f):
            for m in range(FT):
                wide(T5_ + 8 * f + m, P5_ + 12 * f + m, m % 2, before=h2_ready if isinstance(f, int) and f == m == 0 else None)

            def act_ready(k):
                pe.wait_ge(s["act_lo"], FT * f + k + 1)

            for d in range(4):
                pe.wait_ge(s["lo_done"], T5_ + 8 * f + 4 + d + 1)
                for y in range(2):
                    p = P5_ + 12 * f + 4 + 2 * d + y
                    if d == y == 0:
                        first_product(p, 0, AH, AL, FT, 256, act_ready)
                    else:
                        product(p, d % 2, AH, AL, FT, 256, P * y)

        phase5(0)
        with pe.Fori(1, 8) as f:
            phase5(f)

        pe.wait_ge(s["ys_done"], 1)
        for b in range(9):
            n = P if b < 8 else NS
            if b >= 2:
                pe.wait_ge(s["y_done"], b - 1)
            for k in range(KT):
                ins = turn(M[0:n, 2 * (b % 2) + k // 4, P * (k % 4):P * (k % 4) + P], A[:, k, P * b:P * b + n])
            ins.then_inc(s["y_mm"], 1)

    @block.vector
    def _(dve):
        own = Count(dve, s["dve_step"])
        link, mark = own.link, own.mark

        def stt(out, in0, scalar, in1, op0, op1):
            return dve.scalar_tensor_tensor(out=out, in0=in0, scalar=scalar, in1=in1, op0=op0, op1=op1)

        def lo(t, slot):
            dve.wait_ge(s["hi_done"], t + 1)
            dve.tensor_tensor(wlo[:, slot, :], raw[:, slot, :], whi[:, slot, :].bitcast(F32), ALU.subtract) \
               .then_inc(s["lo_done"], 1)

        def alo_(a, slot):
            dve.wait_ge(s["ahi_done"], a + 1)
            dve.tensor_tensor(alo[:, slot, :], araw[:, slot, :], ahi[:, slot, :].bitcast(F32), ALU.subtract) \
               .then_inc(s["alo_done"], 1)

        dve.memset(epsc[:], EPS)
        dve.memset(bg15[:], 0.0).then_inc(s["sm_done"], 1)
        dve.memset(cS[:].bitcast(F32), 0.0)
        dve.memset(GW[:].bitcast(F32), 0.0)
        dve.wait_ge(s["csig_done"], 1)
        dve.tensor_tensor(CG_[0:NB, 0:D], CG_[0:NB, 0:D], CR[0:NB, 0:D], ALU.mult).then_inc(s["csig_done"], 1)
        dve.wait_ge(s["ct_done"], 1)
        dve.tensor_copy(PC[:], M[:, 2, 0:PROWS])
        ct = M[:, 2, 128:128 + NB * KT].rearrange("p (k c) -> p k c", c=NB)
        dve.tensor_copy(cT[:], ct).then_inc(s["ct_used"], 1)
        dve.tensor_copy(NT_[:], M[:, 2, 256:256 + NS])
        dve.tensor_copy(SCV[:], M[:, 2, 288:416].rearrange("p (k c) -> p k c", c=16)).then_inc(s["ct_used"], 1)
        dve.wait_ge(s["ct_used"], 2)
        link(dve.tensor_copy(cS[:, :, 0:NB], cT[:]))
        dve.tensor_tensor(cS[:, :, 32:32 + NB], cT[:], cS[:, :, 0:NB].bitcast(F32), ALU.subtract)
        dve.wait_ge(s["small_in"], 16 * 6)
        for x in range(2):
            mark(dve.tensor_copy(GW[:, :, 32 * x:32 * x + H], wg[:, :, H * x:H * x + H]))
        own.wait(own.base + own.n)
        for x in range(2):
            ins = dve.tensor_tensor(GW[:, :, 64 + 32 * x:64 + 32 * x + H], wg[:, :, H * x:H * x + H],
                                    GW[:, :, 32 * x:32 * x + H].bitcast(F32), ALU.subtract)
        ins.then_inc(s["gw_done"], 1)
        link(dve.tensor_scalar(bg15[:], bg15[:], 1.0 / CAP, None, ALU.mult))

        def arow0(q):
            dve.wait_ge(s["ada0_mm"], 4 * q + 4)
            if q >= 1:
                dve.wait_ge(s["rowt_done"], q)
            dve.tensor_copy(AROW[0:NB, :], M[0:NB, 3 + q % 2, :]).then_inc(s["arow_done"], 1)
            dve.wait_ge(s["rowt_done"], q + 1)
            j = 4 * ADA0[q]
            dve.tensor_tensor(MOD[:, j:j + 4, :], PB[:, 2, 64 * q:64 * q + 64].rearrange("p (x c) -> p x c", c=16)[:, :, 0:NB],
                              PC[:, BAR + j:BAR + j + 4].rearrange("p (x o) -> p x o", o=1).to_broadcast([P, 4, NB]), ALU.add) \
               .then_inc(s["mod_done"], 1)

        def xnorm(g):
            dve.wait_ge(s["xrt_done"], g + 1)
            if g < 2:
                link(dve.reciprocal(rs[:, 3 * g:3 * g + 3], rs[:, 3 * g:3 * g + 3]))
            else:
                link(dve.reciprocal(rs[:, 6:8], rs[:, 6:8]))
                link(dve.reciprocal(rs[0:NS, 8:9], rs[0:NS, 8:9]))
            for b in range(3 * g, 3 * g + 3):
                n = P if b < 8 else NS
                dve.tensor_scalar(xin[0:n, b, :], xin[0:n, b, :], rs[0:n, b:b + 1], None, ALU.mult).then_inc(s["xn_done"], 1)

        arow0(0)
        arow0(1)
        xnorm(0)
        arow0(2)
        xnorm(1)
        arow0(3)
        xnorm(2)
        dve.wait_ge(s["mod_done"], 4)
        link(stt(S1[:], MOD[:, 8:16, :], 1.0, PC[:, G1R:G1R + 8].rearrange("p (x o) -> p x o", o=1).to_broadcast([P, KT, NB]),
                 ALU.add, ALU.mult))
        dve.wait_ge(s["xt_free"], 9)

        def bc(ap, n=ST):
            return ap.rearrange("p k (b o) -> p k b o", o=1).to_broadcast([P, ap.shape[1], SB, n])

        xs_all = A[:, :, TP:T].rearrange("p k (b t) -> p k b t", t=ST)
        for k0 in (0, 4):
            link(dve.tensor_tensor(xs_all[:, k0:k0 + 4].rearrange("p k b t -> p k b t"), xs_all[:, k0:k0 + 4], bc(S1[:, k0:k0 + 4, 1:NB]), ALU.mult))
        for k0 in (0, 4):
            link(dve.tensor_tensor(xs_all[:, k0:k0 + 4], xs_all[:, k0:k0 + 4], bc(MOD[:, k0:k0 + 4, 1:NB]), ALU.add))

        def h_lo(k):
            dve.wait_ge(s["h_hi"], k + 1)
            dve.tensor_tensor(XL[:, k, :], A[:, k, :], XH[:, k, :].bitcast(F32), ALU.subtract).then_inc(s["h_lo"], 1)

        for k in range(KT):
            dve.tensor_scalar(A[:, k, 0:TP], A[:, k, 0:TP], S1[:, k, 0:1], MOD[:, k, 0:1], ALU.mult, ALU.add) \
               .then_inc(s["hf_done"], 1)
            if k >= 1:
                h_lo(k - 1)
        h_lo(KT - 1)
        lo(0, 0)
        lo(1, 1)
        alo_(0, 0)
        alo_(1, 1)

        def phase1(h):
            last = isinstance(h, int) and h == H - 1
            for k in range(4):
                if not (last and k == 3):
                    for x in range(2):
                        alo_(8 * h + 2 * k + 2 + x, x)
                q = 4 + 2 * h + k // 2
                if k % 2 == 1:
                    dve.wait_ge(s["a_used"], 8 * h + 4 * (k // 2) + 4)
                    dve.wait_ge(s["rowt_done"], q)
                    dve.tensor_copy(AROW[:], M[:, 4, :]).then_inc(s["arow_done"], 1)
                    lo(T1_ + 4 * h + k + 2, k % 2)
                    dve.wait_ge(s["rowt_done"], q + 1)
                    ps = M[:, 3, :].rearrange("p (x c) -> p x c", c=P)
                    dst = MOD[:, bass.ds(4 * q, 4), :]
                    link(dve.tensor_tensor(dst, ps[:, :, 0:NB],
                                           PC[:, bass.ds(BAR + 4 * q, 4)].rearrange("p (x o) -> p x o", o=1).to_broadcast([P, 4, NB]),
                                           ALU.add))
                    dve.tensor_tensor(dst, ps[:, :, 32:32 + NB], dst, ALU.add).then_inc(s["mod_done"], 1)
                else:
                    lo(T1_ + 4 * h + k + 2, k % 2)

        def gate_sums():
            for b, (a0, a1) in enumerate(BLOCKS):
                dve.wait_ge(acc_done[b], 1)
                link(dve.tensor_copy(GT[:, a0:a1], PB[64:100, b, 0:BLK]))
                dve.tensor_tensor(GT[:, a0:a1], PB[0:36, b, 0:BLK], GT[:, a0:a1], ALU.add).then_inc(acc_free[b], 1)
            dve.wait_ge(acc_free[2], 1)
            dve.memset(RMK[:], 1.0).then_inc(s["gate_sum"], 1)
            dve.wait_ge(s["gate_sum"], 1)
            link(dve.memset(RMK[:, 0:TP].rearrange("p (c n) -> p c n", n=L)[:, :, 0:1], 0.0))

        def chunks(ap):
            return ap[:, 0:TP].rearrange("p (c n) -> p c n", n=L)

        def steps(ap):
            return ap[:, TP:T].rearrange("p (b t) -> p b t", t=ST)

        def units(ap):
            return ap[:, TP:T].rearrange("p (u b t) -> p b u t", u=2, t=ST)

        def nat(ap):
            return ap[:, TP:T].rearrange("p (b u t) -> p b u t", u=2, t=ST)

        def bcs(ap):
            return ap.rearrange("p (b u o) -> p b u o", u=2, o=1).to_broadcast([H, SB // 2, 2, ST])

        def gate_cumsum():
            dve.wait_ge(s["gate_act"], 1)
            link(dve.tensor_tensor_scan(NBr[32:36, 0:TP], RMK[32:36, 0:TP], GT[32:36, 0:TP], 0.0, ALU.mult, ALU.add))
            nb, lf = steps(NBr[32:36]), steps(GT[32:36])
            link(dve.tensor_copy(nb[:, :, 0], lf[:, :, 0]))
            for t in range(1, ST):
                link(dve.tensor_tensor(nb[:, :, t], nb[:, :, t - 1], lf[:, :, t], ALU.add))
            link(dve.tensor_copy(NB0, NBr[32:36, :]))
            link(dve.memset(DL[:, 0:TP], 0.0))
            link(stt(GT[0:H, :], TH[0:H, :], CAP, NB0, ALU.mult, ALU.add))
            link(dve.tensor_scalar(chunks(DL)[:, 1:NC, 0], chunks(NB0)[:, 0:NC - 1, L - 1], -1.0, None, ALU.mult))

        def gate_max():
            G = GT[0:H]
            link(dve.tensor_tensor_scan(MU[:, 0:TP], DL[:, 0:TP], G[:, 0:TP], 0.0, ALU.add, ALU.max))
            link(dve.memset(MP[:], 0.0))
            mu, g = steps(MU), steps(G)
            link(dve.tensor_tensor(mu[:, :, 0], M0s[:], g[:, :, 0], ALU.max))
            for t in range(1, ST):
                link(dve.tensor_tensor(mu[:, :, t], mu[:, :, t - 1], g[:, :, t], ALU.max))
            cmu, cnb = chunks(MU), chunks(NB0)
            mark(dve.tensor_tensor(MP[:, 1:NC], cmu[:, 0:NC - 1, L - 1], cnb[:, 0:NC - 1, L - 1], ALU.subtract))
            mark(dve.tensor_tensor(PM[:], MU[:, TP - 1:TP], NB0[:, TP - 1:TP], ALU.subtract))
            link(dve.tensor_tensor(SMo[:], mu[:, :, ST - 1], steps(NB0)[:, :, ST - 1], ALU.subtract))
            mp = MP[:].rearrange("p (c o) -> p c o", o=1).to_broadcast([H, NC, L])
            mul = cmu[:, :, L - 1:L].to_broadcast([H, NC, L])
            m0 = bcs(M0s[:])
            mus = nat(MU)[:, :, :, ST - 1:ST].to_broadcast([H, SB // 2, 2, ST])
            sub = ALU.subtract
            dve.tensor_tensor(chunks(RR), mp, cmu, sub)
            dve.tensor_tensor(chunks(GMR), chunks(G), mp, sub)
            dve.tensor_tensor(chunks(WSR), chunks(G), mul, sub)
            dve.tensor_tensor(MRR[:, 0:TP], MU[:, 0:TP], NB0[:, 0:TP], sub)
            dve.tensor_tensor(units(RR), m0, nat(MU), sub)
            dve.tensor_tensor(units(GMR), nat(G), m0, sub)
            dve.tensor_tensor(units(WSR), nat(G), mus, sub)
            dve.tensor_tensor(units(MRR), nat(MU), nat(NB0), sub).then_inc(s["gate_rows"], 1)

        gate_sums()
        phase1(0)
        gate_cumsum()
        phase1(1)
        gate_max()
        phase1(2)
        phase1(3)
        dve.wait_ge(s["mod_done"], 12)
        link(stt(S2[:], MOD[:, 32:40, :], 1.0, PC[:, G2R:G2R + 8].rearrange("p (x o) -> p x o", o=1).to_broadcast([P, KT, NB]),
                 ALU.add, ALU.mult))
        dve.wait_ge(s["cols_done"], 1)
        dve.wait_ge(z_out[0], 32 * 2 * H)
        dve.wait_ge(z_out[1], 32 * 2 * H)
        dve.wait_ge(s["r_out"], 32)
        dve.wait_ge(s["a_used"], 32)
        dve.memset(CA[:], 0.0)
        dve.memset(VT[:, :, DV:DV + 1], 1.0)
        dve.memset(VTU[:, DV:DV + 1], 1.0)
        dve.memset(U[:, 0:2], 0.0)
        link(dve.memset(QM[:], 0.0))
        dve.wait_ge(s["pool_done"], POOL_STEPS)

        base2 = own.base + own.n
        PER2 = 21

        def phase2(c, last=False):
            own.turn(base2, c, PER2)
            first = isinstance(c, int) and c == 0
            col = COL[:, bass.ds(c, 1), :, :].rearrange("p c k h -> p (c k) h")
            cols = COLS[:, bass.ds(c, 1), :].rearrange("p c k -> p (c k)")
            dve.wait_ge(s["rb_in"], 32 * c + 32)
            for h in range(H):
                stt(EX[:, h, :], RB[:, h, :], col[:, GM, h:h + 1], CM[:], ALU.add, ALU.min)
            stt(EU[:], RU[0:16, :], cols[:, GM:GM + 1], CMS[:], ALU.add, ALU.min).then_inc(s["ex_done"], 1)
            dve.wait_ge(s["ib_exp"], c + 1)
            dve.tensor_copy(DEC[:], IB[:, :, L - 1])
            mark(dve.tensor_copy(DECU[:], IU[:].rearrange("p (b t) -> p b t", t=ST)[:, :, ST - 1]))
            dve.wait_ge(s["z_in"], 16 * c + 16)
            dve.wait_ge(s["zu_in"], 16 * c + 16)
            own.wait(own.base + own.n)
            q = Z[:].rearrange("p (h k) n -> p h k n", k=4)[:, :, 0, :]
            dve.tensor_tensor(IB[:], q, IB[:], ALU.mult)
            dve.tensor_tensor(QM[:].rearrange("p (b x) -> p b x", x=20)[:, :, 0:ST], ZU[:, 0, :].rearrange("p (b t) -> p b t", t=ST),
                              IU[:].rearrange("p (b t) -> p b t", t=ST), ALU.mult).then_inc(s["qi_done"], 1)
            dve.wait_ge(s["qk_done"], c + 1)
            dve.wait_ge(s["e_exp"], c + 1)
            stt(EX[:], M[:, 0, :].rearrange("p (h n) -> p h n", n=L), KSCALE, EX[:], ALU.mult, ALU.mult)
            dve.wait_ge(s["vtu_copy"], c + 1)
            stt(EU[:], M[0:16, 4, 0:16], KSCALE, EU[:], ALU.mult, ALU.mult).then_inc(s["p_done"], 1)
            link(dve.tensor_scalar(WM[:], BM[:], cols[:, WS:WS + 1], KSCALE, ALU.mult, ALU.mult))
            for h in range(H):
                dve.tensor_scalar(KW[:, h, :], M[:, 3, h * DK:(h + 1) * DK], col[:, WS, h:h + 1], KSCALE, ALU.mult, ALU.mult)
            for b in range(4):
                ins = dve.tensor_scalar(KU[:, b, :], M[0:16, 4, 384:512], WM[:, b:b + 1], None, ALU.mult)
            ins.then_inc(s["kw_done"], 1)
            nsel = NT_[:].rearrange("p (x u) -> p u x", u=2 * H)[:, bass.ds(c, 1), :].rearrange("p u x -> p (u x)")
            dve.tensor_copy(CU[:, :, DV], nsel).then_inc(s["cn_done"], 1)
            lo(T2_ + 4 * c + 2, 0)
            dve.wait_ge(s["ss_done"], c + 1)
            den, denu = M[:, 0:H, DV], M[0:16, 4, DV:DV + 1]
            mark(stt(sc4[:, 2, :], den, -1.0, col[:, MR, :], ALU.mult, ALU.max))
            link(stt(sc1[:, 2:3], denu, -1.0, cols[:, MR:MR + 1], ALU.mult, ALU.max))
            mark(dve.tensor_tensor(sc4[:, 2, :], den, sc4[:, 2, :], ALU.max))
            link(dve.tensor_tensor(sc1[:, 2:3], denu, sc1[:, 2:3], ALU.max))
            mark(dve.reciprocal(sc4[:, 3, :], sc4[:, 2, :]))
            link(dve.reciprocal(sc1[:, 3:4], sc1[:, 2:3]))
            mark(dve.tensor_tensor(sc4[:, 4, :], sc4[:, 3, :], sc4[:, 3, :], ALU.mult))
            link(dve.tensor_tensor(sc1[:, 4:5], sc1[:, 3:4], sc1[:, 3:4], ALU.mult))
            dve.tensor_tensor(sc4[:, 5, :], sc4[:, 4, :], sc4[:, 0, :], ALU.mult)
            dve.tensor_tensor(sc1[:, 5:6], sc1[:, 4:5], sc1[:, 0:1], ALU.mult).then_inc(s["var_done"], 1)
            dve.wait_ge(s["std_done"], c + 1)
            mark(dve.reciprocal(sc4[:, 6, :], sc4[:, 1, :]))
            link(dve.reciprocal(sc1[:, 6:7], sc1[:, 1:2]))
            mark(dve.tensor_tensor(sc4[:, 7, :], sc4[:, 6, :], sc4[:, 3, :], ALU.mult))
            link(dve.tensor_tensor(sc1[:, 7:8], sc1[:, 6:7], sc1[:, 3:4], ALU.mult))
            for h in range(H):
                dve.tensor_scalar(HT[:, h, :], M[:, h, 0:DV], sc4[:, 7, h:h + 1], None, ALU.mult)
            dve.tensor_scalar(HTU[:], M[0:16, 4, 0:DV], sc1[:, 7:8], None, ALU.mult).then_inc(s["ht_ready"], 1)
            us = U[:, 2 + TP:].rearrange("p (b x) -> p b x", x=6)
            for b, (a0, a1) in enumerate(BLOCKS):
                dve.wait_ge(acc_done[b], P2_ + 4 * c + 2)
                if b == 0:
                    dve.wait_ge(acc_free[2], P2_ + 4 * c + 1)
                if b < 2:
                    dve.tensor_tensor(U[:, 2 + a0:2 + a1], PB[:, b, 0:BLK], G1[:, a0:a1], ALU.mult).then_inc(acc_free[b], 1)
                else:
                    dve.tensor_tensor(U[:, 2 + a0:2 + TP], PB[:, b, 0:LP], G1[:, a0:TP], ALU.mult)
                    dve.tensor_tensor(us[:, :, 2:6], PB[:, b, LP:BLK].rearrange("p (b t) -> p b t", t=ST),
                                      G1[:, TP:T].rearrange("p (b t) -> p b t", t=ST), ALU.mult).then_inc(acc_free[b], 1)
            lo(T2_ + 4 * c + 3, 1)
            scv = SCV[:, bass.ds(c, 1), :].rearrange("p c (b w) -> p (c b) w", w=2)
            mark(dve.memset(U[:, 0:2], 0.0))
            link(dve.tensor_copy(us[:, :, 0:2], scv))
            ncv = NCV[:, bass.ds(c, 1), :].rearrange("p c n -> p (c n)")
            dve.tensor_copy(ncv[:, 16:18], U[:, TP:TP + 2])
            dve.tensor_copy(ncv[:, 0:16].rearrange("p (b w) -> p b w", w=2), us[:, :, 4:6])
            g1s = G1[:, TP:T].rearrange("p (b t) -> p b t", t=ST)

            def cw(w):
                return PC[:, bass.ds(CWR + 8 * w + c, 1)]

            mark(dve.tensor_scalar(G1[:, 0:TP], U[:, 0:TP], cw(0), PC[:, bass.ds(CBR + c, 1)], ALU.mult, ALU.add))
            link(dve.tensor_scalar(g1s, us[:, :, 0:4], cw(0), PC[:, bass.ds(CBR + c, 1)], ALU.mult, ALU.add))
            mark(stt(G1[:, 0:TP], U[:, 1:1 + TP], cw(1), G1[:, 0:TP], ALU.mult, ALU.add))
            link(stt(g1s, us[:, :, 1:5], cw(1), g1s, ALU.mult, ALU.add))
            stt(G1[:, 0:TP], U[:, 2:2 + TP], cw(2), G1[:, 0:TP], ALU.mult, ALU.add)
            stt(g1s, us[:, :, 2:6], cw(2), g1s, ALU.mult, ALU.add).then_inc(s["conv_done"], 1)
            dve.wait_ge(s["cup_done"], c + 1)
            for h in range(H):
                ins = stt(CA[:, h, :], CA[:, h, :], DEC[:, h:h + 1], M[:, h, 0:DV + 1], ALU.mult, ALU.add)
            ins.then_inc(s["c_upd"], 1)
            dve.wait_ge(s["ucup0_done"], c + 1)
            stt(CU[:, 0, :], CU[:, 0, :], DECU[:, 0:1], M[:, 4, 0:DV + 1], ALU.mult, ALU.add).then_inc(s["ucup0_upd"], 1)
            dve.wait_ge(s["conv_done"], c + 1)
            for b, (a0, a1) in enumerate(BLOCKS):
                dve.wait_ge(acc_done[b], P2_ + 4 * c + 3)
                dve.tensor_tensor(G1[:, a0:a1], PB[:, b, 0:BLK], G1[:, a0:a1], ALU.mult).then_inc(acc_free[b], 1)
            lo(T2_ + 4 * c + 4, 0)
            dve.wait_ge(s["ht_done"], c + 1)
            for x in range(2):
                ins = dve.tensor_tensor(hm[:, 4 * x:4 * x + 4, bass.ds(c * L, L)], M[:, x, :].rearrange("p (k n) -> p k n", n=L),
                                        PC[:, HNR + 4 * x:HNR + 4 * x + 4].rearrange("p (x o) -> p x o", o=1).to_broadcast([P, 4, L]),
                                        ALU.mult)
            ins.then_inc(s["hm_done"], 1)
            dve.wait_ge(s["ucup1_done"], c + 1)
            for b in range(1, 4):
                ins = stt(CU[:, b, :], CU[:, b, :], DECU[:, b:b + 1], M[:, 1 + b, 0:DV + 1], ALU.mult, ALU.add)
            link(ins)
            dve.tensor_copy(hms[:, bass.ds(c, 1), :, :].rearrange("p c x n -> p (c x) n"),
                            M[:, 4, 320:352].rearrange("p (x n) -> p x n", n=16))
            dve.tensor_copy(nsel, CU[:, :, DV]).then_inc(s["ucup1_upd"], 1)
            dve.wait_ge(acc_free[2], P2_ + 4 * c + 4)
            dve.tensor_tensor(A[:, bass.ds(c, 1), :].rearrange("p o n -> p (o n)"), G1[:], U[:, 0:T], ALU.mult) \
               .then_inc(s["a_done"], 1)
            lo(T2_ + 4 * c + 5, 1)
            assert own.n == PER2, own.n

        phase2(0)
        with dve.Fori(1, NC) as c:
            phase2(c)
        own.turn(base2, NC, PER2)
        base3 = own.base
        PER3 = 6

        def phase3(j):
            own.turn(base3, j, PER3)
            dve.wait_ge(acc_free[2], P3_ + 2 * j + 1)
            mark(dve.tensor_tensor(G1[:, 0:TP], G1[:, 0:TP], hm[:, bass.ds(j, 1), :].rearrange("p o n -> p (o n)"), ALU.mult))
            g1u = G1[:, TP:T].rearrange("p (b u t) -> p u b t", u=2, t=ST)
            hj = hms[:].rearrange("p (u h) x (b t) -> p u (h x) b t", u=2, t=ST)
            for u in range(2):
                ins = stt(g1u[:, u], hj[:, u, bass.ds(j, 1)].rearrange("p o b t -> p (o b) t"), PC[:, bass.ds(HNR + j, 1)], g1u[:, u],
                          ALU.mult, ALU.mult)
                (mark if u == 0 else link)(ins)
            lo(T3_ + 2 * j + 2, 0)
            aj = A[:, bass.ds(j, 1), :].rearrange("p o n -> p (o n)")
            for b, (a0, a1) in enumerate(BLOCKS):
                dve.wait_ge(acc_free[b], P3_ + 2 * j + 2)
                link(dve.tensor_tensor(U[:, a0:a1], U[:, a0:a1], G1[:, a0:a1], ALU.mult))
                ins = dve.tensor_tensor(aj[:, a0:a1], aj[:, a0:a1], U[:, a0:a1], ALU.add)
            ins.then_inc(s["merged"], 1)
            if not (isinstance(j, int) and j == KT - 1):
                lo(T3_ + 2 * j + 3, 1)
            assert own.n == PER3, own.n

        with dve.Fori(0, KT - 1) as j:
            phase3(j)
        phase3(KT - 1)
        own.turn(base3, KT, PER3)
        for k in range(KT):
            dve.wait_ge(s["split_hi"], k + 1)
            dve.tensor_tensor(XL[:, k, :], A[:, k, :], XH[:, k, :].bitcast(F32), ALU.subtract).then_inc(s["merged_lo"], 1)
        lo(T4_ + 1, 1)
        link(dve.memset(SQA[:], 0.0))
        base4 = own.base + own.n
        PER4 = 1

        def residual(n, b):
            a0, a1 = BLOCKS[b]
            an = A[:, bass.ds(n, 1), :].rearrange("p o n -> p (o n)")
            gt = MOD[:, bass.ds(16 + n, 1), :].rearrange("p o c -> p (o c)")
            dve.wait_ge(acc_done[b], P4_ + n + 1)
            if b < 2:
                stt(an[:, a0:a1], PB[:, b, 0:BLK], gt[:, 0:1], xT[:, a0:a1], ALU.mult, ALU.add).then_inc(acc_free[b], 1)
            else:
                stt(an[:, a0:TP], PB[:, b, 0:LP], gt[:, 0:1], xT[:, a0:TP], ALU.mult, ALU.add)
                link(dve.tensor_tensor(an[:, TP:T].rearrange("p (b t) -> p b t", t=ST),
                                       PB[:, b, LP:BLK].rearrange("p (b t) -> p b t", t=ST),
                                       gt[:, 1:NB].rearrange("p (b o) -> p b o", o=1).to_broadcast([P, SB, ST]), ALU.mult))
                dve.tensor_tensor(an[:, TP:T], an[:, TP:T], xT[:, TP:T], ALU.add).then_inc(acc_free[b], 1)

        def scaled(n, a0, a1):
            an = A[:, bass.ds(n, 1), :].rearrange("p o n -> p (o n)")
            asn = AS[:, bass.ds(n, 1), :].rearrange("p o n -> p (o n)")
            s2 = S2[:, bass.ds(n, 1), :].rearrange("p o c -> p (o c)")
            ins = dve.tensor_scalar(asn[:, a0:min(a1, TP)], an[:, a0:min(a1, TP)], s2[:, 0:1], None, ALU.mult)
            if a1 == T:
                ins = dve.tensor_tensor(asn[:, TP:T].rearrange("p (b t) -> p b t", t=ST), an[:, TP:T].rearrange("p (b t) -> p b t", t=ST),
                                        s2[:, 1:NB].rearrange("p (b o) -> p b o", o=1).to_broadcast([P, SB, ST]), ALU.mult)
            return ins

        def phase4(i):
            for x in range(2):
                n = 2 * i + x
                if isinstance(i, int) and n == KT - 1:
                    continue
                own.turn(base4, n, PER4)
                dve.wait_ge(s["xtr_copy"], n + 1)
                for b in range(3):
                    residual(n, b)
                lo(T4_ + n + 2, x)
                dve.wait_ge(acc_free[2], P4_ + n + 1)
                scaled(n, 0, T)
                dve.wait_ge(s["sq_done"], n + 1)
                dve.tensor_tensor(SQA[:], SQA[:], SQ[:], ALU.add).then_inc(s["sqa_done"], 1)
                dve.wait_ge(s["sqa_done"], n + 1)
                assert own.n == PER4, own.n

        with dve.Fori(0, KT // 2 - 1) as i:
            phase4(i)
        phase4(KT // 2 - 1)
        own.turn(base4, KT - 1, PER4)

        def last_residual(b):
            if b == 0:
                dve.wait_ge(s["xtr_copy"], KT)
            residual(KT - 1, b)
            dve.wait_ge(acc_free[b], P4_ + KT)
            scaled(KT - 1, *BLOCKS[b]).then_inc(s["as_done"], 1)

        def rms_diag(b):
            dve.wait_ge(s["rms_sqrt"], b + 1)
            n = GROUPS[2][1]
            mark(dve.reciprocal(rs[:, 3 * b:3 * b + 2], rs[:, 3 * b:3 * b + 2]))
            link(dve.reciprocal(rs[0:n, 3 * b + 2:3 * b + 3], rs[0:n, 3 * b + 2:3 * b + 3]))
            if b >= 1:
                dve.wait_ge(s["rstd_mm"], b)
            for i, (g, n) in enumerate(GROUPS):
                ins = dve.tensor_scalar(DG[0:n, i, 0:n], ident[0:n, 0:n], rs[0:n, 3 * b + i:3 * b + i + 1], None, ALU.mult)
            ins.then_inc(s["rms_diag"], 1)

        def h2_t(b, k):
            a0, a1 = BLOCKS[b][0], min(BLOCKS[b][1], TP)
            i = H2_DVE.index((b, k))
            dve.wait_ge(s["rstd_done"], b + 1)
            dve.wait_ge(s["as_done"], b + 1)
            dve.tensor_tensor(HB[:, i % 6, 0:a1 - a0], AS[:, k, a0:a1], RSTD[:, a0:a1], ALU.mult).then_inc(s["h2_t"], 1)

        def h2_lo(b, k):
            a0, a1 = BLOCKS[b][0], min(BLOCKS[b][1], TP)
            slot = 6 + POOL_H2.index((b, k)) % 3 if (b, k) in POOL_H2 else H2_DVE.index((b, k)) % 6
            dve.wait_ge(s["h2_hi"], KT * b + k + 1)
            stt(XL[:, k, a0:a1], HB[:, slot, 0:a1 - a0], MOD[:, 24 + k, 0:1], XH[:, k, a0:a1].bitcast(F32), ALU.add, ALU.subtract) \
                .then_inc(s["h2_lo"], 1)

        last_residual(0)
        rms_diag(0)
        h2_t(0, 0)
        last_residual(1)
        for k in (1, 2):
            h2_t(0, k)
            h2_lo(0, k - 1)
        rms_diag(1)
        for k in (3, 4, 5):
            h2_t(0, k)
            h2_lo(0, k - 1)
        last_residual(2)
        h2_t(0, 6)
        h2_lo(0, 5)
        rms_diag(2)
        h2_t(0, 7)
        h2_lo(0, 6)
        h2_lo(0, 7)
        for k in range(4):
            h2_lo(1, k)
        dve.wait_ge(s["rstd_done"], 3)
        dve.wait_ge(s["as_done"], 3)
        link(dve.tensor_tensor(YS[:], AS[:, :, TP:T], RSTD[:, TP:T].rearrange("p (o n) -> p o n", o=1).to_broadcast([P, KT, NS]),
                               ALU.mult))
        ys = YS[:].rearrange("p k (b t) -> p k b t", t=ST)
        mark(dve.tensor_tensor(ys[:, 0:4], ys[:, 0:4], bc(MOD[:, 24:28, 1:NB]), ALU.add))
        dve.tensor_tensor(ys[:, 4:8], ys[:, 4:8], bc(MOD[:, 28:32, 1:NB]), ALU.add).then_inc(s["hs_t"], 1)
        for k in range(4, KT):
            h2_lo(1, k)
        h2_t(2, 0)
        lo(T5_ + 1, 1)
        dve.wait_ge(s["hs_hi"], 1)
        dve.tensor_tensor(XL[:, :, TP:T], YS[:], XH[:, :, TP:T].bitcast(F32), ALU.subtract).then_inc(s["hs_lo"], 1)
        for k in range(1, 4):
            h2_t(2, k)
            h2_lo(2, k - 1)
        for k in range(3, KT):
            h2_lo(2, k)
        dve.memset(YS[:], 0.0).then_inc(s["x2n_done"], 1)

        def phase5(f, last=False):
            for m in range(FT):
                dve.wait_ge(acc_free[2], P5_ + 12 * f + m + 1)
                dve.tensor_tensor(R[:, 0, :], R[:, 0, :], R[:, 0, :], ALU.mult).then_inc(s["rr_done"], 1)
                if m < FT - 1:
                    lo(T5_ + 8 * f + m + 2, m % 2)
                dve.wait_ge(s["act_hi"], FT * f + m + 1)
                dve.tensor_tensor(AL[:, m, :], R[:, 0, :], AH[:, m, :].bitcast(F32), ALU.subtract).then_inc(s["act_lo"], 1)
                if m == FT - 1:
                    lo(T5_ + 8 * f + m + 2, m % 2)
            for d in range(4):
                for y in range(2):
                    n = 2 * d + y
                    for b, (a0, a1) in enumerate(BLOCKS):
                        dve.wait_ge(acc_done[b], P5_ + 12 * f + 4 + n + 1)
                        gt = MOD[:, 40 + n, 0:1]
                        if b < 2:
                            stt(A[:, n, a0:a1], PB[:, b, 0:BLK], gt, A[:, n, a0:a1], ALU.mult, ALU.add).then_inc(acc_free[b], 1)
                        else:
                            stt(A[:, n, a0:TP], PB[:, b, 0:LP], gt, A[:, n, a0:TP], ALU.mult, ALU.add)
                            dve.tensor_tensor(YS[:, n, :], PB[:, b, LP:BLK], YS[:, n, :], ALU.add).then_inc(acc_free[b], 1)
                if not (last and d >= 2):
                    lo(T5_ + 8 * f + 4 + d + 2, d % 2)

        phase5(0)
        with dve.Fori(1, 7) as f:
            phase5(f)
        phase5(7, last=True)
        dve.wait_ge(acc_free[2], P5_ + 12 * 8)
        ys = YS[:].rearrange("p k (b t) -> p k b t", t=ST)
        for k0 in (0, 4):
            link(dve.tensor_tensor(ys[:, k0:k0 + 4], ys[:, k0:k0 + 4], bc(MOD[:, 40 + k0:44 + k0, 1:NB]), ALU.mult))
        dve.tensor_tensor(A[:, :, TP:T], A[:, :, TP:T], YS[:], ALU.add).then_inc(s["ys_done"], 1)
        dve.wait_ge(s["gf_in"], 16)
        for b in range(9):
            n = P if b < 8 else NS
            dve.wait_ge(s["y_std"], b + 1)
            link(dve.reciprocal(rs[0:n, b:b + 1], rs[0:n, b:b + 1]))
            if b >= 2:
                dve.wait_ge(y_out[b % 2], 16 * (b // 2))
            bank = 2 * (b % 2)
            stt(Y[0:n, b % 2, :], M[0:n, bank:bank + 2, :].rearrange("p a n -> p (a n)"), rs[0:n, b:b + 1], GF[0:n, :],
                ALU.mult, ALU.mult).then_inc(s["y_done"], 1)

    ctx.close()


_INS = ["x_prompt", "x_sample", "state_conv", "state_C", "state_n", "state_m", "c_prompt", "c_sample", "w_ada", "b_ada",
        "g_norm1", "g_norm2", "w_in", "b_gate", "conv_w", "conv_b", "hn_g", "w_out", "w_up", "w_down", "g_final"]
_OUTS = {"y_prompt": (1, 1024, 1024), "y_sample": (8, 4, 1024), "p_conv": (1, 1, 2, 1024), "p_C": (1, 1, 4, 128, 256),
         "p_n": (1, 1, 4, 128), "p_m": (1, 1, 4), "s_conv": (1, 8, 2, 1024), "s_C": (1, 8, 4, 128, 256),
         "s_n": (1, 8, 4, 128), "s_m": (1, 8, 4)}


def kernel(**inputs):
    import numpy as np
    import concourse.bacc as bacc
    from concourse.bass_utils import run_bass_kernel_spmd

    nc = bacc.Bacc("TRN2", target_bir_lowering=False, num_devices=1)
    arrays, I, O = {}, {}, {}
    for name in _INS:
        a = np.ascontiguousarray(inputs[name])
        arrays[f"in_{name}"] = a
        I[name] = nc.dram_tensor(f"in_{name}", a.shape, F32, kind="ExternalInput").ap()
    for name, shape in _OUTS.items():
        O[name] = nc.dram_tensor(f"out_{name}", shape, F32, kind="ExternalOutput").ap()
    layer_kernel(nc, I, O)
    r = run_bass_kernel_spmd(nc, [arrays], core_ids=[0])
    return tuple(r.results[0][f"out_{name}"] for name in _OUTS)
```

```python
from contextlib import ExitStack

import concourse.bass as bass
from concourse import mybir
from concourse.alu_op_type import AluOpType as ALU

F32 = mybir.dt.float32
F32R = mybir.dt.float32r
ACT = mybir.ActivationFunctionType

P = 128
D = 1024
KT = D // P
TP = 1024
SB, ST = 8, 4
NS = SB * ST
T = TP + NS
BLK = T // 3
LP = TP - 2 * BLK
H, DK, DV = 4, 128, 256
L = 128
NC = TP // L
FF = 4 * D
FT = FF // P // 8
EPS = 1e-6
CAP = 15.0
KSCALE = DK ** -0.5
NB = 1 + SB
XC, BG, CG, WQ, WK, WV, WO, WGATE, GA, GB = 0, 1024, 2048, 3072, 3584, 4096, 5120, 6144, 6152, 7176
T1_, T2_, T3_, T4_, T5_ = 0, 16, 48, 64, 72
P1_, P2_, P3_, P4_, P5_ = 0, 16, 48, 64, 72
NT = 136
G1R, G2R, CBR, CWR, HNR, BAR, PROWS = 0, 8, 16, 24, 48, 56, 104
RING0 = 7
GM, WS, MR = range(3)
BLOCKS = [(0, BLK), (BLK, 2 * BLK), (2 * BLK, T)]
GROUPS = [(g, min(P, BLK - g)) for g in range(0, BLK, P)]
Y_GROUPS = [(b * BLK + g, n) for b in range(3) for g, n in GROUPS]
POOL_H2 = [(b, k) for b in (1, 2) for k in range(KT) if k % 3 != 0]
H2_DVE = [(b, k) for b in range(3) for k in range(KT) if (b, k) not in POOL_H2]


class Count:

    def __init__(self, eng, sem):
        self.eng, self.sem, self.base, self.n = eng, sem, 0, 0

    def mark(self, ins):
        ins.then_inc(self.sem, 1)
        self.n += 1
        return self.base + self.n

    def wait(self, value):
        self.eng.wait_ge(self.sem, value)

    def link(self, ins):
        self.wait(self.mark(ins))

    def turn(self, base, i, per):
        self.base, self.n = base + i * per, 0


def layer_kernel(nc, I, O):
    ctx = ExitStack()
    early, startup, gates, mixer, mlstm, outp, mlp, norm2 = (ExitStack() for _ in range(8))

    def sb(name, shape, dt=F32, scope=ctx):
        return scope.enter_context(nc.sbuf_tensor(name, shape, dt))

    def sem(name):
        return ctx.enter_context(nc.semaphore(name))

    zp_d = nc.dram_tensor("zp_d", [4 * H, P, TP], F32, kind="Internal").ap()
    zs_d = nc.dram_tensor("zs_d", [2 * H, 4, P, 16], F32, kind="Internal").ap()
    rp_d = nc.dram_tensor("rp_d", [H, TP], F32, kind="Internal").ap()
    rs_d = nc.dram_tensor("rs_d", [2 * H, 16], F32, kind="Internal").ap()

    XH = sb("XH", [P, KT, T], F32R)
    XL = sb("XL", [P, KT, T], F32R)
    A = sb("A", [P, KT, T])
    raw = sb("raw", [P, 2, 1024])
    whi = sb("whi", [P, 2, 1024], F32R)
    wlo = sb("wlo", [P, 2, 1024], F32R)
    ident = sb("ident", [P, P])
    ones = sb("ones", [P, P])
    MOD = sb("MOD", [P, 48, NB])
    S1 = sb("S1", [P, KT, NB])
    S2 = sb("S2", [P, KT, NB])
    PC = sb("PC", [P, PROWS])
    COL = sb("COL", [P, NC, 3, H])
    COLS = sb("COLS", [16, 2 * H, 3])
    CM = sb("CM", [P, P])
    CMS = sb("CMS", [16, 16])
    BM = sb("BM", [16, 4])
    NT_ = sb("NT_", [P, NS])
    SCV = sb("SCV", [P, KT, 16])
    NCV = sb("NCV", [P, KT, 18])
    ss = sb("ss", [P, 9])
    rs = sb("rs", [P, 9])
    epsc = sb("epsc", [P, 1])

    cS = sb("cS", [P, KT, P], F32R, scope=early)
    cT = sb("cT", [P, KT, NB], scope=early)
    GW = sb("GW", [P, KT, P], F32R, scope=early)
    wg = sb("wg", [P, KT, 2 * H], scope=early)
    M0s = sb("M0s", [H, SB], scope=early)
    MP = sb("MP", [H, NC], scope=early)
    PM = sb("PM", [H, 1], scope=early)
    SMo = sb("SMo", [H, SB], scope=early)
    bg15 = sb("bg15", [36, 1], scope=early)
    AROW = sb("AROW", [P, 512], scope=early)
    xin = sb("xin", [P, 9, D], scope=startup)
    araw0 = sb("araw0", [P, RING0, 1024], scope=startup)
    junk = sb("junk", [P, D], scope=startup)
    startup.close()
    araw = sb("araw", [P, 2, 1024], scope=gates)
    ahi = sb("ahi", [P, 2, 1024], F32R, scope=gates)
    alo = sb("alo", [P, 2, 1024], F32R, scope=gates)
    zr = sb("zr", [P, 2, T], scope=gates)
    GT = sb("GT", [36, T], scope=gates)
    TH = sb("TH", [36, T], scope=gates)
    NBr = sb("NBr", [36, T], scope=gates)
    RMK = sb("RMK", [36, T], scope=gates)
    NB0, DL, MU = RMK[0:H], NBr[0:H], TH[0:H]
    RR = sb("RR", [H, T], scope=gates)
    GMR = sb("GMR", [H, T], scope=gates)
    WSR = sb("WSR", [H, T], scope=gates)
    MRR = sb("MRR", [H, T], scope=gates)
    gates.close()
    early.close()
    hm = sb("hm", [P, KT, TP], scope=mixer)
    hms = sb("hms", [P, 2 * H, 2, 16], scope=mixer)
    G1 = sb("G1", [P, T], scope=mixer)
    U = sb("U", [P, 2 + TP + 6 * SB], scope=mixer)
    Z = sb("Z", [P, 4 * H, L], scope=mlstm)
    VT = sb("VT", [P, H, DV + 1], scope=mlstm)
    CA = sb("CA", [P, H, DV + 1], scope=mlstm)
    RB = sb("RB", [P, H, L], scope=mlstm)
    IB = sb("IB", [P, H, L], scope=mlstm)
    EX = sb("EX", [P, H, L], scope=mlstm)
    KW = sb("KW", [P, H, DK], scope=mlstm)
    HT = sb("HT", [P, H, DV], scope=mlstm)
    DEC = sb("DEC", [P, H], scope=mlstm)
    sc4 = sb("sc4", [P, 8, H], scope=mlstm)
    ZU = sb("ZU", [P, 4, 16], scope=mlstm)
    VTU = sb("VTU", [P, DV + 2], F32R, scope=mlstm)
    CU = sb("CU", [P, 4, DV + 1], scope=mlstm)
    RU = sb("RU", [P, 16], scope=mlstm)
    IU = sb("IU", [P, 16], scope=mlstm)
    EU = sb("EU", [16, 16], scope=mlstm)
    QM = sb("QM", [P, 80], scope=mlstm)
    EUS = sb("EUS", [P, 16], F32R, scope=mlstm)
    KU = sb("KU", [P, 4, DK], F32R, scope=mlstm)
    WM = sb("WM", [16, 4], scope=mlstm)
    HTU = sb("HTU", [16, DV], scope=mlstm)
    DECU = sb("DECU", [P, 4], scope=mlstm)
    sc1 = sb("sc1", [16, 8], scope=mlstm)
    mlstm.close()
    NCR = sb("NCR", [18, D], scope=outp)
    NR = sb("NR", [NS, P], scope=outp)
    PN = sb("PN", [H, P], scope=outp)
    xs = sb("xs", [P, 2, 9, P], scope=outp)
    xT = sb("xT", [P, T], scope=outp)
    SQ = sb("SQ", [P, T], scope=outp)
    DG = sb("DG", [P, 3, P], scope=outp)
    outp.close()
    mixer.close()
    AS = sb("AS", [P, KT, T], scope=norm2)
    norm2.close()
    AH = sb("AH", [P, FT, T], F32R, scope=mlp)
    AL = sb("AL", [P, FT, T], F32R, scope=mlp)
    SQA = sb("SQA", [P, T], scope=mlp)
    Y = sb("Y", [P, 2, D], scope=mlp)
    R = sb("R", [P, 3, T], scope=mlp)
    YS = sb("YS", [P, KT, NS], scope=mlp)
    GF = sb("GF", [P, D], scope=mlp)
    mlp.close()
    RSTD = Y[:].rearrange("p a n -> p (a n)")[:, 0:T]
    HB = R[:].rearrange("p a (b n) -> p (a b) n", b=3)
    CR = A[:, 0, :]
    CG_ = A[:, 1, :]
    SCR = raw[:, 0, :]
    PR = raw[:, 1, 0:P]
    SNR = raw[:, 1, P:2 * P]

    PB = ctx.enter_context(nc.psum_tensor("PB", [P, 3, 512], F32))
    M = ctx.enter_context(nc.psum_tensor("M", [P, 5, 512], F32))

    names = """c_in p_in small_in raw0 raw1 hi_done lo_done acc_done0 acc_done1 acc_done2 acc_free0 acc_free1 acc_free2 ada0_mm
    arow_done rowt_done mod_done xrt_done xn_done xt_done xt_free pool_done csig_done ct_done ct_used gw_done
    sm_done h_hi h_lo hf_done araw_in0 araw_in1 ahi_done alo_done a_used z_out0 z_out1 gate_mm gate_sum gate_act
    gate_rows r_out cols_mm cols_done m_out z_in zu_in rb_in cu_in cu_out qk_done kt_done vt_done upre_done
    num_done unum_done cup_done ucup0_done ucup1_done ht_done ib_exp e_exp vt_copy unit_hi wm_done eu_ready
    eu_hi ss_done std_done ex_done qi_done cn_done p_done kw_done var_done ht_ready c_upd ucup0_upd ucup1_upd
    hm_done conv_done a_done fin1_mm fin1_copy st_out merged split_hi xs_in0 xs_in1 xtr_done xtr_copy sq_done
    rms_sqrt h2_t h2_tp h2_hi h2_lo hs_t hs_hi hs_lo sqa_done rms_mm rms_diag rstd_mm rstd_done as_done rr_done
    act_hi act_lo down_done down_free y_mm y_sq y_std y_done y_out0 y_out1 gf_in dve_step act_step x2n_done
    ys_done merged_lo""".split()
    s = {n: sem(n) for n in names}
    xr = [sem(f"x_in{b}") for b in range(9)]
    ar0 = [sem(f"ada_in{b}") for b in range(RING0)]
    raw_in = [s["raw0"], s["raw1"]]
    araw_in = [s["araw_in0"], s["araw_in1"]]
    xs_in = [s["xs_in0"], s["xs_in1"]]
    y_out = [s["y_out0"], s["y_out1"]]
    z_out = [s["z_out0"], s["z_out1"]]
    acc_done = [s[f"acc_done{b}"] for b in range(3)]
    acc_free = [s[f"acc_free{b}"] for b in range(3)]

    w_in = I["w_in"].rearrange("l (k p) n -> (l p) k n", p=P)
    w_out = I["w_out"].rearrange("l (k p) n -> (l p) k n", p=P)
    w_up = I["w_up"].rearrange("l (k p) n -> (l p) k n", p=P)
    w_down = I["w_down"].rearrange("l (k p) n -> (l p) k n", p=P)
    w_ada = I["w_ada"].rearrange("l (k p) n -> (l p) k n", p=P)
    x_p = I["x_prompt"].rearrange("a (b p) n -> p (a b) n", p=P)
    x_s = I["x_sample"].rearrange("a b n -> (a b) n")
    st_C = I["state_C"].rearrange("l (x u) h d v -> l x (u h) d v", u=2)
    so_C = O["s_C"].rearrange("l (x u) h d v -> l x (u h) d v", u=2)
    ADA0 = [0, 2, 1, 3]

    def y_psum(r, n):
        bank = M[0:n, 2 * (r % 2):2 * (r % 2) + 2, :] if r < 8 else PB[0:n, 0:2, :]
        return bank.rearrange("p a n -> p (a n)")

    def y_rows(r, n):
        return Y[0:n, r % 2, :] if r < 8 else R[0:n, 2, 0:D]

    block = ctx.enter_context(nc.Block())

    @block.sync
    def _(sp):
        def tile(t, slot, src):
            if not (isinstance(t, int) and t < 2):
                sp.wait_ge(s["lo_done"], t - 1)
            k = src.shape[1]
            sp.dma_start(raw[:, slot, :].rearrange("p (k n) -> p k n", k=k), src).then_inc(raw_in[slot], 16)

        sp.dma_start(CR[0:1, 0:D], I["c_prompt"]).then_inc(s["c_in"], 16)
        sp.dma_start(CR[1:NB, 0:D], I["c_sample"]).then_inc(s["c_in"], 16)
        params = [(I[name].rearrange("l (r p) -> (l r) p", p=P), r0, n) for name, r0, n in
                  (("b_ada", BAR, 48), ("g_norm1", G1R, 8), ("g_norm2", G2R, 8), ("conv_b", CBR, 8), ("hn_g", HNR, 8))]
        params.append((I["conv_w"].rearrange("l w (r p) -> (l w r) p", p=P), CWR, 24))

        def param(i):
            src, r0, n = params[i]
            sp.dma_start(PR[r0:r0 + n, :], src).then_inc(s["p_in"], 16)

        def load_x(b):
            if b < 8:
                sp.dma_start(xin[:, b, :], x_p[:, b, :]).then_inc(xr[b], 16)
            else:
                sp.dma_start(xin[0:NS, b, :], x_s).then_inc(xr[b], 16)

        def ada0(n):
            if n >= RING0:
                sp.wait_ge(s["ada0_mm"], n - RING0 + 1)
            c = ADA0[n // 4] * 512
            k = n % 4 * 2
            sp.dma_start(araw0[:, n % RING0, :].rearrange("p (k n) -> p k n", k=2),
                         w_ada[:, k:k + 2, c:c + 512]).then_inc(ar0[n % RING0], 16)

        for b in range(3):
            ada0(b)
            param(2 * b)
            load_x(b)
            param(2 * b + 1)
        sp.dma_start(SNR[0:NS, :], I["state_n"].rearrange("l b h d -> (l b h) d")).then_inc(s["p_in"], 16)
        sp.dma_start(SCR[0:16, 0:D], I["state_conv"].rearrange("l b w n -> (l b w) n")).then_inc(s["p_in"], 16)
        ada0(3)
        sp.dma_start(wg[:], w_in[:, :, WGATE:WGATE + 2 * H]).then_inc(s["small_in"], 16)
        sp.wait_ge(s["sm_done"], 1)
        sp.dma_start(bg15[0:H, :], I["b_gate"][:, 0:H].rearrange("l h -> h l"), allow_slow_non_contiguous=True).then_inc(s["small_in"], 16)
        load_x(3)
        sp.dma_start(bg15[32:32 + H, :], I["b_gate"][:, H:2 * H].rearrange("l h -> h l"), allow_slow_non_contiguous=True).then_inc(s["small_in"], 16)
        load_x(4)
        sp.dma_start(M0s[:], I["state_m"].rearrange("l b h -> h (l b)"), allow_slow_non_contiguous=True).then_inc(s["small_in"], 16)
        load_x(5)
        for n in range(4, 7):
            ada0(n)
        load_x(6)
        ada0(7)
        load_x(7)
        load_x(8)
        for n in range(8, 12):
            ada0(n)
        sp.wait_ge(s["ct_used"], 2)
        tile(0, 0, w_in[:, :, WQ:WQ + P])
        for n in range(12, 16):
            ada0(n)
        tile(1, 1, w_in[:, :, WK:WK + P])
        sp.wait_ge(s["ada0_mm"], 16)
        sp.wait_ge(s["xt_done"], 9)

        def atile(a, slot, q, c0):
            if not (isinstance(a, int) and a < 2):
                sp.wait_ge(s["alo_done"], a - 1)
            sp.dma_start(araw[:, slot, :].rearrange("p (k n) -> p k n", k=2),
                         w_ada[:, 2 * q:2 * q + 2, bass.ds(c0, 512)]).then_inc(araw_in[slot], 16)

        atile(0, 0, 0, 2048)
        atile(1, 1, 1, 2048)

        def phase1(h, first_next=None):
            cols = [WV + 256 * h, WV + P + 256 * h, WQ + P + P * h, WK + P + P * h]
            for k in range(4):
                t = T1_ + 4 * h + k
                for x in range(2):
                    a = 2 * k + x + 2
                    if isinstance(h, int) and h == H - 1 and a >= 8:
                        continue
                    atile(8 * h + a, x, a % 4, 2048 + 1024 * h + 512 * (a // 4))
                if isinstance(h, int) and h == H - 1 and k >= 2:
                    tile(t + 2, k % 2, w_in[:, :, [XC, CG][k - 2]:][:, :, 0:P])
                else:
                    tile(t + 2, k % 2, w_in[:, :, bass.ds(cols[k], P)])

        phase1(0)
        with sp.Fori(1, H - 1) as h:
            phase1(h)
        phase1(H - 1)

        def stage(c):
            if isinstance(c, int) and c == 0:
                sp.wait_ge(z_out[0], 32 * 2 * H)
                sp.wait_ge(z_out[1], 32 * 2 * H)
                sp.wait_ge(s["r_out"], 32)
                sp.wait_ge(s["cols_mm"], 1)
                sp.wait_ge(s["a_used"], 32)
                sp.wait_ge(s["m_out"], 32)
            else:
                sp.wait_ge(s["vt_done"], c)
                sp.wait_ge(s["upre_done"], c)
                sp.wait_ge(s["qi_done"], c)
                sp.wait_ge(s["ex_done"], c)
            sp.dma_start(Z[:], zp_d.rearrange("j p n -> p j n")[:, :, bass.ds(c * L, L)]).then_inc(s["z_in"], 16)
            sp.dma_start(RB[:], rp_d[:, bass.ds(c * L, L)].rearrange("(o h) n -> o h n", o=1)
                         .broadcast_to([P, H, L])).then_inc(s["rb_in"], 16)
            sp.dma_start(RU[:], rs_d[bass.ds(c, 1), :].broadcast_to([P, 16])).then_inc(s["rb_in"], 16)
            sp.dma_start(ZU[:], zs_d[bass.ds(c, 1)].rearrange("u k p n -> p (u k) n")).then_inc(s["zu_in"], 16)

        def load_cu(c):
            sp.dma_start(CU[:, :, 0:DV], st_C[0, :, bass.ds(c, 1)].rearrange("x u d v -> d (x u) v")) \
              .then_inc(s["cu_in"], 16)

        def store_cu(c):
            sp.dma_start(so_C[0, :, bass.ds(c, 1)].rearrange("x u d v -> d (x u) v"), CU[:, :, 0:DV]) \
              .then_inc(s["cu_out"], 16)

        def phase2(c, last=False):
            for k, col in ((2, BG), (3, GA)):
                tile(T2_ + 4 * c + k, k % 2, w_in[:, :, bass.ds(col + P * c, P)])
                if k == 2 and not (isinstance(c, int) and c == 0):
                    sp.wait_ge(s["ucup1_upd"], c)
                    store_cu(c - 1)
                    sp.wait_ge(s["cu_out"], 16 * c)
                    load_cu(c)
            if not last:
                stage(c + 1)
            for k in range(2):
                col = [WO, GB][k] if last else [XC + P, CG + P][k] + P * c
                tile(T2_ + 4 * c + 4 + k, k % 2, w_in[:, :, bass.ds(col, P)])

        stage(0)
        load_cu(0)
        phase2(0)
        with sp.Fori(1, NC - 1) as c:
            phase2(c)
        phase2(NC - 1, last=True)
        sp.wait_ge(s["ucup1_upd"], NC)
        store_cu(NC - 1)
        sp.wait_ge(s["c_upd"], NC)
        sp.dma_start(O["p_C"].rearrange("l b h d v -> d (l b h) v"), CA[:, :, 0:DV]).then_inc(s["st_out"], 16)
        with sp.Fori(0, KT - 1) as j:
            tile(T3_ + 2 + 2 * j, 0, w_in[:, :, bass.ds(WO + P + P * j, P)])
            tile(T3_ + 3 + 2 * j, 1, w_in[:, :, bass.ds(GB + P + P * j, P)])
        sp.wait_ge(s["fin1_copy"], 2)
        sp.dma_start(O["s_conv"].rearrange("l b w n -> (l b w) n"), NCR[0:16, :]).then_inc(s["st_out"], 16)
        sp.dma_start(O["p_conv"].rearrange("l b w n -> (l b w) n"), NCR[16:18, :]).then_inc(s["st_out"], 16)
        sp.dma_start(O["s_n"].rearrange("l b h d -> (l b h) d"), NR[:]).then_inc(s["st_out"], 16)
        sp.dma_start(O["p_n"].rearrange("l b h d -> (l b h) d"), PN[:]).then_inc(s["st_out"], 16)
        tile(T4_, 0, w_out[:, :, 0:P])
        tile(T4_ + 1, 1, w_out[:, :, P:2 * P])

        def load_xs(n, slot):
            sp.dma_start(xs[:, slot, 0:8, :], x_p[:, :, bass.ds(n * P, P)]).then_inc(xs_in[slot], 16)
            sp.dma_start(xs[0:NS, slot, 8, :], x_s[:, bass.ds(n * P, P)]).then_inc(xs_in[slot], 16)

        sp.wait_ge(s["cu_out"], 16 * NC)
        sp.wait_ge(s["st_out"], 16)
        load_xs(0, 0)
        load_xs(1, 1)
        with sp.Fori(0, KT // 2 - 1) as i:
            for x in range(2):
                tile(T4_ + 2 + 2 * i + x, x, w_out[:, :, bass.ds((2 + 2 * i + x) * P, P)])
                sp.wait_ge(s["xtr_done"], 2 * i + 1 + x)
                load_xs(2 * i + 2 + x, x)
        tile(T5_, 0, w_up[:, :, 0:P])
        tile(T5_ + 1, 1, w_up[:, :, P:2 * P])

        def mlp_tiles(f, last=False):
            for m in (2, 3):
                tile(T5_ + 8 * f + m, m % 2, w_up[:, :, bass.ds(512 * f + P * m, P)])
            for d in range(4):
                tile(T5_ + 8 * f + 4 + d, d % 2, w_down[:, bass.ds(4 * f, 4), 256 * d:256 * d + 256])
            if not last:
                for m in (0, 1):
                    tile(T5_ + 8 * f + 8 + m, m % 2, w_up[:, :, bass.ds(512 * f + 512 + P * m, P)])

        with sp.Fori(0, 7) as f:
            mlp_tiles(f)
        mlp_tiles(7, last=True)
        sp.wait_ge(s["x2n_done"], 1)
        sp.dma_start(GF[:], I["g_final"].rearrange("(o n) -> o n", o=1).broadcast_to([P, D])).then_inc(s["gf_in"], 16)
        y_p = O["y_prompt"].rearrange("a t n -> (a t) n")
        for r, (t0, n) in enumerate(Y_GROUPS):
            sp.wait_ge(s["y_done"], r + 1)
            m = min(n, TP - t0)
            sp.dma_start(y_p[t0:t0 + m, :], y_rows(r, n)[0:m, :]).then_inc(y_out[r % 2], 16)
            if m < n:
                sp.dma_start(O["y_sample"].rearrange("a b n -> (a b) n"), y_rows(r, n)[m:n, :]).then_inc(y_out[r % 2], 16)
        sp.wait_ge(y_out[0], 16 * 6)
        sp.wait_ge(y_out[1], 16 * 4)
        sp.wait_ge(s["st_out"], 16 * 5)

    @block.gpsimd
    def _(pool):
        n = 0

        def step(ins):
            nonlocal n
            ins.then_inc(s["pool_done"], 1)
            n += 1
            pool.wait_ge(s["pool_done"], n)

        step(pool.memset(ident[:], 0.0))
        step(pool.affine_select(out=ident[:], in_=ident[:], compare_op=ALU.not_equal, fill=1.0, base=0,
                                pattern=[[-1, P]], channel_multiplier=1))
        step(pool.memset(ones[:], 1.0))
        step(pool.memset(CM[:], 0.0))
        step(pool.affine_select(out=CM[:], in_=CM[:], compare_op=ALU.is_ge, fill=-1e30, base=0,
                                pattern=[[1, P]], channel_multiplier=-1))
        step(pool.memset(CMS[:], 0.0))
        step(pool.affine_select(out=CMS[:], in_=CMS[:], compare_op=ALU.is_ge, fill=-1e30, base=0,
                                pattern=[[1, 16]], channel_multiplier=-1))
        v = CMS[:].rearrange("p (b t) -> p b t", t=ST)
        step(pool.affine_select(out=v, in_=v, compare_op=ALU.is_ge, fill=-1e30, base=0,
                                pattern=[[-ST, 4], [0, ST]], channel_multiplier=1))
        step(pool.memset(BM[:], 1.0))
        step(pool.affine_select(out=BM[:], in_=BM[:], compare_op=ALU.is_ge, fill=0.0, base=0,
                                pattern=[[-ST, 4]], channel_multiplier=1))
        step(pool.affine_select(out=BM[:], in_=BM[:], compare_op=ALU.is_ge, fill=0.0, base=ST - 1,
                                pattern=[[ST, 4]], channel_multiplier=-1))

        for i, (b, k) in enumerate(POOL_H2):
            a0, a1 = BLOCKS[b][0], min(BLOCKS[b][1], TP)
            pool.wait_ge(s["rstd_done"], b + 1)
            if i == 0:
                pool.wait_ge(s["as_done"], 2)
            elif (b, k) == (2, KT - 1):
                pool.wait_ge(s["as_done"], 3)
            if i >= 6:
                pool.wait_ge(s["h2_lo"], KT * POOL_H2[i - 6][0] + POOL_H2[i - 6][1] + 1)
            pool.tensor_tensor(HB[:, 3 + i % 6, 0:a1 - a0], AS[:, k, a0:a1], RSTD[:, a0:a1], ALU.mult) \
                .then_inc(s["h2_tp"], 1)

    POOL_STEPS = 11

    @block.scalar
    def _(act):
        own = Count(act, s["act_step"])
        act.wait_ge(s["c_in"], 32)
        act.activation(CG_[0:NB, 0:D], CR[0:NB, 0:D], ACT.Sigmoid).then_inc(s["csig_done"], 1)

        def squares(g):
            for b in range(3 * g, 3 * g + 3):
                n = P if b < 8 else NS
                act.wait_ge(xr[b], 16)
                own.link(act.activation(junk[0:n, :], xin[0:n, b, :], ACT.Square, accum_out=ss[0:n, b:b + 1]))
            if g < 2:
                act.activation(rs[:, 3 * g:3 * g + 3], ss[:, 3 * g:3 * g + 3], ACT.Sqrt, bias=epsc[:, 0:1],
                               scale=1.0 / D).then_inc(s["xrt_done"], 1)
            else:
                act.activation(rs[:, 6:8], ss[:, 6:8], ACT.Sqrt, bias=epsc[:, 0:1], scale=1.0 / D)
                act.activation(rs[0:NS, 8:9], ss[0:NS, 8:9], ACT.Sqrt, bias=epsc[0:NS, 0:1],
                               scale=1.0 / D).then_inc(s["xrt_done"], 1)

        def xt_evac(b):
            n = P if b < 8 else NS
            src = (M if b % 2 == 0 else PB)[:, 0:2, :].rearrange("p a (k n) -> p (a k) n", n=P)[:, :, 0:n]
            act.wait_ge(s["xt_done"], b + 1)
            act.activation(A[:, :, b * P:b * P + n], src, ACT.Copy).then_inc(s["xt_free"], 1)

        act.wait_ge(s["sm_done"], 1)
        squares(0)
        act.wait_ge(s["ct_used"], 1)
        for b in range(3):
            xt_evac(b)
        squares(1)
        for b in range(3, 6):
            xt_evac(b)
        squares(2)

        def hi(t, slot, free=None):
            act.wait_ge(raw_in[slot], 8 * (t - slot) + 16)
            if not (isinstance(t, int) and t < 2):
                act.wait_ge(acc_done[2], t - 1 if free is None else free)
            act.activation(whi[:, slot, :], raw[:, slot, :], ACT.Copy).then_inc(s["hi_done"], 1)

        def ahi_(a, slot):
            act.wait_ge(araw_in[slot], 8 * (a - slot) + 16)
            if not (isinstance(a, int) and a < 2):
                act.wait_ge(s["a_used"], a - 1)
            act.activation(ahi[:, slot, :], araw[:, slot, :], ACT.Copy).then_inc(s["ahi_done"], 1)

        def h_hi(k):
            act.wait_ge(s["hf_done"], k + 1)
            act.activation(XH[:, k, :], A[:, k, :], ACT.Copy).then_inc(s["h_hi"], 1)

        hi(0, 0)
        for b in range(6, 9):
            xt_evac(b)
        for k in range(KT):
            h_hi(k)
        hi(1, 1)
        ahi_(0, 0)
        ahi_(1, 1)

        def phase1(h):
            last = isinstance(h, int) and h == H - 1
            for k in range(4):
                t, slot = T1_ + 4 * h + k, k % 2
                if not (isinstance(h, int) and h == 0 and k < 2):
                    act.wait_ge(z_out[slot], 64 * h + 32 * (k // 2))
                a_after = 2 if isinstance(h, int) and h == k == 0 else 0
                for b, (a0, a1) in enumerate(BLOCKS):
                    act.wait_ge(acc_done[b], P1_ + 4 * h + k + 1)
                    if b < 2:
                        act.activation(zr[:, slot, a0:a1], PB[:, b, 0:BLK], ACT.Copy).then_inc(acc_free[b], 1)
                    else:
                        act.activation(zr[:, slot, a0:TP], PB[:, b, 0:LP], ACT.Copy)
                        act.activation(zr[:, slot, TP:T].rearrange("p (u b t) -> p b u t", u=2, t=ST),
                                       PB[:, b, LP:BLK].rearrange("p (b u t) -> p b u t", u=2, t=ST),
                                       ACT.Copy).then_inc(acc_free[b], 1)
                    if b == a_after and not (last and k == 3):
                        for x in range(2):
                            ahi_(8 * h + 2 * k + 2 + x, x)
                hi(t + 2, slot)
                act.wait_ge(acc_free[2], P1_ + 4 * h + k + 1)
                act.dma_start(zp_d[bass.ds(4 * h + k, 1)].rearrange("o p n -> (o p) n"), zr[:, slot, 0:TP]) \
                   .then_inc(z_out[slot], 16)
                act.dma_start(zs_d.rearrange("(u h) k p n -> k h p u n", u=2)[k, bass.ds(h, 1)]
                              .rearrange("o p u n -> (o p) u n"),
                              zr[:, slot, TP:T].rearrange("p (u n) -> p u n", u=2)).then_inc(z_out[slot], 16)

        def gate_acts():
            act.wait_ge(s["gate_sum"], 1)
            own.link(act.activation(TH[:], GT[:], ACT.Tanh, bias=bg15[:, 0:1], scale=1.0 / CAP))
            own.link(act.activation(GT[32:36, :], TH[32:36, :], ACT.Exp, scale=-CAP))
            act.activation(GT[32:36, :], GT[32:36, :], ACT.Ln, bias=1.0).then_inc(s["gate_act"], 1)

        phase1(0)
        gate_acts()
        phase1(1)
        phase1(2)
        act.wait_ge(s["gate_rows"], 1)
        act.dma_start(rp_d, RR[:, 0:TP]).then_inc(s["r_out"], 16)
        act.dma_start(rs_d.rearrange("(u h) n -> h u n", u=2), RR[:, TP:T].rearrange("h (u n) -> h u n", u=2)) \
           .then_inc(s["r_out"], 16)
        act.dma_start(O["p_m"].rearrange("l b h -> h (l b)"), PM[:], allow_slow_non_contiguous=True).then_inc(s["m_out"], 16)
        act.dma_start(O["s_m"].rearrange("l b h -> h (l b)"), SMo[:], allow_slow_non_contiguous=True).then_inc(s["m_out"], 16)
        phase1(3)
        act.wait_ge(s["cols_mm"], 1)
        cp = M[:, 0, 0:NC * 3 * H].rearrange("p (c k h) -> p c k h", k=3, h=H)
        cs = M[0:16, 1, 0:24].rearrange("p (k u) -> p u k", k=3)
        act.activation(COL[:, :, GM, :], cp[:, :, GM, :], ACT.Copy)
        act.activation(COL[:, :, WS, :], cp[:, :, WS, :], ACT.Exp)
        act.activation(COL[:, :, MR, :], cp[:, :, MR, :], ACT.Exp, scale=-1.0)
        act.activation(COLS[:, :, GM], cs[:, :, GM], ACT.Copy)
        act.activation(COLS[:, :, WS], cs[:, :, WS], ACT.Exp)
        act.activation(COLS[:, :, MR], cs[:, :, MR], ACT.Exp, scale=-1.0).then_inc(s["cols_done"], 1)

        act.wait_ge(z_out[0], 32 * 2 * H)
        act.wait_ge(z_out[1], 32 * 2 * H)
        act.wait_ge(s["r_out"], 32)
        act.wait_ge(s["m_out"], 32)

        def phase2(c):
            first = isinstance(c, int) and c == 0
            if not first:
                act.wait_ge(s["a_done"], c)
            for b, (a0, a1) in enumerate(BLOCKS):
                act.wait_ge(acc_done[b], P2_ + 4 * c + 1)
                ins = act.activation(G1[:, a0:a1], PB[:, b, 0:BLK], ACT.Copy)
                ins.then_inc(acc_free[b], 1)
            hi(T2_ + 4 * c + 2, 0)
            act.wait_ge(s["rb_in"], 32 * c + 32)
            act.activation(IB[:], RB[:], ACT.Exp)
            act.activation(IU[:], RU[:], ACT.Exp).then_inc(s["ib_exp"], 1)
            act.wait_ge(s["ex_done"], c + 1)
            act.activation(EX[:], EX[:], ACT.Exp)
            act.activation(EU[:], EU[:], ACT.Exp).then_inc(s["e_exp"], 1)
            act.wait_ge(s["vt_done"], c + 1)
            for x in range(2):
                last = act.activation(VT[:, 2 * x:2 * x + 2, 0:DV], M[:, 1 + x, :].rearrange("p (h v) -> p h v", v=DV), ACT.Copy)
            last.then_inc(s["vt_copy"], 1)
            act.wait_ge(s["upre_done"], c + 1)
            act.activation(VTU[0:16, 0:DV], M[0:16, 4, 128:128 + DV], ACT.Copy)
            act.wait_ge(s["wm_done"], c + 1)
            for b in range(4):
                last = act.activation(KU[0:16, b, :], M[0:16, 4, 384:512], ACT.Copy, scale=WM[:, b:b + 1])
            last.then_inc(s["unit_hi"], 1)
            act.wait_ge(s["eu_ready"], c + 1)
            for r in (0, 32):
                last = act.activation(EUS[r:r + 16, :], EU[:], ACT.Copy)
            last.then_inc(s["eu_hi"], 1)
            hi(T2_ + 4 * c + 3, 1)
            act.wait_ge(s["num_done"], c + 1)
            for h in range(H):
                act.activation(HT[:, h, :], M[:, h, 0:DV], ACT.Square, accum_out=sc4[:, 0, h:h + 1])
            act.wait_ge(s["unum_done"], c + 1)
            act.activation(HTU[:], M[0:16, 4, 0:DV], ACT.Square, accum_out=sc1[:, 0:1]).then_inc(s["ss_done"], 1)
            act.wait_ge(s["var_done"], c + 1)
            act.activation(sc4[:, 1, :], sc4[:, 5, :], ACT.Sqrt, bias=epsc[:, 0:1], scale=1.0 / DV)
            act.activation(sc1[:, 1:2], sc1[:, 5:6], ACT.Sqrt, bias=epsc[0:16, 0:1], scale=1.0 / DV) \
               .then_inc(s["std_done"], 1)
            hi(T2_ + 4 * c + 4, 0)
            act.wait_ge(s["conv_done"], c + 1)
            for b, (a0, a1) in enumerate(BLOCKS):
                act.wait_ge(acc_done[b], P2_ + 4 * c + 4)
                ins = act.activation(U[:, a0:a1], PB[:, b, 0:BLK], ACT.Sigmoid)
                ins.then_inc(acc_free[b], 1)
            hi(T2_ + 4 * c + 5, 1)

        phase2(0)
        with act.Fori(1, NC) as c:
            phase2(c)

        def phase3(j):
            first = isinstance(j, int) and j == 0
            act.wait_ge(s["a_done"] if first else s["merged"], NC if first else j)
            for k, buf in enumerate((G1, U)):
                for b, (a0, a1) in enumerate(BLOCKS):
                    act.wait_ge(acc_done[b], P3_ + 2 * j + k + 1)
                    act.activation(buf[:, a0:a1], PB[:, b, 0:BLK], ACT.Sigmoid).then_inc(acc_free[b], 1)
                if not (isinstance(j, int) and j == KT - 1 and k == 1):
                    hi(T3_ + 2 * j + k + 2, k)
                if first and k == 0:
                    act.wait_ge(s["fin1_mm"], 1)
                    act.wait_ge(s["cu_out"], 16 * NC)
                    act.wait_ge(s["st_out"], 16)
                    act.activation(NCR[:], M[0:18, 0:2, :].rearrange("p a n -> p (a n)"), ACT.Copy).then_inc(s["fin1_copy"], 1)
                    act.activation(NR[:], M[0:NS, 2, 0:P], ACT.Copy)
                    act.activation(PN[:], M[0:H, 3, 0:P], ACT.Copy).then_inc(s["fin1_copy"], 1)

        phase3(0)
        with act.Fori(1, KT - 1) as j:
            phase3(j)
        phase3(KT - 1)
        for k in range(KT):
            act.wait_ge(s["merged"], k + 1)
            if k == 0:
                act.wait_ge(acc_done[2], P4_)
            act.activation(XH[:, k, :], A[:, k, :], ACT.Copy).then_inc(s["split_hi"], 1)
        hi(T4_ + 1, 1)

        def phase4(i):
            for x in range(2):
                n = 2 * i + x
                last = isinstance(i, int) and n == KT - 1
                act.wait_ge(s["xtr_done"], n + 1)
                if not (isinstance(i, int) and n == 0):
                    act.wait_ge(acc_free[2], P4_ + n)
                act.activation(xT[:, 0:TP], M[:, 0:2, :].rearrange("p a n -> p (a n)"), ACT.Copy)
                act.activation(xT[:, TP:T], M[:, 2, 0:NS], ACT.Copy).then_inc(s["xtr_copy"], 1)
                if not last:
                    act.wait_ge(acc_free[2], P4_ + n + 1)
                    act.activation(SQ[:], A[:, bass.ds(n, 1), :].rearrange("p o n -> p (o n)"), ACT.Square) \
                       .then_inc(s["sq_done"], 1)
                    if not (isinstance(i, int) and n == KT - 2):
                        hi(T4_ + n + 2, x)

        phase4(0)
        with act.Fori(1, KT // 2 - 1) as i:
            phase4(i)
        phase4(KT // 2 - 1)

        def square(b):
            a0, a1 = BLOCKS[b]
            act.wait_ge(acc_free[b], P4_ + KT)
            act.wait_ge(s["sqa_done"], KT - 1)
            act.activation(SQ[:, a0:a1], A[:, KT - 1, a0:a1], ACT.Square).then_inc(s["sq_done"], 1)

        def rms(b):
            act.wait_ge(s["rms_mm"], b + 1)
            bank = 3 + b % 2
            act.activation(rs[:, 3 * b:3 * b + 2], M[:, bank, 0:2], ACT.Sqrt, bias=epsc[:, 0:1], scale=1.0 / D)
            n = GROUPS[2][1]
            act.activation(rs[0:n, 3 * b + 2:3 * b + 3], M[0:n, bank, 2:3], ACT.Sqrt, bias=epsc[0:n, 0:1], scale=1.0 / D) \
               .then_inc(s["rms_sqrt"], 1)

        def rstd(b):
            a0, a1 = BLOCKS[b]
            act.wait_ge(s["rstd_mm"], b + 1)
            if b == 0:
                act.wait_ge(s["st_out"], 16 * 5)
            act.activation(RSTD[:, a0:a1], M[:, b, 0:BLK], ACT.Copy).then_inc(s["rstd_done"], 1)

        def h2_hi(b, k):
            a0, a1 = BLOCKS[b][0], min(BLOCKS[b][1], TP)
            if (b, k) in POOL_H2:
                i = POOL_H2.index((b, k))
                act.wait_ge(s["h2_tp"], i + 1)
                src = HB[:, 3 + i % 6, 0:a1 - a0]
            else:
                i = H2_DVE.index((b, k))
                act.wait_ge(s["h2_t"], i + 1)
                src = HB[:, i % 3, 0:a1 - a0]
            act.activation(XH[:, k, a0:a1], src, ACT.Identity, bias=MOD[:, 24 + k, 0:1]).then_inc(s["h2_hi"], 1)

        square(0)
        hi(T5_, 0)
        rms(0)
        rstd(0)
        h2_hi(0, 0)
        square(1)
        h2_hi(0, 1)
        rms(1)
        h2_hi(0, 2)
        h2_hi(0, 3)
        rstd(1)
        square(2)
        h2_hi(0, 4)
        h2_hi(0, 5)
        rms(2)
        h2_hi(0, 6)
        h2_hi(0, 7)
        rstd(2)
        for k in range(KT):
            h2_hi(1, k)
            if k == 3:
                hi(T5_ + 1, 1)
        act.wait_ge(s["hs_t"], 1)
        act.activation(XH[:, :, TP:T], YS[:], ACT.Copy).then_inc(s["hs_hi"], 1)
        for k in range(KT):
            h2_hi(2, k)

        def phase5(f, last=False):
            for m in range(FT):
                if isinstance(f, int) and f == m == 0:
                    act.wait_ge(s["h2_lo"], 3 * KT)
                elif not (isinstance(f, int) and f == 0 and m == 1):
                    act.wait_ge(s["act_lo"], FT * f + m - 1)
                for b, (a0, a1) in enumerate(BLOCKS):
                    act.wait_ge(acc_done[b], P5_ + 12 * f + m + 1)
                    act.activation(R[:, m % 2, a0:a1], PB[:, b, 0:BLK], ACT.Relu).then_inc(acc_free[b], 1)
                hi(T5_ + 8 * f + m + 2, m % 2, P5_ + 12 * f + m + 1)
                act.wait_ge(s["rr_done"], FT * f + m + 1)
                act.activation(AH[:, m, :], R[:, m % 2, :], ACT.Copy).then_inc(s["act_hi"], 1)
            if last:
                act.wait_ge(acc_done[2], P5_ + 12 * f + FT)
                for d in (2, 3):
                    t = T5_ + 8 * f + 4 + d
                    act.wait_ge(raw_in[d % 2], 8 * (t - d % 2) + 16)
                    act.activation(XH[:, d - 2, 0:1024], raw[:, d % 2, :], ACT.Copy).then_inc(s["hi_done"], 1)
                return
            for d in range(4):
                hi(T5_ + 8 * f + 4 + d + 2, d % 2, P5_ + 12 * f + 4 + 2 * d + 2)

        phase5(0)
        with act.Fori(1, 7) as f:
            phase5(f)
        phase5(7, last=True)
        for r, (_, n) in enumerate(Y_GROUPS):
            act.wait_ge(s["y_mm"], r + 1)
            act.activation(R[0:n, r % 2, 0:D], y_psum(r, n), ACT.Square, accum_out=ss[0:n, r:r + 1]).then_inc(s["y_sq"], 1)
            act.wait_ge(s["y_sq"], r + 1)
            act.activation(rs[0:n, r:r + 1], ss[0:n, r:r + 1], ACT.Sqrt, bias=epsc[0:n, 0:1], scale=1.0 / D) \
               .then_inc(s["y_std"], 1)

    @block.tensor
    def _(pe):
        def turn(dst, src):
            n = src.shape[0]
            return pe.transpose(dst, src, ident[0:n, 0:n])

        pe.wait_ge(s["pool_done"], 2)
        pe.wait_ge(s["csig_done"], 2)
        for k in range(KT):
            ins = turn(M[:, 2, 128 + NB * k:128 + NB * (k + 1)], CG_[0:NB, k * P:(k + 1) * P])
        ins.then_inc(s["ct_done"], 1)
        pe.wait_ge(s["ct_used"], 1)

        def ada0(q):
            if q >= 2:
                pe.wait_ge(s["mod_done"], q - 1)
            for n in range(4 * q, 4 * q + 4):
                pe.wait_ge(ar0[n % RING0], 16 * (n // RING0 + 1))
                for x in range(2):
                    ins = pe.matmul(M[0:NB, 3 + q % 2, :], cT[:, n % 4 * 2 + x, :],
                                    araw0[:, n % RING0, 512 * x:512 * x + 512], start=(n % 4 + x == 0), stop=(n % 4 == 3 and x == 1))
                ins.then_inc(s["ada0_mm"], 1)

        def rowt0(q):
            pe.wait_ge(s["arow_done"], q + 1)
            for x in range(4):
                ins = turn(M[:, 3 + q % 2, 16 * x:16 * x + NB], AROW[0:NB, P * x:P * x + P])
            ins.then_inc(s["rowt_done"], 1)

        def xturn(b):
            n = P if b < 8 else NS
            pe.wait_ge(s["xn_done"], b + 1)
            if b >= 2:
                pe.wait_ge(s["xt_free"], b - 1)
            dst = M if b % 2 == 0 else PB
            for k in range(KT):
                ins = turn(dst[:, k // 4, P * (k % 4):P * (k % 4) + n], xin[0:n, b, k * P:(k + 1) * P])
            ins.then_inc(s["xt_done"], 1)

        ada0(0)
        pe.wait_ge(s["p_in"], 16 * 8)
        turn(M[:, 2, 0:PROWS], PR[0:PROWS, :])
        turn(M[:, 2, 256:256 + NS], SNR[0:NS, :])
        for k in range(KT):
            ins = turn(M[:, 2, 288 + 16 * k:304 + 16 * k], SCR[0:16, k * P:(k + 1) * P])
        ins.then_inc(s["ct_done"], 1)
        for b in range(3):
            xturn(b)
        rowt0(0)
        ada0(1)
        for b in range(3, 6):
            xturn(b)
        rowt0(1)
        ada0(2)
        for b in range(6, 9):
            xturn(b)
        rowt0(2)
        ada0(3)
        rowt0(3)

        def gate_k(k):
            if k == 0:
                pe.wait_ge(s["gw_done"], 1)
            for b, (a0, a1) in enumerate(BLOCKS):
                for part in (XH, XL):
                    ins = pe.matmul(M[:, b, 0:BLK], GW[:, k, :], part[:, k, a0:a1],
                                    start=(k == 0 and part is XH), stop=(k == KT - 1 and part is XL))
            if k == KT - 1:
                ins.then_inc(s["gate_mm"], 1)

        def k_tile(bank, wh, wl, w0, xh, xl, k, n_k, a0, a1):
            for j, (w, x) in enumerate(((wh, xh), (wh, xl), (wl, xh))):
                ins = pe.matmul(PB[:, bank, 0:BLK], w[:, w0:w0 + P], x[:, k, a0:a1],
                                start=(k == 0 and j == 0), stop=(k == n_k - 1 and j == 2))
            return ins

        def product(p, slot, xh, xl, n_k, w_stride, w_off, before=None):
            for b, (a0, a1) in enumerate(BLOCKS):
                pe.wait_ge(acc_free[b], p)
                for k in range(n_k):
                    if before is not None:
                        before(b, k)
                    ins = k_tile(b, whi[:, slot], wlo[:, slot], w_stride * k + w_off, xh, xl, k, n_k, a0, a1)
                ins.then_inc(acc_done[b], 1)

        def first_product(p, slot, xh, xl, n_k, w_stride, ready):
            for k in range(n_k):
                ready(k)
                for b, (a0, a1) in enumerate(BLOCKS):
                    if k == 0 and not (isinstance(p, int) and p == 0):
                        pe.wait_ge(acc_free[b], p)
                    ins = k_tile(b, whi[:, slot], wlo[:, slot], w_stride * k, xh, xl, k, n_k, a0, a1)
                    if k == n_k - 1:
                        ins.then_inc(acc_done[b], 1)

        def wide(t, p, slot, ready=None, before=None):
            pe.wait_ge(s["lo_done"], t + 1)
            if ready is None:
                product(p, slot, XH, XL, KT, P, 0, before)
            else:
                first_product(p, slot, XH, XL, KT, P, ready)

        def x_ready(k):
            if k == 0:
                pe.wait_ge(s["xt_free"], 9)
            pe.wait_ge(s["h_lo"], k + 1)
            gate_k(k)

        def phase1(h):
            first = isinstance(h, int) and h == 0
            for k in range(4):
                def modulation(b, j):
                    if (b, j) == (1, 0):
                        for x in range(2):
                            a = 2 * k + x
                            pe.wait_ge(s["alo_done"], 8 * h + a + 1)
                            if first and a == 0:
                                pe.wait_ge(s["mod_done"], 4)
                            elif a % 4 == 0:
                                pe.wait_ge(s["arow_done"], 4 + 2 * h + a // 4)
                            for y in range(2):
                                for w in (ahi, alo):
                                    ins = pe.matmul(M[:, 4, :], cS[:, 2 * (a % 4) + y, :], w[:, x, 512 * y:512 * y + 512],
                                                    start=(a % 4 == 0 and y == 0 and w is ahi), stop=(a % 4 == 3 and y == 1 and w is alo))
                            ins.then_inc(s["a_used"], 1)
                    if (b, j) == (2, 4) and k % 2 == 1:
                        pe.wait_ge(s["arow_done"], 4 + 2 * h + k // 2 + 1)
                        pe.wait_ge(s["mod_done"], 4 + 2 * h + k // 2)
                        for x in range(4):
                            ins = turn(M[:, 3, P * x:P * x + P], AROW[:, P * x:P * x + P])
                        ins.then_inc(s["rowt_done"], 1)

                if first and k == 0:
                    wide(T1_, P1_, 0, x_ready)
                    modulation(1, 0)
                else:
                    wide(T1_ + 4 * h + k, P1_ + 4 * h + k, k % 2, before=modulation)

        phase1(0)
        with pe.Fori(1, H) as h:
            phase1(h)

        pe.wait_ge(s["gate_rows"], 1)
        for c in range(NC):
            for kind, row in ((GM, GMR), (WS, WSR), (MR, MRR)):
                j = (c * 3 + kind) * H
                turn(M[:, 0, j:j + H], row[:, c * L:(c + 1) * L])
        for kind, row in ((GM, GMR), (WS, WSR), (MR, MRR)):
            for u in range(2):
                ins = turn(M[0:16, 1, 8 * kind + H * u:8 * kind + H * u + H], row[:, TP + 16 * u:TP + 16 * u + 16])
        ins.then_inc(s["cols_mm"], 1)

        def phase2(c):
            first = isinstance(c, int) and c == 0
            wide(T2_ + 4 * c, P2_ + 4 * c, 0)
            pe.wait_ge(s["z_in"], 16 * c + 16)
            pe.wait_ge(s["zu_in"], 16 * c + 16)
            if first:
                pe.wait_ge(s["cols_done"], 1)
                pe.wait_ge(s["mod_done"], 12)
            else:
                pe.wait_ge(s["hm_done"], c)
                pe.wait_ge(s["ucup1_upd"], c)
            for h in range(H):
                ins = pe.matmul(M[:, 0, h * L:(h + 1) * L], Z[:, 4 * h + 1, :], Z[:, 4 * h, :], start=True, stop=True)
            ins.then_inc(s["qk_done"], 1)
            for h in range(H):
                ins = turn(M[:, 3, h * DK:(h + 1) * DK], Z[:, 4 * h + 1, :])
            ins.then_inc(s["kt_done"], 1)
            for j in range(2 * H):
                ins = turn(M[:, 1 + j // 4, P * (j % 4):P * (j % 4) + P], Z[:, 4 * (j // 2) + 2 + j % 2, :])
            ins.then_inc(s["vt_done"], 1)
            pe.matmul(M[0:16, 4, 0:16], ZU[:, 1, :], ZU[:, 0, :], start=True, stop=True)
            for x in range(2):
                turn(M[0:16, 4, 128 + P * x:256 + P * x], ZU[:, 2 + x, :])
            turn(M[0:16, 4, 384:512], ZU[:, 1, :]).then_inc(s["upre_done"], 1)
            wide(T2_ + 4 * c + 1, P2_ + 4 * c + 1, 1)
            pe.wait_ge(s["p_done"], c + 1)
            pe.wait_ge(s["qi_done"], c + 1)
            pe.wait_ge(s["vt_copy"], c + 1)
            pe.wait_ge(s["kw_done"], c + 1)
            if not first:
                pe.wait_ge(s["c_upd"], c)
            for h in range(H):
                ins = pe.matmul(M[:, h, 0:DV + 1], EX[:, h, :], VT[:, h, :], start=True, stop=first)
                if not first:
                    ins = pe.matmul(M[:, h, 0:DV + 1], IB[:, h, :], CA[:, h, :], start=False, stop=True)
            ins.then_inc(s["num_done"], 1)
            pe.wait_ge(s["cn_done"], c + 1)
            pe.wait_ge(s["cu_in"], 16 * c + 16)
            pe.matmul(M[0:16, 4, 0:DV + 2], EUS[:], VTU[:], start=True, stop=False)
            for b in range(4):
                ins = pe.matmul(M[0:16, 4, 0:DV + 1], QM[:, 16 * b:16 * b + 16], CU[:, b, :], start=False, stop=(b == 3))
            ins.then_inc(s["unum_done"], 1)
            wide(T2_ + 4 * c + 2, P2_ + 4 * c + 2, 0)
            pe.wait_ge(s["ht_ready"], c + 1)
            for h in range(H):
                ins = pe.matmul(M[:, h, 0:DV + 1], KW[:, h, :], VT[:, h, :], start=True, stop=True)
            ins.then_inc(s["cup_done"], 1)
            pe.matmul(M[:, 4, 0:DV + 2], KU[:, 0, :], VTU[:], start=True, stop=True).then_inc(s["ucup0_done"], 1)
            wide(T2_ + 4 * c + 3, P2_ + 4 * c + 3, 1)
            pe.wait_ge(s["c_upd"], c + 1)
            for j in range(2 * H):
                ins = turn(M[:, j // 4, P * (j % 4):P * (j % 4) + P], HT[:, j // 2, P * (j % 2):P * (j % 2) + P])
            ins.then_inc(s["ht_done"], 1)
            pe.wait_ge(s["ucup0_upd"], c + 1)
            for b in range(1, 4):
                ins = pe.matmul(M[:, 1 + b, 0:DV + 2], KU[:, b, :], VTU[:], start=True, stop=True)
            for x in range(2):
                ins = turn(M[:, 4, 320 + 16 * x:336 + 16 * x], HTU[:, P * x:P * x + P])
            ins.then_inc(s["ucup1_done"], 1)

        phase2(0)
        with pe.Fori(1, NC) as c:
            phase2(c)

        wide(T3_, P3_, 0)
        pe.wait_ge(s["hm_done"], NC)
        pe.wait_ge(s["ucup1_upd"], NC)
        for k in range(KT):
            turn(M[0:18, k // 4, P * (k % 4):P * (k % 4) + P], NCV[:, k, :])
        turn(M[0:NS, 2, 0:P], NT_[:])
        turn(M[0:H, 3, 0:P], CA[:, :, DV]).then_inc(s["fin1_mm"], 1)
        wide(T3_ + 1, P3_ + 1, 1)
        with pe.Fori(1, KT) as j:
            wide(T3_ + 2 * j, P3_ + 2 * j, 0)
            wide(T3_ + 2 * j + 1, P3_ + 2 * j + 1, 1)

        def merged_ready(k):
            pe.wait_ge(s["merged_lo"], k + 1)

        def phase4(i):
            for x in range(2):
                n = 2 * i + x
                pe.wait_ge(xs_in[x], 32 * i + 32)
                if isinstance(i, int) and n == 0:
                    pe.wait_ge(s["fin1_copy"], 2)
                else:
                    pe.wait_ge(s["xtr_copy"], n)
                for b in range(8):
                    turn(M[:, b // 4, P * (b % 4):P * (b % 4) + P], xs[:, x, b, :])
                turn(M[:, 2, 0:NS], xs[0:NS, x, 8, :]).then_inc(s["xtr_done"], 1)
                wide(T4_ + n, P4_ + n, x, merged_ready if isinstance(i, int) and n == 0 else None,
                     norm_work if isinstance(i, int) and n == KT - 1 else None)

        def rms_cols(b):
            a0 = BLOCKS[b][0]
            pe.wait_ge(s["sq_done"], KT + b)
            if b == 0:
                pe.wait_ge(s["sqa_done"], KT - 1)
            for i, (g, n) in enumerate(GROUPS):
                for part in (SQA, SQ):
                    ins = pe.matmul(M[0:n, 3 + b % 2, i:i + 1], part[:, a0 + g:a0 + g + n], ones[:, 0:1],
                                    start=part is SQA, stop=part is SQ)
            ins.then_inc(s["rms_mm"], 1)

        def rstd_rows(b):
            pe.wait_ge(s["rms_diag"], b + 1)
            if b == 0:
                pe.wait_ge(s["xtr_copy"], KT)
            for i, (g, n) in enumerate(GROUPS):
                ins = pe.matmul(M[:, b, g:g + n], ones[0:n, :], DG[0:n, i, 0:n], start=True, stop=True)
            ins.then_inc(s["rstd_mm"], 1)

        def norm_work(b, k):
            if b >= 1 and k == 3:
                rms_cols(b - 1)
            if b >= 1 and k == 7:
                rstd_rows(b - 1)

        phase4(0)
        with pe.Fori(1, KT // 2 - 1) as i:
            phase4(i)
        phase4(KT // 2 - 1)
        rms_cols(2)
        rstd_rows(2)

        def h2_ready(b, k):
            if b == 2 and k == 0:
                pe.wait_ge(s["hs_lo"], 1)
            pe.wait_ge(s["h2_lo"], KT * b + k + 1)

        def phase5(f, last=False):
            for m in range(FT):
                wide(T5_ + 8 * f + m, P5_ + 12 * f + m, m % 2, before=h2_ready if isinstance(f, int) and f == m == 0 else None)

            def act_ready(k):
                pe.wait_ge(s["act_lo"], FT * f + k + 1)

            if last:
                last_down(f, act_ready)
                return
            for d in range(4):
                pe.wait_ge(s["lo_done"], T5_ + 8 * f + 4 + d + 1)
                for y in range(2):
                    p = P5_ + 12 * f + 4 + 2 * d + y
                    if d == y == 0:
                        first_product(p, 0, AH, AL, FT, 256, act_ready)
                    else:
                        product(p, d % 2, AH, AL, FT, 256, P * y)

        def last_down(f, act_ready):
            def part(b, n, k):
                a0, a1 = BLOCKS[b]
                d = n // 2
                wh, wl = (whi[:, d], wlo[:, d]) if d < 2 else (XH[:, d - 2, :], XL[:, d - 2, :])
                return k_tile((KT * b + n) % 3, wh, wl, 2 * P * k + P * (n % 2), AH, AL, k, FT, a0, a1)

            def turns(r, ks):
                t0, n = Y_GROUPS[r]
                pe.wait_ge(s["down_free"], KT * (r // 3) + ks[-1] + 1)
                if ks[0] == 0 and 2 <= r < 8:
                    pe.wait_ge(s["y_done"], r - 1)
                if r == 8:
                    pe.wait_ge(s["ys_done"], KT)
                for k in ks:
                    ins = turn(y_psum(r, n)[:, P * k:P * k + P], A[:, k, t0:t0 + n])
                if ks[-1] == KT - 1:
                    ins.then_inc(s["y_mm"], 1)

            for b in range(3):
                for n in range(KT):
                    q = KT * b + n
                    if b == 0 and n in (0, 4, 6):
                        pe.wait_ge(s["lo_done"], T5_ + 8 * f + 4 + n // 2 + 1)
                    if q == 0:
                        for x in range(3):
                            pe.wait_ge(acc_free[x], P5_ + 12 * f + FT)
                            if x == 2:
                                pe.wait_ge(s["lo_done"], T5_ + 8 * f + 6)
                            for k in range(FT - 1):
                                act_ready(k)
                                part(0, x, k)
                        act_ready(FT - 1)
                        for x in range(3):
                            part(0, x, FT - 1).then_inc(s["down_done"], 1)
                    elif q >= 3:
                        pe.wait_ge(s["down_free"], q - 2)
                        for k in range(FT):
                            ins = part(b, n, k)
                        ins.then_inc(s["down_done"], 1)
                    if b >= 1 and n in (0, 2, 4):
                        turns(3 * (b - 1) + n // 2, range(KT))
                    if b == 2 and n == 6:
                        turns(6, range(KT - 2))
                        turns(7, range(KT - 2))
            turns(6, range(KT - 2, KT))
            turns(7, range(KT - 2, KT))
            turns(8, range(KT))

        phase5(0)
        with pe.Fori(1, 7) as f:
            phase5(f)
        phase5(7, last=True)

    @block.vector
    def _(dve):
        own = Count(dve, s["dve_step"])
        link, mark = own.link, own.mark

        def stt(out, in0, scalar, in1, op0, op1):
            return dve.scalar_tensor_tensor(out=out, in0=in0, scalar=scalar, in1=in1, op0=op0, op1=op1)

        def lo(t, slot):
            dve.wait_ge(s["hi_done"], t + 1)
            dve.tensor_tensor(wlo[:, slot, :], raw[:, slot, :], whi[:, slot, :].bitcast(F32), ALU.subtract) \
               .then_inc(s["lo_done"], 1)

        def alo_(a, slot):
            dve.wait_ge(s["ahi_done"], a + 1)
            dve.tensor_tensor(alo[:, slot, :], araw[:, slot, :], ahi[:, slot, :].bitcast(F32), ALU.subtract) \
               .then_inc(s["alo_done"], 1)

        dve.memset(epsc[:], EPS)
        dve.memset(bg15[:], 0.0).then_inc(s["sm_done"], 1)
        dve.memset(cS[:].bitcast(F32), 0.0)
        dve.memset(GW[:].bitcast(F32), 0.0)
        dve.wait_ge(s["csig_done"], 1)
        dve.tensor_tensor(CG_[0:NB, 0:D], CG_[0:NB, 0:D], CR[0:NB, 0:D], ALU.mult).then_inc(s["csig_done"], 1)
        dve.wait_ge(s["ct_done"], 1)
        ct = M[:, 2, 128:128 + NB * KT].rearrange("p (k c) -> p k c", c=NB)
        dve.tensor_copy(cT[:], ct).then_inc(s["ct_used"], 1)
        dve.wait_ge(s["ct_used"], 1)
        link(dve.tensor_copy(cS[:, :, 0:NB], cT[:]))
        dve.tensor_tensor(cS[:, :, 32:32 + NB], cT[:], cS[:, :, 0:NB].bitcast(F32), ALU.subtract)

        def arow0(q):
            dve.wait_ge(s["ada0_mm"], 4 * q + 4)
            if q >= 1:
                dve.wait_ge(s["rowt_done"], q)
            dve.tensor_copy(AROW[0:NB, :], M[0:NB, 3 + q % 2, :]).then_inc(s["arow_done"], 1)

        def mod0(q):
            dve.wait_ge(s["rowt_done"], q + 1)
            j = 4 * ADA0[q]
            dve.tensor_tensor(MOD[:, j:j + 4, :], M[:, 3 + q % 2, 0:64].rearrange("p (x c) -> p x c", c=16)[:, :, 0:NB],
                              PC[:, BAR + j:BAR + j + 4].rearrange("p (x o) -> p x o", o=1).to_broadcast([P, 4, NB]), ALU.add) \
               .then_inc(s["mod_done"], 1)

        def xnorm(g):
            dve.wait_ge(s["xrt_done"], g + 1)
            if g < 2:
                link(dve.reciprocal(rs[:, 3 * g:3 * g + 3], rs[:, 3 * g:3 * g + 3]))
            else:
                link(dve.reciprocal(rs[:, 6:8], rs[:, 6:8]))
                link(dve.reciprocal(rs[0:NS, 8:9], rs[0:NS, 8:9]))
            for b in range(3 * g, 3 * g + 3):
                n = P if b < 8 else NS
                dve.tensor_scalar(xin[0:n, b, :], xin[0:n, b, :], rs[0:n, b:b + 1], None, ALU.mult).then_inc(s["xn_done"], 1)

        def bc(ap, n=ST):
            return ap.rearrange("p k (b o) -> p k b o", o=1).to_broadcast([P, ap.shape[1], SB, n])

        xs_all = A[:, :, TP:T].rearrange("p k (b t) -> p k b t", t=ST)

        def modulate_samples(k0):
            dve.wait_ge(s["mod_done"], 2 if k0 == 0 else 4)
            link(stt(S1[:, k0:k0 + 4], MOD[:, 8 + k0:12 + k0, :], 1.0,
                     PC[:, G1R + k0:G1R + k0 + 4].rearrange("p (x o) -> p x o", o=1).to_broadcast([P, 4, NB]), ALU.add, ALU.mult))
            dve.wait_ge(s["xt_free"], 9)
            link(dve.tensor_tensor(xs_all[:, k0:k0 + 4], xs_all[:, k0:k0 + 4], bc(S1[:, k0:k0 + 4, 1:NB]), ALU.mult))
            link(dve.tensor_tensor(xs_all[:, k0:k0 + 4], xs_all[:, k0:k0 + 4], bc(MOD[:, k0:k0 + 4, 1:NB]), ALU.add))

        def hf(k):
            dve.tensor_scalar(A[:, k, 0:TP], A[:, k, 0:TP], S1[:, k, 0:1], MOD[:, k, 0:1], ALU.mult, ALU.add) \
               .then_inc(s["hf_done"], 1)

        def h_lo(k):
            dve.wait_ge(s["h_hi"], k + 1)
            dve.tensor_tensor(XL[:, k, :], A[:, k, :], XH[:, k, :].bitcast(F32), ALU.subtract).then_inc(s["h_lo"], 1)

        xnorm(0)
        arow0(0)
        dve.wait_ge(s["ct_done"], 2)
        dve.tensor_copy(PC[:], M[:, 2, 0:PROWS])
        dve.tensor_copy(NT_[:], M[:, 2, 256:256 + NS])
        dve.tensor_copy(SCV[:], M[:, 2, 288:416].rearrange("p (k c) -> p k c", c=16)).then_inc(s["ct_used"], 1)
        dve.wait_ge(s["ct_used"], 2)
        mod0(0)
        xnorm(1)
        dve.wait_ge(s["small_in"], 16 * 4)
        for x in range(2):
            mark(dve.tensor_copy(GW[:, :, 32 * x:32 * x + H], wg[:, :, H * x:H * x + H]))
        own.wait(own.base + own.n)
        for x in range(2):
            ins = dve.tensor_tensor(GW[:, :, 64 + 32 * x:64 + 32 * x + H], wg[:, :, H * x:H * x + H],
                                    GW[:, :, 32 * x:32 * x + H].bitcast(F32), ALU.subtract)
        ins.then_inc(s["gw_done"], 1)
        link(dve.tensor_scalar(bg15[:], bg15[:], 1.0 / CAP, None, ALU.mult))
        arow0(1)
        mod0(1)
        xnorm(2)
        arow0(2)
        lo(0, 0)
        modulate_samples(0)
        hf(0)
        hf(1)
        h_lo(0)
        mod0(2)
        hf(2)
        h_lo(1)
        arow0(3)
        hf(3)
        h_lo(2)
        mod0(3)
        h_lo(3)
        modulate_samples(4)
        hf(4)
        for k in range(5, KT):
            hf(k)
            h_lo(k - 1)
        h_lo(KT - 1)
        lo(1, 1)
        alo_(0, 0)
        alo_(1, 1)

        def phase1(h):
            last = isinstance(h, int) and h == H - 1
            for k in range(4):
                if not (last and k == 3):
                    for x in range(2):
                        alo_(8 * h + 2 * k + 2 + x, x)
                q = 4 + 2 * h + k // 2
                if k % 2 == 1:
                    dve.wait_ge(s["a_used"], 8 * h + 4 * (k // 2) + 4)
                    dve.wait_ge(s["rowt_done"], q)
                    dve.tensor_copy(AROW[:], M[:, 4, :]).then_inc(s["arow_done"], 1)
                    lo(T1_ + 4 * h + k + 2, k % 2)
                    dve.wait_ge(s["rowt_done"], q + 1)
                    ps = M[:, 3, :].rearrange("p (x c) -> p x c", c=P)
                    dst = MOD[:, bass.ds(4 * q, 4), :]
                    link(dve.tensor_tensor(dst, ps[:, :, 0:NB],
                                           PC[:, bass.ds(BAR + 4 * q, 4)].rearrange("p (x o) -> p x o", o=1).to_broadcast([P, 4, NB]),
                                           ALU.add))
                    dve.tensor_tensor(dst, ps[:, :, 32:32 + NB], dst, ALU.add).then_inc(s["mod_done"], 1)
                else:
                    lo(T1_ + 4 * h + k + 2, k % 2)

        def gate_sums():
            dve.wait_ge(s["gate_mm"], 1)
            for b, (a0, a1) in enumerate(BLOCKS):
                link(dve.tensor_copy(GT[:, a0:a1], M[64:100, b, 0:BLK]))
                link(dve.tensor_tensor(GT[:, a0:a1], M[0:36, b, 0:BLK], GT[:, a0:a1], ALU.add))
            dve.memset(RMK[:], 1.0).then_inc(s["gate_sum"], 1)
            dve.wait_ge(s["gate_sum"], 1)
            link(dve.memset(RMK[:, 0:TP].rearrange("p (c n) -> p c n", n=L)[:, :, 0:1], 0.0))

        def chunks(ap):
            return ap[:, 0:TP].rearrange("p (c n) -> p c n", n=L)

        def steps(ap):
            return ap[:, TP:T].rearrange("p (b t) -> p b t", t=ST)

        def units(ap):
            return ap[:, TP:T].rearrange("p (u b t) -> p b u t", u=2, t=ST)

        def nat(ap):
            return ap[:, TP:T].rearrange("p (b u t) -> p b u t", u=2, t=ST)

        def bcs(ap):
            return ap.rearrange("p (b u o) -> p b u o", u=2, o=1).to_broadcast([H, SB // 2, 2, ST])

        def gate_cumsum():
            dve.wait_ge(s["gate_act"], 1)
            link(dve.tensor_tensor_scan(NBr[32:36, 0:TP], RMK[32:36, 0:TP], GT[32:36, 0:TP], 0.0, ALU.mult, ALU.add))
            nb, lf = steps(NBr[32:36]), steps(GT[32:36])
            link(dve.tensor_copy(nb[:, :, 0], lf[:, :, 0]))
            for t in range(1, ST):
                link(dve.tensor_tensor(nb[:, :, t], nb[:, :, t - 1], lf[:, :, t], ALU.add))
            link(dve.tensor_copy(NB0, NBr[32:36, :]))
            link(dve.memset(DL[:, 0:TP], 0.0))
            link(stt(GT[0:H, :], TH[0:H, :], CAP, NB0, ALU.mult, ALU.add))
            link(dve.tensor_scalar(chunks(DL)[:, 1:NC, 0], chunks(NB0)[:, 0:NC - 1, L - 1], -1.0, None, ALU.mult))

        def gate_max():
            G = GT[0:H]
            link(dve.tensor_tensor_scan(MU[:, 0:TP], DL[:, 0:TP], G[:, 0:TP], 0.0, ALU.add, ALU.max))
            link(dve.memset(MP[:], 0.0))
            mu, g = steps(MU), steps(G)
            link(dve.tensor_tensor(mu[:, :, 0], M0s[:], g[:, :, 0], ALU.max))
            for t in range(1, ST):
                link(dve.tensor_tensor(mu[:, :, t], mu[:, :, t - 1], g[:, :, t], ALU.max))
            cmu, cnb = chunks(MU), chunks(NB0)
            mark(dve.tensor_tensor(MP[:, 1:NC], cmu[:, 0:NC - 1, L - 1], cnb[:, 0:NC - 1, L - 1], ALU.subtract))
            mark(dve.tensor_tensor(PM[:], MU[:, TP - 1:TP], NB0[:, TP - 1:TP], ALU.subtract))
            link(dve.tensor_tensor(SMo[:], mu[:, :, ST - 1], steps(NB0)[:, :, ST - 1], ALU.subtract))
            mp = MP[:].rearrange("p (c o) -> p c o", o=1).to_broadcast([H, NC, L])
            mul = cmu[:, :, L - 1:L].to_broadcast([H, NC, L])
            m0 = bcs(M0s[:])
            mus = nat(MU)[:, :, :, ST - 1:ST].to_broadcast([H, SB // 2, 2, ST])
            sub = ALU.subtract
            dve.tensor_tensor(chunks(RR), mp, cmu, sub)
            dve.tensor_tensor(chunks(GMR), chunks(G), mp, sub)
            dve.tensor_tensor(chunks(WSR), chunks(G), mul, sub)
            dve.tensor_tensor(MRR[:, 0:TP], MU[:, 0:TP], NB0[:, 0:TP], sub)
            dve.tensor_tensor(units(RR), m0, nat(MU), sub)
            dve.tensor_tensor(units(GMR), nat(G), m0, sub)
            dve.tensor_tensor(units(WSR), nat(G), mus, sub)
            dve.tensor_tensor(units(MRR), nat(MU), nat(NB0), sub).then_inc(s["gate_rows"], 1)

        gate_sums()
        phase1(0)
        gate_cumsum()
        phase1(1)
        gate_max()
        phase1(2)
        phase1(3)
        dve.wait_ge(s["mod_done"], 12)
        link(stt(S2[:], MOD[:, 32:40, :], 1.0, PC[:, G2R:G2R + 8].rearrange("p (x o) -> p x o", o=1).to_broadcast([P, KT, NB]),
                 ALU.add, ALU.mult))
        dve.wait_ge(s["cols_done"], 1)
        dve.wait_ge(z_out[0], 32 * 2 * H)
        dve.wait_ge(z_out[1], 32 * 2 * H)
        dve.wait_ge(s["r_out"], 32)
        dve.wait_ge(s["a_used"], 32)
        dve.memset(CA[:], 0.0)
        dve.memset(VT[:, :, DV:DV + 1], 1.0)
        for part in (VTU, KU, EUS):
            mark(dve.memset(part[:].bitcast(F32), 0.0))
        own.wait(own.base + own.n)
        for r in (0, 64):
            dve.memset(VTU[r:r + 16, DV:DV + 1].bitcast(F32), 1.0)
        dve.memset(U[:, 0:2], 0.0)
        link(dve.memset(QM[:], 0.0))
        dve.wait_ge(s["pool_done"], POOL_STEPS)

        base2 = own.base + own.n
        PER2 = 20

        def phase2(c, last=False):
            own.turn(base2, c, PER2)
            first = isinstance(c, int) and c == 0
            col = COL[:, bass.ds(c, 1), :, :].rearrange("p c k h -> p (c k) h")
            cols = COLS[:, bass.ds(c, 1), :].rearrange("p c k -> p (c k)")
            dve.tensor_scalar(WM[:], BM[:], cols[:, WS:WS + 1], KSCALE, ALU.mult, ALU.mult).then_inc(s["wm_done"], 1)
            dve.wait_ge(s["rb_in"], 32 * c + 32)
            for h in range(H):
                stt(EX[:, h, :], RB[:, h, :], col[:, GM, h:h + 1], CM[:], ALU.add, ALU.min)
            stt(EU[:], RU[0:16, :], cols[:, GM:GM + 1], CMS[:], ALU.add, ALU.min).then_inc(s["ex_done"], 1)
            dve.wait_ge(s["ib_exp"], c + 1)
            dve.tensor_copy(DEC[:], IB[:, :, L - 1])
            mark(dve.tensor_copy(DECU[:], IU[:].rearrange("p (b t) -> p b t", t=ST)[:, :, ST - 1]))
            dve.wait_ge(s["z_in"], 16 * c + 16)
            dve.wait_ge(s["zu_in"], 16 * c + 16)
            own.wait(own.base + own.n)
            q = Z[:].rearrange("p (h k) n -> p h k n", k=4)[:, :, 0, :]
            dve.tensor_tensor(IB[:], q, IB[:], ALU.mult)
            dve.tensor_tensor(QM[:].rearrange("p (b x) -> p b x", x=20)[:, :, 0:ST], ZU[:, 0, :].rearrange("p (b t) -> p b t", t=ST),
                              IU[:].rearrange("p (b t) -> p b t", t=ST), ALU.mult).then_inc(s["qi_done"], 1)
            lo(T2_ + 4 * c + 2, 0)
            dve.wait_ge(s["qk_done"], c + 1)
            dve.wait_ge(s["e_exp"], c + 1)
            stt(EX[:], M[:, 0, :].rearrange("p (h n) -> p h n", n=L), KSCALE, EX[:], ALU.mult, ALU.mult)
            dve.wait_ge(s["unit_hi"], c + 1)
            stt(EU[:], M[0:16, 4, 0:16], KSCALE, EU[:], ALU.mult, ALU.mult).then_inc(s["eu_ready"], 1)
            dve.wait_ge(s["kt_done"], c + 1)
            for h in range(H):
                dve.tensor_scalar(KW[:, h, :], M[:, 3, h * DK:(h + 1) * DK], col[:, WS, h:h + 1], KSCALE, ALU.mult, ALU.mult)
            dve.tensor_tensor(VTU[32:48, 0:DV], M[0:16, 4, 128:128 + DV], VTU[0:16, 0:DV].bitcast(F32), ALU.subtract)
            for b in range(4):
                stt(KU[64:80, b, :], M[0:16, 4, 384:512], WM[:, b:b + 1], KU[0:16, b, :].bitcast(F32), ALU.mult, ALU.subtract)
            dve.tensor_copy(VTU[64:80, 0:DV], VTU[0:16, 0:DV])
            dve.tensor_copy(KU[32:48, :, :], KU[0:16, :, :]).then_inc(s["kw_done"], 1)
            dve.wait_ge(s["eu_hi"], c + 1)
            dve.tensor_tensor(EUS[64:80, :], EU[:], EUS[0:16, :].bitcast(F32), ALU.subtract).then_inc(s["p_done"], 1)
            nsel = NT_[:].rearrange("p (x u) -> p u x", u=2 * H)[:, bass.ds(c, 1), :].rearrange("p u x -> p (u x)")
            dve.tensor_copy(CU[:, :, DV], nsel).then_inc(s["cn_done"], 1)
            us = U[:, 2 + TP:].rearrange("p (b x) -> p b x", x=6)
            for b, (a0, a1) in enumerate(BLOCKS):
                dve.wait_ge(acc_done[b], P2_ + 4 * c + 2)
                if b == 0:
                    dve.wait_ge(acc_free[2], P2_ + 4 * c + 1)
                if b < 2:
                    dve.tensor_tensor(U[:, 2 + a0:2 + a1], PB[:, b, 0:BLK], G1[:, a0:a1], ALU.mult).then_inc(acc_free[b], 1)
                else:
                    dve.tensor_tensor(U[:, 2 + a0:2 + TP], PB[:, b, 0:LP], G1[:, a0:TP], ALU.mult)
                    dve.tensor_tensor(us[:, :, 2:6], PB[:, b, LP:BLK].rearrange("p (b t) -> p b t", t=ST),
                                      G1[:, TP:T].rearrange("p (b t) -> p b t", t=ST), ALU.mult).then_inc(acc_free[b], 1)
            lo(T2_ + 4 * c + 3, 1)
            scv = SCV[:, bass.ds(c, 1), :].rearrange("p c (b w) -> p (c b) w", w=2)
            mark(dve.memset(U[:, 0:2], 0.0))
            link(dve.tensor_copy(us[:, :, 0:2], scv))
            ncv = NCV[:, bass.ds(c, 1), :].rearrange("p c n -> p (c n)")
            dve.tensor_copy(ncv[:, 16:18], U[:, TP:TP + 2])
            dve.tensor_copy(ncv[:, 0:16].rearrange("p (b w) -> p b w", w=2), us[:, :, 4:6])
            g1s = G1[:, TP:T].rearrange("p (b t) -> p b t", t=ST)

            def cw(w):
                return PC[:, bass.ds(CWR + 8 * w + c, 1)]

            mark(dve.tensor_scalar(G1[:, 0:TP], U[:, 0:TP], cw(0), PC[:, bass.ds(CBR + c, 1)], ALU.mult, ALU.add))
            link(dve.tensor_scalar(g1s, us[:, :, 0:4], cw(0), PC[:, bass.ds(CBR + c, 1)], ALU.mult, ALU.add))
            mark(stt(G1[:, 0:TP], U[:, 1:1 + TP], cw(1), G1[:, 0:TP], ALU.mult, ALU.add))
            link(stt(g1s, us[:, :, 1:5], cw(1), g1s, ALU.mult, ALU.add))
            stt(G1[:, 0:TP], U[:, 2:2 + TP], cw(2), G1[:, 0:TP], ALU.mult, ALU.add)
            stt(g1s, us[:, :, 2:6], cw(2), g1s, ALU.mult, ALU.add).then_inc(s["conv_done"], 1)
            dve.wait_ge(s["ss_done"], c + 1)
            den, denu = M[:, 0:H, DV], M[0:16, 4, DV:DV + 1]
            mark(stt(sc4[:, 2, :], den, -1.0, col[:, MR, :], ALU.mult, ALU.max))
            link(stt(sc1[:, 2:3], denu, -1.0, cols[:, MR:MR + 1], ALU.mult, ALU.max))
            mark(dve.tensor_tensor(sc4[:, 2, :], den, sc4[:, 2, :], ALU.max))
            link(dve.tensor_tensor(sc1[:, 2:3], denu, sc1[:, 2:3], ALU.max))
            mark(dve.reciprocal(sc4[:, 3, :], sc4[:, 2, :]))
            link(dve.reciprocal(sc1[:, 3:4], sc1[:, 2:3]))
            mark(dve.tensor_tensor(sc4[:, 4, :], sc4[:, 3, :], sc4[:, 3, :], ALU.mult))
            link(dve.tensor_tensor(sc1[:, 4:5], sc1[:, 3:4], sc1[:, 3:4], ALU.mult))
            dve.tensor_tensor(sc4[:, 5, :], sc4[:, 4, :], sc4[:, 0, :], ALU.mult)
            dve.tensor_tensor(sc1[:, 5:6], sc1[:, 4:5], sc1[:, 0:1], ALU.mult).then_inc(s["var_done"], 1)
            dve.wait_ge(s["std_done"], c + 1)
            mark(dve.reciprocal(sc4[:, 6, :], sc4[:, 1, :]))
            link(dve.reciprocal(sc1[:, 6:7], sc1[:, 1:2]))
            mark(dve.tensor_tensor(sc4[:, 7, :], sc4[:, 6, :], sc4[:, 3, :], ALU.mult))
            link(dve.tensor_tensor(sc1[:, 7:8], sc1[:, 6:7], sc1[:, 3:4], ALU.mult))
            for h in range(H):
                dve.tensor_scalar(HT[:, h, :], M[:, h, 0:DV], sc4[:, 7, h:h + 1], None, ALU.mult)
            dve.tensor_scalar(HTU[:], M[0:16, 4, 0:DV], sc1[:, 7:8], None, ALU.mult).then_inc(s["ht_ready"], 1)
            dve.wait_ge(s["conv_done"], c + 1)
            for b, (a0, a1) in enumerate(BLOCKS):
                dve.wait_ge(acc_done[b], P2_ + 4 * c + 3)
                dve.tensor_tensor(G1[:, a0:a1], PB[:, b, 0:BLK], G1[:, a0:a1], ALU.mult).then_inc(acc_free[b], 1)
            lo(T2_ + 4 * c + 4, 0)
            dve.wait_ge(s["cup_done"], c + 1)
            for h in range(H):
                ins = stt(CA[:, h, :], CA[:, h, :], DEC[:, h:h + 1], M[:, h, 0:DV + 1], ALU.mult, ALU.add)
            ins.then_inc(s["c_upd"], 1)
            dve.wait_ge(s["ucup0_done"], c + 1)
            stt(CU[:, 0, :], CU[:, 0, :], DECU[:, 0:1], M[:, 4, 0:DV + 1], ALU.mult, ALU.add).then_inc(s["ucup0_upd"], 1)
            dve.wait_ge(acc_free[2], P2_ + 4 * c + 4)
            dve.tensor_tensor(A[:, bass.ds(c, 1), :].rearrange("p o n -> p (o n)"), G1[:], U[:, 0:T], ALU.mult) \
               .then_inc(s["a_done"], 1)
            lo(T2_ + 4 * c + 5, 1)
            dve.wait_ge(s["ht_done"], c + 1)
            for x in range(2):
                ins = dve.tensor_tensor(hm[:, 4 * x:4 * x + 4, bass.ds(c * L, L)], M[:, x, :].rearrange("p (k n) -> p k n", n=L),
                                        PC[:, HNR + 4 * x:HNR + 4 * x + 4].rearrange("p (x o) -> p x o", o=1).to_broadcast([P, 4, L]),
                                        ALU.mult)
            ins.then_inc(s["hm_done"], 1)
            dve.wait_ge(s["ucup1_done"], c + 1)
            for b in range(1, 4):
                ins = stt(CU[:, b, :], CU[:, b, :], DECU[:, b:b + 1], M[:, 1 + b, 0:DV + 1], ALU.mult, ALU.add)
            link(ins)
            dve.tensor_copy(hms[:, bass.ds(c, 1), :, :].rearrange("p c x n -> p (c x) n"),
                            M[:, 4, 320:352].rearrange("p (x n) -> p x n", n=16))
            dve.tensor_copy(nsel, CU[:, :, DV]).then_inc(s["ucup1_upd"], 1)
            assert own.n == PER2, own.n

        phase2(0)
        with dve.Fori(1, NC) as c:
            phase2(c)
        own.turn(base2, NC, PER2)
        base3 = own.base
        PER3 = 6

        def phase3(j):
            own.turn(base3, j, PER3)
            dve.wait_ge(acc_free[2], P3_ + 2 * j + 1)
            mark(dve.tensor_tensor(G1[:, 0:TP], G1[:, 0:TP], hm[:, bass.ds(j, 1), :].rearrange("p o n -> p (o n)"), ALU.mult))
            g1u = G1[:, TP:T].rearrange("p (b u t) -> p u b t", u=2, t=ST)
            hj = hms[:].rearrange("p (u h) x (b t) -> p u (h x) b t", u=2, t=ST)
            for u in range(2):
                ins = stt(g1u[:, u], hj[:, u, bass.ds(j, 1)].rearrange("p o b t -> p (o b) t"), PC[:, bass.ds(HNR + j, 1)], g1u[:, u],
                          ALU.mult, ALU.mult)
                (mark if u == 0 else link)(ins)
            lo(T3_ + 2 * j + 2, 0)
            aj = A[:, bass.ds(j, 1), :].rearrange("p o n -> p (o n)")
            for b, (a0, a1) in enumerate(BLOCKS):
                dve.wait_ge(acc_free[b], P3_ + 2 * j + 2)
                link(dve.tensor_tensor(U[:, a0:a1], U[:, a0:a1], G1[:, a0:a1], ALU.mult))
                ins = dve.tensor_tensor(aj[:, a0:a1], aj[:, a0:a1], U[:, a0:a1], ALU.add)
            ins.then_inc(s["merged"], 1)
            if not (isinstance(j, int) and j == KT - 1):
                lo(T3_ + 2 * j + 3, 1)
            assert own.n == PER3, own.n

        with dve.Fori(0, KT - 1) as j:
            phase3(j)
        phase3(KT - 1)
        own.turn(base3, KT, PER3)
        for k in range(KT):
            dve.wait_ge(s["split_hi"], k + 1)
            dve.tensor_tensor(XL[:, k, :], A[:, k, :], XH[:, k, :].bitcast(F32), ALU.subtract).then_inc(s["merged_lo"], 1)
        lo(T4_ + 1, 1)
        link(dve.memset(SQA[:], 0.0))
        base4 = own.base + own.n
        PER4 = 1

        def residual(n, b):
            a0, a1 = BLOCKS[b]
            an = A[:, bass.ds(n, 1), :].rearrange("p o n -> p (o n)")
            gt = MOD[:, bass.ds(16 + n, 1), :].rearrange("p o c -> p (o c)")
            dve.wait_ge(acc_done[b], P4_ + n + 1)
            if b < 2:
                stt(an[:, a0:a1], PB[:, b, 0:BLK], gt[:, 0:1], xT[:, a0:a1], ALU.mult, ALU.add).then_inc(acc_free[b], 1)
            else:
                stt(an[:, a0:TP], PB[:, b, 0:LP], gt[:, 0:1], xT[:, a0:TP], ALU.mult, ALU.add)
                link(dve.tensor_tensor(an[:, TP:T].rearrange("p (b t) -> p b t", t=ST),
                                       PB[:, b, LP:BLK].rearrange("p (b t) -> p b t", t=ST),
                                       gt[:, 1:NB].rearrange("p (b o) -> p b o", o=1).to_broadcast([P, SB, ST]), ALU.mult))
                dve.tensor_tensor(an[:, TP:T], an[:, TP:T], xT[:, TP:T], ALU.add).then_inc(acc_free[b], 1)

        def scaled(n, a0, a1):
            an = A[:, bass.ds(n, 1), :].rearrange("p o n -> p (o n)")
            asn = AS[:, bass.ds(n, 1), :].rearrange("p o n -> p (o n)")
            s2 = S2[:, bass.ds(n, 1), :].rearrange("p o c -> p (o c)")
            ins = dve.tensor_scalar(asn[:, a0:min(a1, TP)], an[:, a0:min(a1, TP)], s2[:, 0:1], None, ALU.mult)
            if a1 == T:
                ins = dve.tensor_tensor(asn[:, TP:T].rearrange("p (b t) -> p b t", t=ST), an[:, TP:T].rearrange("p (b t) -> p b t", t=ST),
                                        s2[:, 1:NB].rearrange("p (b o) -> p b o", o=1).to_broadcast([P, SB, ST]), ALU.mult)
            return ins

        def phase4(i):
            for x in range(2):
                n = 2 * i + x
                if isinstance(i, int) and n == KT - 1:
                    continue
                own.turn(base4, n, PER4)
                dve.wait_ge(s["xtr_copy"], n + 1)
                for b in range(3):
                    residual(n, b)
                if not (isinstance(i, int) and n == KT - 2):
                    lo(T4_ + n + 2, x)
                dve.wait_ge(acc_free[2], P4_ + n + 1)
                scaled(n, 0, T)
                dve.wait_ge(s["sq_done"], n + 1)
                dve.tensor_tensor(SQA[:], SQA[:], SQ[:], ALU.add).then_inc(s["sqa_done"], 1)
                dve.wait_ge(s["sqa_done"], n + 1)
                assert own.n == PER4, own.n

        with dve.Fori(0, KT // 2 - 1) as i:
            phase4(i)
        phase4(KT // 2 - 1)
        own.turn(base4, KT - 1, PER4)

        def last_residual(b):
            if b == 0:
                dve.wait_ge(s["xtr_copy"], KT)
            residual(KT - 1, b)
            dve.wait_ge(acc_free[b], P4_ + KT)
            scaled(KT - 1, *BLOCKS[b]).then_inc(s["as_done"], 1)

        def rms_diag(b):
            dve.wait_ge(s["rms_sqrt"], b + 1)
            n = GROUPS[2][1]
            mark(dve.reciprocal(rs[:, 3 * b:3 * b + 2], rs[:, 3 * b:3 * b + 2]))
            link(dve.reciprocal(rs[0:n, 3 * b + 2:3 * b + 3], rs[0:n, 3 * b + 2:3 * b + 3]))
            if b >= 1:
                dve.wait_ge(s["rstd_mm"], b)
            for i, (g, n) in enumerate(GROUPS):
                ins = dve.tensor_scalar(DG[0:n, i, 0:n], ident[0:n, 0:n], rs[0:n, 3 * b + i:3 * b + i + 1], None, ALU.mult)
            ins.then_inc(s["rms_diag"], 1)

        def h2_t(b, k):
            a0, a1 = BLOCKS[b][0], min(BLOCKS[b][1], TP)
            i = H2_DVE.index((b, k))
            dve.wait_ge(s["rstd_done"], b + 1)
            dve.wait_ge(s["as_done"], b + 1)
            if i >= 3:
                dve.wait_ge(s["h2_lo"], KT * H2_DVE[i - 3][0] + H2_DVE[i - 3][1] + 1)
            dve.tensor_tensor(HB[:, i % 3, 0:a1 - a0], AS[:, k, a0:a1], RSTD[:, a0:a1], ALU.mult).then_inc(s["h2_t"], 1)

        def h2_lo(b, k):
            a0, a1 = BLOCKS[b][0], min(BLOCKS[b][1], TP)
            slot = 3 + POOL_H2.index((b, k)) % 6 if (b, k) in POOL_H2 else H2_DVE.index((b, k)) % 3
            dve.wait_ge(s["h2_hi"], KT * b + k + 1)
            stt(XL[:, k, a0:a1], HB[:, slot, 0:a1 - a0], MOD[:, 24 + k, 0:1], XH[:, k, a0:a1].bitcast(F32), ALU.add, ALU.subtract) \
                .then_inc(s["h2_lo"], 1)

        last_residual(0)
        rms_diag(0)
        lo(T5_, 0)
        h2_t(0, 0)
        last_residual(1)
        for k in (1, 2):
            h2_t(0, k)
            h2_lo(0, k - 1)
        rms_diag(1)
        for k in (3, 4):
            h2_t(0, k)
            h2_lo(0, k - 1)
        last_residual(2)
        h2_t(0, 5)
        h2_lo(0, 4)
        h2_t(0, 6)
        rms_diag(2)
        h2_lo(0, 5)
        h2_t(0, 7)
        h2_lo(0, 6)
        def h2_block(b, ks):
            for k in ks:
                if (b, k + 1) in H2_DVE:
                    h2_t(b, k + 1)
                h2_lo(b, k)

        h2_t(1, 0)
        h2_lo(0, 7)
        h2_block(1, range(4))
        dve.wait_ge(s["rstd_done"], 3)
        dve.wait_ge(s["as_done"], 3)
        link(dve.tensor_tensor(YS[:], AS[:, :, TP:T], RSTD[:, TP:T].rearrange("p (o n) -> p o n", o=1).to_broadcast([P, KT, NS]),
                               ALU.mult))
        ys = YS[:].rearrange("p k (b t) -> p k b t", t=ST)
        mark(dve.tensor_tensor(ys[:, 0:4], ys[:, 0:4], bc(MOD[:, 24:28, 1:NB]), ALU.add))
        dve.tensor_tensor(ys[:, 4:8], ys[:, 4:8], bc(MOD[:, 28:32, 1:NB]), ALU.add).then_inc(s["hs_t"], 1)
        h2_block(1, range(4, KT - 1))
        h2_t(2, 0)
        h2_lo(1, KT - 1)
        lo(T5_ + 1, 1)
        dve.wait_ge(s["hs_hi"], 1)
        dve.tensor_tensor(XL[:, :, TP:T], YS[:], XH[:, :, TP:T].bitcast(F32), ALU.subtract).then_inc(s["hs_lo"], 1)
        h2_block(2, range(KT))
        dve.memset(YS[:], 0.0).then_inc(s["x2n_done"], 1)

        def phase5(f, last=False):
            for m in range(FT):
                dve.wait_ge(acc_free[2], P5_ + 12 * f + m + 1)
                r = R[:, m % 2, :]
                dve.tensor_tensor(r, r, r, ALU.mult).then_inc(s["rr_done"], 1)
                lo(T5_ + 8 * f + m + 2, m % 2)
                dve.wait_ge(s["act_hi"], FT * f + m + 1)
                dve.tensor_tensor(AL[:, m, :], r, AH[:, m, :].bitcast(F32), ALU.subtract).then_inc(s["act_lo"], 1)
            if last:
                last_down(f)
                return
            for d in range(4):
                for y in range(2):
                    n = 2 * d + y
                    for b, (a0, a1) in enumerate(BLOCKS):
                        dve.wait_ge(acc_done[b], P5_ + 12 * f + 4 + n + 1)
                        gt = MOD[:, 40 + n, 0:1]
                        if b < 2:
                            stt(A[:, n, a0:a1], PB[:, b, 0:BLK], gt, A[:, n, a0:a1], ALU.mult, ALU.add).then_inc(acc_free[b], 1)
                        else:
                            stt(A[:, n, a0:TP], PB[:, b, 0:LP], gt, A[:, n, a0:TP], ALU.mult, ALU.add)
                            dve.tensor_tensor(YS[:, n, :], PB[:, b, LP:BLK], YS[:, n, :], ALU.add).then_inc(acc_free[b], 1)
                lo(T5_ + 8 * f + 4 + d + 2, d % 2)

        def last_down(f):
            def lo_down(d):
                t = T5_ + 8 * f + 4 + d
                dve.wait_ge(s["hi_done"], t + 1)
                dve.tensor_tensor(XL[:, d - 2, 0:1024], raw[:, d % 2, :], XH[:, d - 2, 0:1024].bitcast(F32), ALU.subtract) \
                   .then_inc(s["lo_done"], 1)

            def out(r):
                n = Y_GROUPS[r][1]
                dve.wait_ge(s["y_std"], r + 1)
                link(dve.reciprocal(rs[0:n, r:r + 1], rs[0:n, r:r + 1]))
                if r == 0:
                    dve.wait_ge(s["gf_in"], 16)
                if 2 <= r < 8:
                    dve.wait_ge(y_out[r % 2], 16 * (r // 2))
                stt(y_rows(r, n), y_psum(r, n), rs[0:n, r:r + 1], GF[0:n, :], ALU.mult, ALU.mult).then_inc(s["y_done"], 1)

            for b, (a0, a1) in enumerate(BLOCKS):
                for n in range(KT):
                    q = KT * b + n
                    bank = PB[:, q % 3, :]
                    if q in (0, 3):
                        lo_down(2 + q // 3)
                    dve.wait_ge(s["down_done"], q + 1)
                    ins = stt(A[:, n, a0:min(a1, TP)], bank[:, 0:min(a1, TP) - a0], MOD[:, 40 + n, 0:1], A[:, n, a0:min(a1, TP)],
                              ALU.mult, ALU.add)
                    if b < 2:
                        ins.then_inc(s["down_free"], 1)
                    else:
                        dve.tensor_tensor(YS[:, n, :], bank[:, LP:BLK], YS[:, n, :], ALU.add).then_inc(s["down_free"], 1)
                        dve.wait_ge(s["down_free"], q + 1)
                        ysn = YS[:, n, :].rearrange("p (b t) -> p b t", t=ST)
                        link(dve.tensor_tensor(ysn, ysn, MOD[:, 40 + n, 1:NB].rearrange("p (b o) -> p b o", o=1)
                                               .to_broadcast([P, SB, ST]), ALU.mult))
                        dve.tensor_tensor(A[:, n, TP:T], A[:, n, TP:T], YS[:, n, :], ALU.add).then_inc(s["ys_done"], 1)
                    if b >= 1 and n in (1, 3, 5):
                        out(3 * (b - 1) + n // 2)
            for r in (6, 7, 8):
                out(r)

        phase5(0)
        with dve.Fori(1, 7) as f:
            phase5(f)
        phase5(7, last=True)

    ctx.close()


_INS = ["x_prompt", "x_sample", "state_conv", "state_C", "state_n", "state_m", "c_prompt", "c_sample", "w_ada", "b_ada",
        "g_norm1", "g_norm2", "w_in", "b_gate", "conv_w", "conv_b", "hn_g", "w_out", "w_up", "w_down", "g_final"]
_OUTS = {"y_prompt": (1, 1024, 1024), "y_sample": (8, 4, 1024), "p_conv": (1, 1, 2, 1024), "p_C": (1, 1, 4, 128, 256),
         "p_n": (1, 1, 4, 128), "p_m": (1, 1, 4), "s_conv": (1, 8, 2, 1024), "s_C": (1, 8, 4, 128, 256),
         "s_n": (1, 8, 4, 128), "s_m": (1, 8, 4)}


def kernel(**inputs):
    import numpy as np
    import concourse.bacc as bacc
    from concourse.bass_utils import run_bass_kernel_spmd

    nc = bacc.Bacc("TRN2", target_bir_lowering=False, num_devices=1)
    arrays, I, O = {}, {}, {}
    for name in _INS:
        a = np.ascontiguousarray(inputs[name])
        arrays[f"in_{name}"] = a
        I[name] = nc.dram_tensor(f"in_{name}", a.shape, F32, kind="ExternalInput").ap()
    for name, shape in _OUTS.items():
        O[name] = nc.dram_tensor(f"out_{name}", shape, F32, kind="ExternalOutput").ap()
    layer_kernel(nc, I, O)
    r = run_bass_kernel_spmd(nc, [arrays], core_ids=[0])
    return tuple(r.results[0][f"out_{name}"] for name in _OUTS)
```
